# Optimizing a Trainium2 kernel written in Bass

```python
import jax, jax.numpy as jnp
from jax import lax
import numpy as np
import math

D_MODEL = 1024
BATCH = 1
SEQ = 512
DEPTH = 1

GRID_W = 64
CTX_LEN = 256
MIX_W = D_MODEL
NA_HEADS = 8
NA_HEAD_DIM = 64
NA_W = NA_HEADS * NA_HEAD_DIM
NA_KH = 8
NA_KW = 16
SGU_GROUPS = 8
SGU_W = MIX_W - NA_W
SGU_GROUP_DIM = SGU_W // SGU_GROUPS
SGU_CHUNK = 128
IN_COLS = 3 * NA_W + 2 * SGU_W
N_GROUPS = 4
EXPERTS_PER_GROUP = 4
N_EXPERTS = N_GROUPS * EXPERTS_PER_GROUP
TOP_K = 2
D_EXPERT = D_MODEL // 2
N_MOD = 6
EPS = 1e-6


def _rms(x):
    x32 = x.astype(jnp.float32)
    return (x32 * lax.rsqrt(jnp.mean(x32 * x32, -1, keepdims=True) + EPS)).astype(x.dtype)

def _layernorm(x, g):
    x32 = x.astype(jnp.float32)
    mu = jnp.mean(x32, -1, keepdims=True)
    var = jnp.mean(jnp.square(x32 - mu), -1, keepdims=True)
    return ((x32 - mu) * lax.rsqrt(var + EPS)).astype(x.dtype) * g

def _adaln(cond, w, b):
    return jnp.split(jax.nn.silu(cond) @ w + b, N_MOD, axis=-1)

def _modulate(x, shift, scale):
    return _rms(x) * (1 + scale) + shift

def _heads(t):
    return t.reshape(t.shape[:-1] + (NA_HEADS, NA_HEAD_DIM))

def _project(h, w_in, q_gain, k_gain):
    p = h @ w_in
    q = _rms(_heads(p[..., :NA_W])) * q_gain
    k = _rms(_heads(p[..., NA_W:2 * NA_W])) * k_gain
    v = _heads(p[..., 2 * NA_W:3 * NA_W])
    u = p[..., 3 * NA_W:3 * NA_W + SGU_W]
    vs = p[..., 3 * NA_W + SGU_W:]
    return q, k, v, u, vs

def _project_kv(h, w_in, k_gain):
    p = h @ w_in[:, NA_W:3 * NA_W]
    return _rms(_heads(p[..., :NA_W])) * k_gain, _heads(p[..., NA_W:])

def _neighborhood_attention(q, k, v, k_ctx, v_ctx, rpb):
    bsz, seq, heads, dh = q.shape
    rows = seq // GRID_W
    kh = min(NA_KH, rows)
    kw = NA_KW
    scale = dh ** -0.5
    q_rows = jnp.moveaxis(q.reshape(bsz, rows, GRID_W, heads, dh), 1, 0)
    k_grid = k.reshape(bsz, rows, GRID_W, heads, dh)
    v_grid = v.reshape(bsz, rows, GRID_W, heads, dh)
    col = jnp.arange(GRID_W)
    col_start = jnp.clip(col - kw // 2, 0, GRID_W - kw)
    col_idx = col_start[:, None] + jnp.arange(kw)[None, :]
    rpb_cols = rpb[:, :, col_idx - col[:, None] + (NA_KW - 1)].astype(jnp.float32)

    def row_block(args):
        q_r, r = args
        r_start = jnp.clip(r - kh // 2, 0, rows - kh)
        k_win = lax.dynamic_slice_in_dim(k_grid, r_start, kh, axis=1)[:, :, col_idx]
        v_win = lax.dynamic_slice_in_dim(v_grid, r_start, kh, axis=1)[:, :, col_idx]
        bias = rpb_cols[:, r_start + jnp.arange(kh) - r + (NA_KH - 1)]
        s_win = jnp.einsum('bqhd,bkqwhd->bhqkw', q_r, k_win).astype(jnp.float32) * scale
        s_win = s_win + jnp.transpose(bias, (0, 2, 1, 3))[None]
        s_ctx = jnp.einsum('bqhd,bchd->bhqc', q_r, k_ctx).astype(jnp.float32) * scale
        s = jnp.concatenate([s_win.reshape(bsz, heads, GRID_W, kh * kw), s_ctx], axis=-1)
        p = jax.nn.softmax(s, axis=-1).astype(v.dtype)
        p_win = p[..., :kh * kw].reshape(bsz, heads, GRID_W, kh, kw)
        p_ctx = p[..., kh * kw:]
        return (jnp.einsum('bhqkw,bkqwhd->bqhd', p_win, v_win)
                + jnp.einsum('bhqc,bchd->bqhd', p_ctx, v_ctx))

    out = lax.map(row_block, (q_rows, jnp.arange(rows)))
    return jnp.moveaxis(out, 0, 1).reshape(bsz, seq, heads * dh)

def _context_attention(q, k, v):
    bsz, clen, heads, dh = q.shape
    s = jnp.einsum('bqhd,bkhd->bhqk', q, k).astype(jnp.float32) * dh ** -0.5
    p = jax.nn.softmax(s, axis=-1).astype(v.dtype)
    return jnp.einsum('bhqk,bkhd->bqhd', p, v).reshape(bsz, clen, heads * dh)

def _sgu(u, v, ln_g, w_s, b_s):
    bsz, length, _ = u.shape
    u = jax.nn.gelu(u)
    v = _layernorm(jax.nn.gelu(v), ln_g)
    v = v.reshape(bsz, length // SGU_CHUNK, SGU_CHUNK, SGU_GROUPS, SGU_GROUP_DIM)
    mixed = jnp.einsum('hpq,bnqhd->bnphd', w_s, v) + b_s.T[:, :, None]
    return u * mixed.reshape(bsz, length, SGU_W)

def _merge(o_na, o_sgu, out_gain, w_out):
    y = jnp.concatenate([_rms(o_na), _rms(o_sgu)], axis=-1) * out_gain
    return y @ w_out

def _hier_moe(h, rg_w, rg_b, re_w, re_b, w1, w3, w2):
    shp = h.shape
    t = h.reshape(-1, D_MODEL)
    p_g = jax.nn.softmax((t @ rg_w).astype(jnp.float32) + rg_b, axis=-1)
    p_top, g_idx = lax.top_k(p_g, 1)
    e_all = jnp.einsum('nd,gde->nge', t, re_w).astype(jnp.float32) + re_b
    e_logits = jnp.take_along_axis(e_all, g_idx[:, :, None], axis=1)[:, 0]
    e_top, e_idx = lax.top_k(jax.nn.softmax(e_logits, axis=-1), TOP_K)
    w = e_top / jnp.sum(e_top, -1, keepdims=True) * p_top
    within = jnp.sum(jax.nn.one_hot(e_idx, EXPERTS_PER_GROUP, dtype=jnp.float32) * w[..., None], axis=1)
    gate = (jax.nn.one_hot(g_idx[:, 0], N_GROUPS, dtype=jnp.float32)[:, :, None]
            * within[:, None, :]).reshape(-1, N_EXPERTS).astype(t.dtype)
    out = jnp.zeros_like(t)
    for e in range(N_EXPERTS):
        hid = jax.nn.silu(t @ w1[e]) * (t @ w3[e])
        out = out + gate[:, e:e + 1] * (hid @ w2[e])
    return out.reshape(shp)

def first_inputs(seed: int = 0) -> dict:
    key = jax.random.key(seed)
    ks = jax.random.split(key, 22)

    def nrm(k, shape, s):
        return jax.random.normal(k, shape, jnp.float32) * s

    return {
        'x': nrm(ks[0], (BATCH, SEQ, D_MODEL), 1.0),
        'c': nrm(ks[1], (BATCH, D_MODEL), 1.0),
        'ctx': nrm(ks[2], (BATCH, CTX_LEN, D_MODEL), 1.0),
        'c_ctx': nrm(ks[3], (D_MODEL,), 1.0),
        'w_ada': nrm(ks[4], (DEPTH, D_MODEL, N_MOD * D_MODEL), 0.5 * D_MODEL ** -0.5),
        'b_ada': nrm(ks[5], (DEPTH, N_MOD * D_MODEL), 0.02),
        'w_in': nrm(ks[6], (DEPTH, D_MODEL, IN_COLS), D_MODEL ** -0.5),
        'q_gain': 1.0 + nrm(ks[7], (DEPTH, NA_HEAD_DIM), 0.02),
        'k_gain': 1.0 + nrm(ks[8], (DEPTH, NA_HEAD_DIM), 0.02),
        'rpb': nrm(ks[9], (DEPTH, NA_HEADS, 2 * NA_KH - 1, 2 * NA_KW - 1), 0.1),
        'sgu_ln': 1.0 + nrm(ks[10], (DEPTH, SGU_W), 0.02),
        'sgu_w': nrm(ks[11], (DEPTH, SGU_GROUPS, SGU_CHUNK, SGU_CHUNK), SGU_CHUNK ** -0.5),
        'sgu_b': 1.0 + nrm(ks[12], (DEPTH, SGU_GROUPS, SGU_CHUNK), 0.02),
        'out_gain': 1.0 + nrm(ks[13], (DEPTH, MIX_W), 0.02),
        'w_out': nrm(ks[14], (DEPTH, MIX_W, D_MODEL), MIX_W ** -0.5),
        'rg_w': nrm(ks[15], (DEPTH, D_MODEL, N_GROUPS), D_MODEL ** -0.5),
        'rg_b': nrm(ks[16], (DEPTH, N_GROUPS), 0.01),
        're_w': nrm(ks[17], (DEPTH, N_GROUPS, D_MODEL, EXPERTS_PER_GROUP), D_MODEL ** -0.5),
        're_b': nrm(ks[18], (DEPTH, N_GROUPS, EXPERTS_PER_GROUP), 0.01),
        'w1': nrm(ks[19], (DEPTH, N_EXPERTS, D_MODEL, D_EXPERT), D_MODEL ** -0.5),
        'w3': nrm(ks[20], (DEPTH, N_EXPERTS, D_MODEL, D_EXPERT), D_MODEL ** -0.5),
        'w2': nrm(ks[21], (DEPTH, N_EXPERTS, D_EXPERT, D_MODEL), D_EXPERT ** -0.5),
    }

def first_block(x, c, ctx, c_ctx, w_ada, b_ada, w_in, q_gain, k_gain, rpb, sgu_ln, sgu_w, sgu_b,
              out_gain, w_out, rg_w, rg_b, re_w, re_b, w1, w3, w2):
    for i in range(DEPTH):
        last = i == DEPTH - 1
        sh_a, sc_a, g_a, sh_f, sc_f, g_f = _adaln(c, w_ada[i], b_ada[i])
        csh_a, csc_a, cg_a, csh_f, csc_f, cg_f = _adaln(c_ctx, w_ada[i], b_ada[i])

        h = _modulate(x, sh_a[:, None], sc_a[:, None])
        hc = _modulate(ctx, csh_a, csc_a)
        q, k, v, u, vs = _project(h, w_in[i], q_gain[i], k_gain[i])
        if last:
            kc, vc = _project_kv(hc, w_in[i], k_gain[i])
        else:
            qc, kc, vc, uc, vsc = _project(hc, w_in[i], q_gain[i], k_gain[i])
        o_na = _neighborhood_attention(q, k, v, kc, vc, rpb[i])
        o_sg = _sgu(u, vs, sgu_ln[i], sgu_w[i], sgu_b[i])
        x = x + g_a[:, None] * _merge(o_na, o_sg, out_gain[i], w_out[i])

        hf = _modulate(x, sh_f[:, None], sc_f[:, None])
        x = x + g_f[:, None] * _hier_moe(hf, rg_w[i], rg_b[i], re_w[i], re_b[i], w1[i], w3[i], w2[i])

        if not last:
            oc_na = _context_attention(qc, kc, vc)
            oc_sg = _sgu(uc, vsc, sgu_ln[i], sgu_w[i], sgu_b[i])
            ctx = ctx + cg_a * _merge(oc_na, oc_sg, out_gain[i], w_out[i])
            hcf = _modulate(ctx, csh_f, csc_f)
            ctx = ctx + cg_f * _hier_moe(hcf, rg_w[i], rg_b[i], re_w[i], re_b[i], w1[i], w3[i], w2[i])
    return x


DEPTH_2 = 2

D_MIX = D_MODEL
D_CONV = D_MIX // 4
D_LRU = D_MIX // 4
D_ATTN = D_MIX // 2
CONV_KERNEL = 31
LRU_HEADS = 4
LRU_HEAD_DIM = D_LRU // LRU_HEADS
LRU_CONV = 4
LRU_C = 8.0
HEAD_DIM = 64
N_Q_HEADS = D_ATTN // HEAD_DIM
N_KV_HEADS = 2
GQA_REP = N_Q_HEADS // N_KV_HEADS
KV_DIM = N_KV_HEADS * HEAD_DIM
WINDOW = 128
BLOCK = 128
REL_BUCKETS = 32
REL_MAX_DIST = 128
D_FF = 2816
ALPHA = (2.0 * DEPTH_2) ** 0.25
BETA = (8.0 * DEPTH_2) ** -0.25
LN_EPS = 1e-5
D_IN = 2 * D_CONV + 2 * D_LRU + D_ATTN + 2 * KV_DIM


def _layernorm_2(x, g, b):
    xf = x.astype(jnp.float32)
    mu = jnp.mean(xf, axis=-1, keepdims=True)
    var = jnp.mean(jnp.square(xf - mu), axis=-1, keepdims=True)
    return ((xf - mu) * lax.rsqrt(var + LN_EPS)).astype(x.dtype) * g + b

def _swiglu(x, wg, wu, wd):
    return (jax.nn.silu(x @ wg) * (x @ wu)) @ wd

def _causal_dw_conv(x, w):
    k = w.shape[0]
    return lax.conv_general_dilated(
        x, w[:, None, :].astype(x.dtype), window_strides=(1,), padding=[(k - 1, 0)],
        dimension_numbers=('NWC', 'WIO', 'NWC'), feature_group_count=x.shape[-1])

def _conv_module(u, dw_w, dw_b, g, b):
    a, gate = jnp.split(u, 2, axis=-1)
    y = a * jax.nn.sigmoid(gate)
    y = _causal_dw_conv(y, dw_w) + dw_b
    y = _layernorm_2(y, g, b)
    return jax.nn.silu(y)

def _lin_combine(left, right):
    a1, b1 = left
    a2, b2 = right
    return a1 * a2, a2 * b1 + b2

def _recurrent(u, conv_w, conv_b, wa, ba, wx, bx, lam):
    B, S, _ = u.shape
    xb, gb = jnp.split(u, 2, axis=-1)
    xb = _causal_dw_conv(xb, conv_w) + conv_b
    xh = xb.reshape(B, S, LRU_HEADS, LRU_HEAD_DIM)
    r = jax.nn.sigmoid(jnp.einsum('bshi,hij->bshj', xh, wa).reshape(B, S, D_LRU) + ba)
    i = jax.nn.sigmoid(jnp.einsum('bshi,hij->bshj', xh, wx).reshape(B, S, D_LRU) + bx)
    log_a = LRU_C * r.astype(jnp.float32) * jax.nn.log_sigmoid(lam.astype(jnp.float32))
    a = jnp.exp(log_a)
    mult = jnp.sqrt(-jnp.expm1(2.0 * log_a))
    bterm = mult * (i * xb).astype(jnp.float32)
    _, h = lax.associative_scan(_lin_combine, (a, bterm), axis=1)
    return h.astype(u.dtype) * jax.nn.gelu(gb)

def _rel_bucket(dist):
    max_exact = REL_BUCKETS // 2
    is_small = dist < max_exact
    large = max_exact + (jnp.log(jnp.maximum(dist, 1).astype(jnp.float32) / max_exact)
                         / math.log(REL_MAX_DIST / max_exact)
                         * (REL_BUCKETS - max_exact)).astype(jnp.int32)
    large = jnp.minimum(large, REL_BUCKETS - 1)
    return jnp.where(is_small, dist, large)

def _band_bias_and_mask(rel_bias, seq):
    nb = seq // BLOCK
    qi = jnp.arange(BLOCK)[:, None]
    kj = jnp.arange(2 * BLOCK)[None, :]
    dist = qi - kj + BLOCK
    bucket = _rel_bucket(jnp.maximum(dist, 0))
    bias = rel_bias[bucket].astype(jnp.float32)
    bias = jnp.transpose(bias, (2, 0, 1)).reshape(N_KV_HEADS, GQA_REP, BLOCK, 2 * BLOCK)
    blk = jnp.arange(nb)[:, None, None]
    valid = (dist >= 0) & (dist < WINDOW) & (blk * BLOCK + kj - BLOCK >= 0)
    return bias, valid

def _band(t, nb):
    B = t.shape[0]
    tp = jnp.pad(t, ((0, 0), (BLOCK, 0), (0, 0), (0, 0)))
    tp = tp.reshape(B, nb + 1, BLOCK, t.shape[2], t.shape[3])
    return jnp.concatenate([tp[:, :-1], tp[:, 1:]], axis=2)

def _swa(q, k, v, band_bias, valid, sinks):
    B, S, _ = q.shape
    nb = S // BLOCK
    qb = q.reshape(B, nb, BLOCK, N_KV_HEADS, GQA_REP, HEAD_DIM)
    kb = _band(k.reshape(B, S, N_KV_HEADS, HEAD_DIM), nb)
    vb = _band(v.reshape(B, S, N_KV_HEADS, HEAD_DIM), nb)
    s = jnp.einsum('bnqgrd,bnkgd->bngrqk', qb, kb).astype(jnp.float32) * (HEAD_DIM ** -0.5)
    s = s + band_bias[None, None]
    s = jnp.where(valid[None, :, None, None], s, -1e30)
    sink = jnp.broadcast_to(sinks.astype(jnp.float32).reshape(1, 1, N_KV_HEADS, GQA_REP, 1, 1),
                            s.shape[:-1] + (1,))
    p = jax.nn.softmax(jnp.concatenate([s, sink], axis=-1), axis=-1)[..., :-1]
    o = jnp.einsum('bngrqk,bnkgd->bnqgrd', p.astype(vb.dtype), vb)
    return o.reshape(B, S, D_ATTN)

def _mixer(x, w_in, conv_dw_w, conv_dw_b, conv_ln_g, conv_ln_b, lru_conv_w, lru_conv_b,
           lru_wa, lru_ba, lru_wx, lru_bx, lru_lambda, sinks, w_out, band_bias, valid):
    u = x @ w_in
    o1 = 2 * D_CONV
    o2 = o1 + 2 * D_LRU
    o3 = o2 + D_ATTN
    o4 = o3 + KV_DIM
    u_conv, u_lru, q, k, v = jnp.split(u, [o1, o2, o3, o4], axis=-1)
    y_conv = _conv_module(u_conv, conv_dw_w, conv_dw_b, conv_ln_g, conv_ln_b)
    y_lru = _recurrent(u_lru, lru_conv_w, lru_conv_b, lru_wa, lru_ba, lru_wx, lru_bx, lru_lambda)
    y_attn = _swa(q, k, v, band_bias, valid, sinks)
    return jnp.concatenate([y_conv, y_lru, y_attn], axis=-1) @ w_out

def second_inputs(seed: int = 0) -> dict:
    key = jax.random.key(seed)
    ks = jax.random.split(key, 24)
    f32 = jnp.float32
    nrm = lambda k, shape, scale: jax.random.normal(k, shape, f32) * scale
    x = nrm(ks[0], (BATCH, SEQ, D_MODEL), 1.0)
    rel_bias = nrm(ks[1], (REL_BUCKETS, N_Q_HEADS), 0.5)
    ln_g = 1.0 + nrm(ks[2], (DEPTH_2, 3, D_MODEL), 0.1)
    ln_b = nrm(ks[3], (DEPTH_2, 3, D_MODEL), 0.02)
    ffn_w_gate = nrm(ks[4], (DEPTH_2, 2, D_MODEL, D_FF), D_MODEL ** -0.5)
    ffn_w_up = nrm(ks[5], (DEPTH_2, 2, D_MODEL, D_FF), D_MODEL ** -0.5)
    ffn_w_down = nrm(ks[6], (DEPTH_2, 2, D_FF, D_MODEL), BETA * D_FF ** -0.5)
    w_in = nrm(ks[7], (DEPTH_2, D_MODEL, D_IN), D_MODEL ** -0.5)
    conv_dw_w = nrm(ks[8], (DEPTH_2, CONV_KERNEL, D_CONV), CONV_KERNEL ** -0.5)
    conv_dw_b = nrm(ks[9], (DEPTH_2, D_CONV), 0.02)
    conv_ln_g = 1.0 + nrm(ks[10], (DEPTH_2, D_CONV), 0.1)
    conv_ln_b = nrm(ks[11], (DEPTH_2, D_CONV), 0.02)
    lru_conv_w = nrm(ks[12], (DEPTH_2, LRU_CONV, D_LRU), LRU_CONV ** -0.5)
    lru_conv_b = nrm(ks[13], (DEPTH_2, D_LRU), 0.02)
    lru_wa = nrm(ks[14], (DEPTH_2, LRU_HEADS, LRU_HEAD_DIM, LRU_HEAD_DIM), LRU_HEAD_DIM ** -0.5)
    lru_ba = nrm(ks[15], (DEPTH_2, D_LRU), 0.02)
    lru_wx = nrm(ks[16], (DEPTH_2, LRU_HEADS, LRU_HEAD_DIM, LRU_HEAD_DIM), LRU_HEAD_DIM ** -0.5)
    lru_bx = nrm(ks[17], (DEPTH_2, D_LRU), 0.02)
    a_init = jax.random.uniform(ks[18], (DEPTH_2, D_LRU), f32, 0.9, 0.999)
    sig = a_init ** (1.0 / LRU_C)
    lru_lambda = jnp.log(sig) - jnp.log1p(-sig)
    attn_sinks = nrm(ks[19], (DEPTH_2, N_Q_HEADS), 0.5)
    w_out = nrm(ks[20], (DEPTH_2, D_MIX, D_MODEL), BETA * D_MIX ** -0.5)
    return {'x': x, 'rel_bias': rel_bias, 'ln_g': ln_g, 'ln_b': ln_b,
            'ffn_w_gate': ffn_w_gate, 'ffn_w_up': ffn_w_up, 'ffn_w_down': ffn_w_down,
            'w_in': w_in, 'conv_dw_w': conv_dw_w, 'conv_dw_b': conv_dw_b,
            'conv_ln_g': conv_ln_g, 'conv_ln_b': conv_ln_b,
            'lru_conv_w': lru_conv_w, 'lru_conv_b': lru_conv_b,
            'lru_wa': lru_wa, 'lru_ba': lru_ba, 'lru_wx': lru_wx, 'lru_bx': lru_bx,
            'lru_lambda': lru_lambda, 'attn_sinks': attn_sinks, 'w_out': w_out}

def second_block(x, rel_bias, ln_g, ln_b, ffn_w_gate, ffn_w_up, ffn_w_down, w_in,
              conv_dw_w, conv_dw_b, conv_ln_g, conv_ln_b, lru_conv_w, lru_conv_b,
              lru_wa, lru_ba, lru_wx, lru_bx, lru_lambda, attn_sinks, w_out):
    band_bias, valid = _band_bias_and_mask(rel_bias, x.shape[1])
    for l in range(DEPTH_2):
        h = 0.5 * _swiglu(x, ffn_w_gate[l, 0], ffn_w_up[l, 0], ffn_w_down[l, 0])
        x = _layernorm_2(ALPHA * x + h, ln_g[l, 0], ln_b[l, 0])
        h = _mixer(x, w_in[l], conv_dw_w[l], conv_dw_b[l], conv_ln_g[l], conv_ln_b[l],
                   lru_conv_w[l], lru_conv_b[l], lru_wa[l], lru_ba[l], lru_wx[l], lru_bx[l],
                   lru_lambda[l], attn_sinks[l], w_out[l], band_bias, valid)
        x = _layernorm_2(ALPHA * x + h, ln_g[l, 1], ln_b[l, 1])
        h = 0.5 * _swiglu(x, ffn_w_gate[l, 1], ffn_w_up[l, 1], ffn_w_down[l, 1])
        x = _layernorm_2(ALPHA * x + h, ln_g[l, 2], ln_b[l, 2])
    return x


def setup_inputs(seed=0):
    out = dict(first_inputs(seed))
    for name, value in second_inputs(seed + 1).items():
        if name != "x":
            out[name + "_2"] = value
    return out


def reference(
    x, c, ctx, c_ctx, w_ada, b_ada, w_in, q_gain, k_gain, rpb, sgu_ln, sgu_w, sgu_b, out_gain,
    w_out, rg_w, rg_b, re_w, re_b, w1, w3, w2, rel_bias_2, ln_g_2, ln_b_2, ffn_w_gate_2,
    ffn_w_up_2, ffn_w_down_2, w_in_2, conv_dw_w_2, conv_dw_b_2, conv_ln_g_2, conv_ln_b_2,
    lru_conv_w_2, lru_conv_b_2, lru_wa_2, lru_ba_2, lru_wx_2, lru_bx_2, lru_lambda_2,
    attn_sinks_2, w_out_2,
):
    x = first_block(
        x, c, ctx, c_ctx, w_ada, b_ada, w_in, q_gain, k_gain, rpb, sgu_ln, sgu_w, sgu_b,
        out_gain, w_out, rg_w, rg_b, re_w, re_b, w1, w3, w2,
    )
    return second_block(
        x, rel_bias_2, ln_g_2, ln_b_2, ffn_w_gate_2, ffn_w_up_2, ffn_w_down_2, w_in_2,
        conv_dw_w_2, conv_dw_b_2, conv_ln_g_2, conv_ln_b_2, lru_conv_w_2, lru_conv_b_2,
        lru_wa_2, lru_ba_2, lru_wx_2, lru_bx_2, lru_lambda_2, attn_sinks_2, w_out_2,
    )


_drawn_inputs = setup_inputs


def setup_inputs(seed=0):
    import zlib

    import numpy as np

    out = dict(_drawn_inputs(seed))
    spreads = {}
    factors = {'q_gain': 8.0,
     'k_gain': 8.0,
     'rpb': 8.0,
     'sgu_ln': 200.0,
     'sgu_b': 200.0,
     'out_gain': 16.587,
     'rg_b': 200.0,
     're_b': 200.0,
     'conv_dw_b_2': 8.0,
     'conv_ln_g_2': 3.138,
     'conv_ln_b_2': 8.0,
     'lru_conv_b_2': 3.857,
     'lru_ba_2': 64.0,
     'lru_bx_2': 31.638,
     'attn_sinks_2': 23.436,
     'rg_w': 2.889,
     're_w': 3.533,
     'w1': 2.746,
     'rel_bias_2': 2.782}
    for name, (base, spread) in spreads.items():
        noise = np.random.default_rng([zlib.crc32(name.encode()), seed]).standard_normal(out[name].shape)
        drawn = base * np.exp(spread * noise) if base else spread * noise
        out[name] = __import__('jax').numpy.asarray(drawn.astype(out[name].dtype))
    for name, factor in factors.items():
        out[name] = (out[name] * factor).astype(out[name].dtype)
    return out
```

```python
import concourse.bass as bass
from concourse import mybir
from contextlib import ExitStack
import numpy as np
import math

f32 = mybir.dt.float32
f32r = mybir.dt.float32r
ALU = mybir.AluOpType
ACT = mybir.ActivationFunctionType
AX = mybir.AxisListType
ds = bass.ds

P = 128
SEQ = 512
D = 1024
KC = D // P
TB = SEQ // P
HALF = 512
LAYERS = 2
D_FF = 2816
FC = D_FF // P
ALPHA = (2.0 * LAYERS) ** 0.25
LN_EPS = 1e-5
N_UP = 2 * FC
N_DOWN = FC
N_FFN = N_UP + N_DOWN
N_MIN = 14
N_MOUT = 8
N_LAYER = 2 * N_FFN + N_MIN + N_MOUT
HD = 64
CONV_K = 31
LRU_K = 4
LRU_C = 8.0
QH = 8
BAND = 2 * P
NEG = -1e30
REL_BUCKETS = 32
REL_MAX_DIST = 128


CTX = 256
CB_ = CTX // P
EPS = 1e-6
NCOL = 5
NB_ROWS = 8
GRID = 64
KW = 16
RP = 2 * GRID - 1
NDR = 15
GROUPS, EPG, EXPERTS = 4, 4, 16
D_EXP = 512
MAX_BLOCKS = 23
N_WIN = 4 * 7
AW = 256
AN = D // AW
N_FIRST = N_WIN + 8


class Tile:

    def __init__(self, at, pairs=0):
        self.at, self.pairs, self.slot = at, pairs, at % 2

    def plus(self, n):
        return self.at + n + 2 * self.pairs

    def loads(self):
        return 16 * (self.at // 2 + 1) + 16 * self.pairs


class Shared:
    pass


def shared(nc, ctx):
    S = Shared()
    sb = lambda n, shape, dt=f32: ctx.enter_context(nc.sbuf_tensor(n, shape, dt))
    sem = lambda n: ctx.enter_context(nc.semaphore(n))
    S.xtok = sb("xtok", [P, TB, D])
    S.xT_hi = sb("xT_hi", [P, KC, SEQ], f32r)
    S.xT_lo = sb("xT_lo", [P, KC, SEQ], f32r)
    S.raw = sb("w_raw", [P, 2, D])
    S.whi = sb("w_part_hi", [P, 2, D], f32r)
    S.wlo = sb("w_part_lo", [P, 2, D], f32r)
    S.ident = sb("identity", [P, P])
    S.PS = ctx.enter_context(nc.psum_tensor("PS", [P, 8, 512], f32))
    S.w_loaded = [sem("w_loaded0"), sem("w_loaded1")]
    S.w_hi, S.w_lo, S.w_used = sem("w_hi_ready"), sem("w_lo_ready"), sem("w_used")
    return S


def first_block(nc, ctx0, S, A, stop=None):
    xtok, xT_hi, xT_lo, raw, whi, wlo, ident, PS = S.xtok, S.xT_hi, S.xT_lo, S.raw, S.whi, S.wlo, S.ident, S.PS
    w_loaded, w_hi, w_lo, w_used = S.w_loaded, S.w_hi, S.w_lo, S.w_used
    ctx = ctx0.enter_context(ExitStack())

    def sem(n):
        return ctx0.enter_context(nc.semaphore(n))

    def sb(c, n, shape, dt=f32):
        return c.enter_context(nc.sbuf_tensor(n, shape, dt))

    def load_tile(sp, t, src):
        if t.plus(-1) > 0:
            sp.wait_ge(w_lo, t.plus(-1))
        sp.dma_start(raw[:, t.slot, :].rearrange("p (a n) -> p a n", n=src.shape[-1]), src).then_inc(w_loaded[t.slot], 16)

    def split_hi(t):
        nc.scalar.wait_ge(w_loaded[t.slot], t.loads())
        if t.plus(-1) > 0:
            nc.scalar.wait_ge(w_used, t.plus(-1))
        nc.scalar.activation(whi[:, t.slot, :], raw[:, t.slot, :], ACT.Copy).then_inc(w_hi, 1)

    def split_lo(t):
        nc.vector.wait_ge(w_hi, t.plus(1))
        nc.vector.tensor_tensor(wlo[:, t.slot, :], raw[:, t.slot, :], whi[:, t.slot, :].bitcast(f32), ALU.subtract).then_inc(w_lo, 1)

    def product(out, a, a_at, b, b_at, first, last):
        nc.tensor.matmul(out, a[0][a_at], b[0][b_at], start=first, stop=False)
        nc.tensor.matmul(out, a[0][a_at], b[1][b_at], start=False, stop=False)
        return nc.tensor.matmul(out, a[1][a_at], b[0][b_at], start=False, stop=last)

    W = (whi, wlo)
    XT = (xT_hi, xT_lo)

    ga_row = sb(ctx, "ga_row", [P, D])
    gf_row = sb(ctx, "gf_row", [P, D])
    modT = sb(ctx, "modT", [P, 4, KC, 2])
    eps6 = sb(ctx, "eps6", [P, 1])
    ssum = sb(ctx, "sum_of_squares", [P, 8])
    tmp = sb(ctx, "evac_tmp1", [P, 2, SEQ])
    out_gT = sb(ctx, "out_gainT", [P, KC])
    rpad_rows = nc.dram_tensor("rpb_rows", [8 * NDR, GRID, RP], f32, kind="Internal").ap()
    ys = nc.dram_tensor("expert_rows", [MAX_BLOCKS * P, D], f32, kind="Internal").ap()

    keep = ctx.enter_context(ExitStack())
    v_tok = sb(keep, "v_tok", [P, TB + CB_, HALF])
    ug = sb(keep, "u_gelu", [P, TB, HALF])
    vs = sb(keep, "vs_tok", [P, TB, HALF])
    qT = sb(keep, "qT1", [P, 4, SEQ])
    kT = sb(keep, "kT1", [P, 4, SEQ + CTX])
    qk_gain = sb(keep, "qk_gain", [P, 2])

    s_in, s_c, s_cb, s_scb = sem("x_loaded"), sem("c_loaded"), sem("c_silu"), sem("c_bcast")
    s_aw = [sem("ada_w0"), sem("ada_w1")]
    s_mm, s_mod, s_bias = sem("ada_mm"), sem("ada_out"), sem("ada_bias")
    s_ss, s_rt, s_rpb, s_rpr, s_rps = sem("ssum_ready"), sem("ssum_root"), sem("rpb_in"), sem("rpb_rows_sem"), sem("rpb_pad")
    s_xn = sem("xn_ready")
    proj = ExitStack()
    q_tok = sb(proj, "q_tok", [P, TB, HALF])
    k_tok = sb(proj, "k_tok", [P, TB + CB_, HALF])
    sqb = sb(proj, "square_buf", [P, TB, HALF])
    hsum = sb(proj, "head_sums", [P, 3, TB * 8])
    ln_row = sb(proj, "sgu_ln_row", [P, HALF])
    norm = ExitStack()
    xn = sb(norm, "xn", [P, TB + CB_, D])
    ada = ExitStack()
    wada = sb(ada, "wada", [P, 2, KC, AW])
    sc2 = sb(ada, "silu_c", [P, KC, 2])
    c2 = sb(ada, "c_in", [P, KC, 2])
    scb = sqb[:, 0:2, :].rearrange("p a n -> p (a n)").rearrange("p (k m) -> p k m", m=P)
    b_adaT = sb(ada, "b_adaT", [P, 6, KC])
    rpad = sb(ada, "rpb_padded", [8 * NDR, RP])
    turns = [("f", 0, 0), ("f", 1, 1), ("r", 2, ga_row), ("f", 3, 2), ("f", 4, 3), ("r", 5, gf_row)]
    with nc.Block() as block:
        @block.sync
        def _(sp):
            sp.dma_start(c2[:, :, :], A["cT"]).then_inc(s_c, 16)
            sp.dma_start(b_adaT[:, :, :], A["b_adaT"]).then_inc(s_bias, 16)
            sp.dma_start(ga_row[:, :], A["b_ada"][0, 2 * D:3 * D].partition_broadcast(P)).then_inc(s_bias, 16)
            sp.dma_start(gf_row[:, :], A["b_ada"][0, 5 * D:6 * D].partition_broadcast(P)).then_inc(s_bias, 16)
            for n, (_, sec, _) in enumerate(turns):
                for h in range(AN):
                    i = AN * n + h
                    if i >= 2:
                        sp.wait_ge(s_mm, i - 1)
                    sp.dma_start(wada[:, i % 2, :, :], A["w_ada"][0, :, sec * D + h * AW:sec * D + (h + 1) * AW].rearrange("(k p) n -> p k n", p=P)).then_inc(s_aw[i % 2], 16)

        @block.gpsimd
        def _(pool):
            nc.gpsimd.memset(rpad[:, :], 0.0)
            nc.gpsimd.memset(eps6[:, :], EPS)
            pool.drain().then_inc(s_rps, 1)

        @block.scalar
        def _(act):
            act.dma_start(xtok[:, :, :], A["x"][0].rearrange("(b p) d -> p b d", p=P)).then_inc(s_in, 16)
            act.dma_start(xn[:, TB:, :], A["ctx"][0].rearrange("(b p) d -> p b d", p=P)).then_inc(s_in, 16)
            act.dma_start(ident[:, :], A["ident"]).then_inc(s_in, 16)
            act.dma_start(ln_row[:, :], A["sgu_ln"][0].partition_broadcast(P)).then_inc(s_in, 16)
            act.dma_start(out_gT[:, :], A["out_gainT"]).then_inc(s_in, 16)
            act.dma_start(qk_gain[:, :], A["qk_gainT"]).then_inc(s_in, 16)
            act.wait_ge(s_rps, 1)
            act.dma_start(rpad[:, 48:79], A["rpb"][0].rearrange("h r w -> (h r) w")).then_inc(s_rpb, 16)
            act.wait_ge(s_rpb, 16)
            act.dma_start(rpad_rows, rpad[:, :].unsqueeze(1).to_broadcast([8 * NDR, GRID, RP])).then_inc(s_rpr, 16)
            act.wait_ge(s_c, 16)
            nc.scalar.activation(sc2[:, :, :], c2[:, :, :], ACT.Silu).then_inc(s_cb, 1)
            act.wait_ge(s_in, 96)
            for b in range(TB):
                nc.scalar.activation(xn[:, b, :], xtok[:, b, :], ACT.Square, accum_out=ssum[:, b:b + 1])
            for b in range(CB_):
                nc.scalar.activation(xT_lo[:, 0:2, :].rearrange("p a n -> p (a n)"), xn[:, TB + b, :], ACT.Square, accum_out=ssum[:, TB + b:TB + b + 1])
                act.drain()
            nc.scalar.activation(ssum[:, 0:6], ssum[:, 0:6], ACT.Sqrt, bias=eps6[:, 0:1], scale=1.0 / D).then_inc(s_rt, 1)
            act.wait_ge(s_rpr, 16)

        @block.vector
        def _(dve):
            dve.wait_ge(s_cb, 1)
            nc.vector.tensor_copy(scb, sc2[:, :, 0:1].to_broadcast([P, KC, P])).then_inc(s_scb, 1)
            dve.wait_ge(s_rt, 1)
            nc.vector.reciprocal(ssum[:, 0:6], ssum[:, 0:6])
            dve.drain()
            for b in range(TB):
                nc.vector.tensor_scalar(xn[:, b, :], xtok[:, b, :], ssum[:, b:b + 1], None, ALU.mult)
            for b in range(CB_):
                nc.vector.tensor_scalar(xn[:, TB + b, :], xn[:, TB + b, :], ssum[:, TB + b:TB + b + 1], None, ALU.mult)
            nc.vector.tensor_tensor(qk_gain[:, 0:1], qk_gain[:, 0:1], qk_gain[:, 1:2], ALU.mult)
            dve.drain()
            nc.vector.tensor_scalar(qk_gain[:, 0:1], qk_gain[:, 0:1], HD ** -0.5, None, ALU.mult)
            dve.wait_ge(s_bias, 48)
            for n, (kind, sec, dst) in enumerate(turns):
                for h in range(AN):
                    i = AN * n + h
                    dve.wait_ge(s_mm, i + 1)
                    if kind == "f":
                        nc.vector.tensor_tensor(modT[:, dst, AW // P * h:AW // P * (h + 1), :], PS[:, i % 2, 0:2 * AW // P].rearrange("p (c v) -> p c v", v=2),
                                                b_adaT[:, sec, AW // P * h:AW // P * (h + 1)].unsqueeze(2).to_broadcast([P, AW // P, 2]), ALU.add).then_inc(s_mod, 1)
                    else:
                        nc.vector.tensor_tensor(dst[:, h * AW:(h + 1) * AW], PS[:, i % 2, 0:AW], dst[:, h * AW:(h + 1) * AW], ALU.add).then_inc(s_mod, 1)
            dve.drain()
            for k in (1, 3):
                nc.vector.tensor_scalar(modT[:, k, :, :], modT[:, k, :, :], 1.0, None, ALU.add)

        @block.tensor
        def _(pe):
            pe.wait_ge(s_scb, 1)
            for n, (kind, sec, _) in enumerate(turns):
                for h in range(AN):
                    i = AN * n + h
                    pe.wait_ge(s_aw[i % 2], 16 * (i // 2 + 1))
                    if i >= 2:
                        pe.wait_ge(s_mod, i - 1)
                    if kind == "f":
                        for c in range(AW // P):
                            for kc in range(KC):
                                last = nc.tensor.matmul(PS[:, i % 2, 2 * c:2 * c + 2], wada[:, i % 2, kc, c * P:(c + 1) * P], sc2[:, kc, :], start=kc == 0, stop=kc == KC - 1, skip_group_check=True)
                    else:
                        for kc in range(KC):
                            last = nc.tensor.matmul(PS[:, i % 2, 0:AW], scb[:, kc, :], wada[:, i % 2, kc, :], start=kc == 0, stop=kc == KC - 1)
                    last.then_inc(s_mm, 1)
    ada.close()
    hcT = ExitStack()
    hc_hi = sb(hcT, "hc_hi", [P, KC, CTX], f32r)
    hc_lo = sb(hcT, "hc_lo", [P, KC, CTX], f32r)
    HC = (hc_hi, hc_lo)

    def modulate_act(act, tr, ready, n0, count, hi, width, sh, col):
        for kc in range(KC):
            act.wait_ge(tr, n0 + kc + 1)
            if n0 + kc >= 2:
                act.wait_ge(ready, n0 + kc - 1)
            s, b = modT[:, sh + 1, kc, col:col + 1], modT[:, sh, kc, col:col + 1]
            nc.scalar.activation(tmp[:, kc % 2, 0:width], PS[:, kc, 0:width], ACT.Identity, bias=b, scale=s)
            nc.scalar.activation(hi[:, kc, :], PS[:, kc, 0:width], ACT.Identity, bias=b, scale=s).then_inc(count, 1)

    tr1, hi1, rd1, evac1 = sem("h_tr"), sem("h_hi"), sem("h_ready"), sem("proj_evac")
    nv, nr, lnv = sem("head_sq"), sem("head_root"), sem("vs_norm")
    cols = [0, 1, 2, 3, 4, 1, 2]
    with nc.Block() as block:
        @block.sync
        def _(sp):
            for n in range(N_WIN):
                g, kp = n // 4, n % 4
                load_tile(sp, Tile(n), A["w_in"][0, kp * 2 * P:(kp + 1) * 2 * P, cols[g] * HALF:(cols[g] + 1) * HALF].rearrange("(k p) n -> p k n", p=P))

        @block.tensor
        def _(pe):
            for kc in range(KC):
                for b in range(TB):
                    last = nc.tensor.transpose(PS[:, kc, b * P:(b + 1) * P], xn[:, b, kc * P:(kc + 1) * P], ident[:, :])
                last.then_inc(tr1, 1)
            for kc in range(KC):
                pe.wait_ge(rd1, kc + 1)
                for b in range(CB_):
                    last = nc.tensor.transpose(PS[:, kc, b * P:(b + 1) * P], xn[:, TB + b, kc * P:(kc + 1) * P], ident[:, :])
                last.then_inc(tr1, 1)
            pe.wait_ge(rd1, 2 * KC)
            for n in range(N_WIN):
                g, kp = n // 4, n % 4
                t = Tile(n)
                pe.wait_ge(w_lo, t.plus(1))
                if kp == 0 and g >= 2:
                    pe.wait_ge(evac1, g - 1)
                src, nb = (XT, TB) if g < NCOL else (HC, CB_)
                for kk in range(2):
                    kc = 2 * kp + kk
                    for b in range(nb):
                        last = product(PS[:, 4 * (g % 2) + b, :], src, (slice(None), kc, slice(b * P, (b + 1) * P)), W, (slice(None), t.slot, slice(kk * HALF, (kk + 1) * HALF)), kc == 0, kc == KC - 1)
                last.then_inc(w_used, 1)

        @block.scalar
        def _(act):
            split_hi(Tile(0))
            split_hi(Tile(1))
            modulate_act(act, tr1, rd1, 0, hi1, xT_hi, SEQ, 0, 0)
            modulate_act(act, tr1, rd1, KC, hi1, hc_hi, CTX, 0, 1)
            dst = [(q_tok[:, :, :], ACT.Copy), (k_tok[:, 0:TB, :], ACT.Copy), (v_tok[:, 0:TB, :], ACT.Copy), (ug[:, :, :], ACT.Gelu_apprx_tanh),
                   (vs[:, :, :], ACT.Gelu_apprx_tanh), (k_tok[:, TB:, :], ACT.Copy), (v_tok[:, TB:, :], ACT.Copy)]
            for g in range(7):
                for kp in range(4):
                    n = 4 * g + kp + 2
                    if n < N_WIN:
                        split_hi(Tile(n))
                    if kp == 2 and g in (1, 2, 6):
                        r = {1: 0, 2: 1, 6: 2}[g]
                        act.wait_ge(nv, r + 1)
                        w = TB * 8 if g != 6 else CB_ * 8
                        nc.scalar.activation(hsum[:, r, 0:w], hsum[:, r, 0:w], ACT.Sqrt, bias=eps6[:, 0:1], scale=1.0 / HD).then_inc(nr, 1)
                    if kp == 2 and g == 5:
                        act.wait_ge(lnv, 1)
                        nc.scalar.activation(ssum[:, 0:TB], ssum[:, 0:TB], ACT.Sqrt, bias=eps6[:, 0:1]).then_inc(lnv, 1)
                act.wait_ge(w_used, 4 * (g + 1))
                d, fn = dst[g]
                nb = d.shape[1]
                nc.scalar.activation(d, PS[:, 4 * (g % 2):4 * (g % 2) + nb, :], fn).then_inc(evac1, 1)

        @block.vector
        def _(dve):
            V = nc.vector
            split_lo(Tile(0))
            split_lo(Tile(1))
            for i in range(2 * KC):
                kc = i % KC
                dve.wait_ge(hi1, i + 1)
                if i < KC:
                    V.tensor_tensor(xT_lo[:, kc, :], tmp[:, kc % 2, :], xT_hi[:, kc, :].bitcast(f32), ALU.subtract).then_inc(rd1, 1)
                else:
                    V.tensor_tensor(hc_lo[:, kc, :], tmp[:, kc % 2, 0:CTX], hc_hi[:, kc, :].bitcast(f32), ALU.subtract).then_inc(rd1, 1)

            def head_norm(step, src, nb, r):
                s3 = src.rearrange("p b (h d) -> p (b h) d", d=HD)
                q3 = sqb[:, 0:nb, :].rearrange("p b (h d) -> p (b h) d", d=HD)
                if step == 0:
                    V.tensor_tensor(sqb[:, 0:nb, :], src, src, ALU.mult)
                    dve.drain()
                if step == 1:
                    V.tensor_reduce(hsum[:, r, 0:8 * nb], q3, AX.X, ALU.add).then_inc(nv, 1)
                if step == 2:
                    dve.wait_ge(nr, r + 1)
                    V.reciprocal(hsum[:, r, 0:8 * nb], hsum[:, r, 0:8 * nb])
                    dve.drain()
                if step == 3:
                    V.tensor_tensor(s3, s3, hsum[:, r, 0:8 * nb].unsqueeze(2).to_broadcast([P, 8 * nb, HD]), ALU.mult)

            def vs_norm(step):
                if step == 0:
                    for b in range(TB):
                        V.bn_stats(sqb[:, 0, 6 * b:6 * b + 6], vs[:, b, :])
                    dve.drain()
                if step == 1:
                    for b in range(TB):
                        V.bn_aggr(sqb[:, 1, 2 * b:2 * b + 2], sqb[:, 0, 6 * b:6 * b + 6])
                    dve.drain()
                    V.tensor_copy(ssum[:, 0:TB], sqb[:, 1, 0:2 * TB].rearrange("p (b v) -> p b v", v=2)[:, :, 1]).then_inc(lnv, 1)
                if step == 2:
                    dve.wait_ge(lnv, 2)
                    V.reciprocal(ssum[:, 0:TB], ssum[:, 0:TB])
                    dve.drain()
                    for b in range(TB):
                        V.tensor_scalar(vs[:, b, :], vs[:, b, :], sqb[:, 1, 2 * b:2 * b + 1], ssum[:, b:b + 1], ALU.subtract, ALU.mult)
                if step == 3:
                    dve.drain()
                    V.tensor_tensor(vs[:, :, :], vs[:, :, :], ln_row[:, :].unsqueeze(1).to_broadcast([P, TB, HALF]), ALU.mult)
                    dve.drain()

            for g in range(7):
                for kp in range(4):
                    n = 4 * g + kp + 2
                    if n < N_WIN:
                        split_lo(Tile(n))
                    if g >= 1 and kp == 0:
                        dve.wait_ge(evac1, g)
                    if g == 1:
                        head_norm(kp, q_tok[:, :, :], TB, 0)
                    if g == 2:
                        head_norm(kp, k_tok[:, 0:TB, :], TB, 1)
                    if g == 5:
                        vs_norm(kp)
                    if g == 6:
                        head_norm(kp, k_tok[:, TB:, :], CB_, 2)
    hcT.close()
    norm.close()

    table = ctx.enter_context(ExitStack())
    tq, ev3, sg, so = sem("qk_tr"), sem("qk_evac"), sem("sgu_mm"), sem("sgu_out")
    s_w, s_tab = sem("sgu_w_loaded"), sem("nb_table")
    nbt = sb(proj, "nb_bias", [P, 8, 16 * GRID])
    nbm = sb(proj, "nb_mask", [P, GRID])
    wsT = sb(proj, "sgu_wT", [P, 8, P])
    bsT = sb(proj, "sgu_bT", [P, 8])
    sgr = sem("sgu_ss")
    with nc.Block() as block:
        @block.sync
        def _(sp):
            sp.dma_start(wsT[:, :, :], A["sgu_wT"]).then_inc(s_w, 16)
            sp.dma_start(bsT[:, :], A["sgu_bT"]).then_inc(s_w, 16)
            sp.dma_start(nbm[:, :], A["nb_mask"]).then_inc(s_tab, 16)
            for up in range(2):
                for h in range(8):
                    skew = bass.AP(rpad_rows.tensor, h * NDR * GRID * RP + GRID - 1, [[RP - 1, GRID], [GRID * RP, NDR], [1, GRID]])
                    sp.dma_start(nbt[up * GRID:(up + 1) * GRID, h, up * GRID:(up + NDR) * GRID].rearrange("p (r k) -> p r k", k=GRID), skew).then_inc(s_tab, 16)

        @block.gpsimd
        def _(pool):
            pool.wait_ge(s_tab, 16 * 17)
            for up in range(2):
                at = slice(up * GRID, (up + 1) * GRID)
                for h in range(8):
                    t = nbt[at, h, up * GRID:(up + NDR) * GRID].rearrange("p (r k) -> p r k", k=GRID)
                    nc.gpsimd.tensor_tensor(t, t, nbm[at, :].unsqueeze(1).to_broadcast([GRID, NDR, GRID]), ALU.add)

        @block.tensor
        def _(pe):
            for c in range(4):
                for b in range(TB):
                    last = nc.tensor.transpose(PS[:, c, b * P:(b + 1) * P], q_tok[:, b, c * P:(c + 1) * P], ident[:, :])
                last.then_inc(tq, 1)
                for b in range(TB):
                    last = nc.tensor.transpose(PS[:, 4 + c, b * P:(b + 1) * P], k_tok[:, b, c * P:(c + 1) * P], ident[:, :])
                last.then_inc(tq, 1)
            for c in range(4):
                pe.wait_ge(ev3, 2 * c + 1)
                for b in range(CB_):
                    last = nc.tensor.transpose(PS[:, c, b * P:(b + 1) * P], k_tok[:, TB + b, c * P:(c + 1) * P], ident[:, :])
                last.then_inc(tq, 1)
            pe.wait_ge(s_w, 32)
            pe.wait_ge(ev3, 8)
            for h in range(8):
                last = nc.tensor.matmul(PS[:, 4 + h // 2, (h % 2) * 256:(h % 2 + 1) * 256].rearrange("p (b d) -> p b d", d=HD), wsT[:, h, :], vs[:, :, h * HD:(h + 1) * HD], start=True, stop=True, skip_group_check=True)
                last.then_inc(sg, 1)

        @block.scalar
        def _(act):
            for c in range(4):
                act.wait_ge(tq, 2 * c + 1)
                nc.scalar.activation(qT[:, c, :], PS[:, c, :], ACT.Copy, scale=qk_gain[:, 0:1]).then_inc(ev3, 1)
                act.wait_ge(tq, 2 * c + 2)
                nc.scalar.activation(kT[:, c, 0:SEQ], PS[:, 4 + c, :], ACT.Copy).then_inc(ev3, 1)
            for c in range(4):
                act.wait_ge(tq, 8 + c + 1)
                nc.scalar.activation(kT[:, c, SEQ:], PS[:, c, 0:CTX], ACT.Copy).then_inc(ev3, 1)
            act.wait_ge(so, 8)
            for b in range(TB):
                nc.scalar.activation(vs[:, b, :], ug[:, b, :], ACT.Square, accum_out=ssum[:, b:b + 1])
            act.drain()
            nc.scalar.activation(ssum[:, 0:TB], ssum[:, 0:TB], ACT.Sqrt, bias=eps6[:, 0:1], scale=1.0 / HALF).then_inc(sgr, 1)

        @block.vector
        def _(dve):
            for h in range(8):
                dve.wait_ge(sg, h // 2 * 2 + 2)
                u = ug[:, :, h * HD:(h + 1) * HD]
                nc.vector.scalar_tensor_tensor(u, PS[:, 4 + h // 2, (h % 2) * 256:(h % 2 + 1) * 256].rearrange("p (b d) -> p b d", d=HD), bsT[:, h:h + 1], u, ALU.add, ALU.mult).then_inc(so, 1)
            dve.wait_ge(sgr, 1)
            nc.vector.reciprocal(ssum[:, 0:TB], ssum[:, 0:TB])
            dve.drain()
            for b in range(TB):
                nc.vector.tensor_scalar(ug[:, b, :], ug[:, b, :], ssum[:, b:b + 1], None, ALU.mult)

    att = ExitStack()
    qs = sb(att, "q_stage1", [P, SEQ])
    ks = sb(att, "k_stage1", [P, SEQ + CTX])
    NK = SEQ + CTX
    spare = k_tok[:, :, :].rearrange("p b n -> p (b n)")
    prob = spare[:, 0:2 * NK].rearrange("p (s n) -> p s n", s=2)
    pT = spare[:, 2 * NK:4 * NK].rearrange("p (s j q) -> p s j q", s=2, q=P)
    mx = sb(att, "row_max1", [P, 2, 2])
    nmx = sb(att, "neg_max1", [P, 2])
    dn = sb(att, "row_sum1", [P, 2, 2])
    rdn = sb(att, "row_inv1", [P, 2])
    ona = q_tok
    a_st, a_sc, a_mx, a_pr, a_tr, a_pt, a_o, a_oo = [sem("na_" + n) for n in ("staged", "scores", "max", "probs", "ptr", "pt", "o", "out")]
    s_z, s_zd = sem("zeros_set"), sem("rows_cleared")
    MIN_BLOCKS = 2 * SEQ // P
    with nc.Block() as block:
        @block.gpsimd
        def _(pool):
            nc.gpsimd.memset(vs[:, 0:2, :], 0.0).then_inc(s_z, 1)

        @block.sync
        def _(sp):
            sp.wait_ge(s_z, 1)
            sp.dma_start(ys[MIN_BLOCKS * P:, :].rearrange("(j p) d -> p j d", p=P),
                         vs[:, 0:2, :].rearrange("p a n -> p (a n)").unsqueeze(1).to_broadcast([P, MAX_BLOCKS - MIN_BLOCKS, D])).then_inc(s_zd, 16)
            sp.wait_ge(s_zd, 16)

        @block.tensor
        def _(pe):
            with pe.Fori(0, 4) as c:
                pe.wait_ge(a_st, c + 1)

                def scores(w):
                    p, b, s = w // TB, w % TB, w % 2
                    hp = slice(p * HD, (p + 1) * HD)
                    if w >= 2:
                        pe.wait_ge(a_pr, c * 8 + w - 1)
                    nc.tensor.matmul(PS[:, 2 * s, :], qs[hp, b * P:(b + 1) * P], ks[hp, 0:SEQ], start=True, stop=True)
                    nc.tensor.matmul(PS[:, 2 * s + 1, 0:CTX], qs[hp, b * P:(b + 1) * P], ks[hp, SEQ:], start=True, stop=True).then_inc(a_sc, 1)
                scores(0)
                for w in range(8):
                    p, b, s = w // TB, w % TB, w % 2
                    if w < 7:
                        scores(w + 1)
                    pe.wait_ge(a_pr, c * 8 + w + 1)
                    pe.wait_ge(a_pt, c * 8 + w + 1)
                    for j in range(NK // P):
                        last = nc.tensor.transpose(PS[:, 4 + j // 4, (j % 4) * P:(j % 4 + 1) * P], prob[:, s, j * P:(j + 1) * P], ident[:, :])
                    last.then_inc(a_tr, 1)
                    pe.wait_ge(a_pt, c * 8 + w + 2)
                    pe.wait_ge(a_oo, c * 8 + w + 1)
                    for j in range(NK // P):
                        last = nc.tensor.matmul(PS[:, 6 + s, 0:HD], pT[:, s, j, :], v_tok[:, j, ds((2 * c + p) * HD, HD)], start=j == 0, stop=j == NK // P - 1)
                    last.then_inc(a_o, 1)

        @block.scalar
        def _(act):
            with act.Fori(0, 4) as c:
                for w in range(8):
                    s = w % 2
                    act.wait_ge(a_mx, c * 8 + w + 1)
                    nc.scalar.activation(prob[:, s, SEQ:], PS[:, 2 * s + 1, 0:CTX], ACT.Exp, bias=nmx[:, s:s + 1], accum_out=dn[:, s, 1:2])
                    nc.scalar.activation(prob[:, s, 0:SEQ], prob[:, s, 0:SEQ], ACT.Exp, bias=nmx[:, s:s + 1], accum_out=dn[:, s, 0:1])
                    act.drain().then_inc(a_pr, 1)
                    if w >= 1:
                        act.wait_ge(a_tr, c * 8 + w)
                        nc.scalar.activation(pT[:, 1 - s, :, :].rearrange("p j q -> p (j q)"), PS[:, 4:6, :].rearrange("p a n -> p (a n)")[:, 0:NK], ACT.Copy).then_inc(a_pt, 1)
                act.wait_ge(a_tr, c * 8 + 8)
                nc.scalar.activation(pT[:, 1, :, :].rearrange("p j q -> p (j q)"), PS[:, 4:6, :].rearrange("p a n -> p (a n)")[:, 0:NK], ACT.Copy).then_inc(a_pt, 1)

        @block.vector
        def _(dve):
            V = nc.vector
            V.sem_inc(a_pt, 1)
            V.sem_inc(a_oo, 2)
            with dve.Fori(0, 4) as c:
                V.tensor_copy(qs[:, :], qT[:, ds(c, 1), :].rearrange("p a n -> p (a n)"))
                V.tensor_copy(ks[:, :], kT[:, ds(c, 1), :].rearrange("p a n -> p (a n)"))
                dve.drain().then_inc(a_st, 1)

                def finish(w):
                    p, b, s = w // TB, w % TB, w % 2
                    dve.wait_ge(a_o, c * 8 + w + 1)
                    V.tensor_scalar(ona[:, b, ds((2 * c + p) * HD, HD)], PS[:, 6 + s, 0:HD], rdn[:, s:s + 1], None, ALU.mult).then_inc(a_oo, 1)
                for w in range(8):
                    p, b, s = w // TB, w % TB, w % 2
                    dve.wait_ge(a_sc, c * 8 + w + 1)
                    V.tensor_tensor(prob[:, s, 0:SEQ], PS[:, 2 * s, :], nbt[:, ds(2 * c + p, 1), (7 - 2 * b) * GRID:(15 - 2 * b) * GRID].rearrange("p a n -> p (a n)"), ALU.add)
                    V.tensor_reduce(mx[:, s, 1:2], PS[:, 2 * s + 1, 0:CTX], AX.X, ALU.max)
                    dve.drain()
                    V.tensor_reduce(mx[:, s, 0:1], prob[:, s, 0:SEQ], AX.X, ALU.max)
                    dve.drain()
                    V.tensor_scalar(nmx[:, s:s + 1], mx[:, s, 0:1], mx[:, s, 1:2], -1.0, ALU.max, ALU.mult).then_inc(a_mx, 1)
                    if w >= 1:
                        finish(w - 1)
                    dve.wait_ge(a_pr, c * 8 + w + 1)
                    V.tensor_tensor(dn[:, s, 0:1], dn[:, s, 0:1], dn[:, s, 1:2], ALU.add)
                    dve.drain()
                    V.reciprocal(rdn[:, s:s + 1], dn[:, s, 0:1])
                    dve.drain()
                finish(7)

    s_sq, s_sr, tr5, hi5, rd5 = [sem("mrg_" + n) for n in ("sq", "root", "tr", "hi", "ready")]
    s_n = sem("mrg_norm")
    with nc.Block() as block:
        @block.sync
        def _(sp):
            for n in range(8):
                half, kp = n // 4, n % 4
                load_tile(sp, Tile(N_WIN + n), A["w_out"][0, kp * 2 * P:(kp + 1) * 2 * P, half * HALF:(half + 1) * HALF].rearrange("(k p) n -> p k n", p=P))

        @block.scalar
        def _(act):
            for b in range(TB):
                nc.scalar.activation(vs[:, b, :], ona[:, b, :], ACT.Square, accum_out=ssum[:, b:b + 1])
            act.drain()
            nc.scalar.activation(ssum[:, 0:TB], ssum[:, 0:TB], ACT.Sqrt, bias=eps6[:, 0:1], scale=1.0 / HALF).then_inc(s_sr, 1)
            split_hi(Tile(N_WIN))
            split_hi(Tile(N_WIN + 1))
            for i in range(KC):
                kc = (i + 4) % KC
                act.wait_ge(tr5, i + 1)
                if i >= 2:
                    act.wait_ge(rd5, i - 1)
                nc.scalar.activation(tmp[:, i % 2, :], PS[:, kc, :], ACT.Copy, scale=out_gT[:, kc:kc + 1])
                nc.scalar.activation(xT_hi[:, kc, :], PS[:, kc, :], ACT.Copy, scale=out_gT[:, kc:kc + 1]).then_inc(hi5, 1)
            for n in range(2, 8):
                split_hi(Tile(N_WIN + n))

        @block.vector
        def _(dve):
            V = nc.vector
            dve.wait_ge(s_sr, 1)
            V.reciprocal(ssum[:, 0:TB], ssum[:, 0:TB])
            dve.drain()
            for b in range(TB):
                V.tensor_scalar(ona[:, b, :], ona[:, b, :], ssum[:, b:b + 1], None, ALU.mult)
            dve.drain().then_inc(s_n, 1)
            split_lo(Tile(N_WIN))
            split_lo(Tile(N_WIN + 1))
            for i in range(KC):
                kc = (i + 4) % KC
                dve.wait_ge(hi5, i + 1)
                V.tensor_tensor(xT_lo[:, kc, :], tmp[:, i % 2, :], xT_hi[:, kc, :].bitcast(f32), ALU.subtract).then_inc(rd5, 1)

            def residual(half):
                for b in range(TB):
                    x = xtok[:, b, half * HALF:(half + 1) * HALF]
                    V.tensor_tensor(tmp[:, b % 2, :], PS[:, 4 * half + b, :], ga_row[:, half * HALF:(half + 1) * HALF], ALU.mult)
                    dve.drain()
                    V.tensor_tensor(x, x, tmp[:, b % 2, :], ALU.add)
                    dve.drain()
            for n in range(2, 8):
                split_lo(Tile(N_WIN + n))
                if n == 5:
                    dve.wait_ge(w_used, N_WIN + 4)
                    residual(0)
            dve.wait_ge(w_used, N_WIN + 8)
            residual(1)

        @block.tensor
        def _(pe):
            for i in range(KC):
                kc = (i + 4) % KC
                src = ug if kc >= 4 else ona
                if i == 4:
                    pe.wait_ge(s_n, 1)
                for b in range(TB):
                    last = nc.tensor.transpose(PS[:, kc, b * P:(b + 1) * P], src[:, b, (kc % 4) * P:(kc % 4 + 1) * P], ident[:, :])
                last.then_inc(tr5, 1)
            pe.wait_ge(rd5, KC)
            for n in range(8):
                half, kp = n // 4, n % 4
                t = Tile(N_WIN + n)
                pe.wait_ge(w_lo, t.plus(1))
                for kk in range(2):
                    kc = 2 * kp + kk
                    for b in range(TB):
                        last = product(PS[:, 4 * half + b, :], XT, (slice(None), kc, slice(b * P, (b + 1) * P)), W, (slice(None), t.slot, slice(kk * HALF, (kk + 1) * HALF)), kc == 0, kc == KC - 1)
                last.then_inc(w_used, 1)
    att.close()
    proj.close()
    table.close()
    keep.close()
    if stop == "attn":
        ctx.close()
        return

    moe = ExitStack()
    xn_hi = xT_hi[:, :, :].rearrange("p k n -> p (k n)").rearrange("p (b d) -> p b d", d=D)
    xn_lo = xT_lo[:, :, :].rearrange("p k n -> p (k n)").rearrange("p (b d) -> p b d", d=D)
    slots = sb(moe, "slots", [P, 2, TB])
    slot_i = sb(moe, "slot_index", [P, 2, TB], mybir.dt.int32)
    gates = sb(moe, "gates", [P, 2, TB])
    iota = sb(moe, "iota_row", [P, P])
    plan = sb(moe, "plan", [P, 32], mybir.dt.int32)
    rt = ExitStack()
    xn2 = sb(rt, "xn2", [P, TB, D])
    hfT = sb(rt, "hfT", [P, KC, SEQ])
    rw = sb(rt, "router_w", [P, KC, 20])
    rb = sb(rt, "router_b", [P, 20])
    lower = sb(rt, "before", [P, P])
    ones = sb(rt, "ones_rt", [P, P])
    first4 = sb(rt, "first4", [P, 4])
    jrow = sb(rt, "block_numbers", [P, 24])
    lg = sb(rt, "logits", [P, TB, 20])
    r4 = sb(rt, "r4", [P, 8, TB, 4])
    r1 = sb(rt, "r1", [P, 12, TB])
    r16 = sb(rt, "r16", [P, 6, TB, 16])
    cnt = sb(rt, "counts", [P, 8, 16])
    bj = sb(rt, "by_block", [P, 24, 16])
    bjf = sb(rt, "by_block_sum", [P, 32])
    q_ld, q_ss, q_n, q_tr, q_ev, q_lg, q_e1, q_e2, q_m, q_rk, q_x, q_hi = [sem("rt_" + n) for n in ("loaded", "root", "norm", "tr", "evac", "logits", "exp1", "exp2", "mask", "rank", "in", "hi")]
    with nc.Block() as block:
        @block.sync
        def _(sp):
            for d, n in ((rw[:, :, :], "router_w"), (lower[:, :], "before"), (iota[:, :], "iota"), (first4[:, :], "first4"), (jrow[:, :], "jrow")):
                sp.dma_start(d, A[n]).then_inc(q_ld, 16)
            sp.dma_start(rb[:, 0:4], A["rg_b"][0].partition_broadcast(P)).then_inc(q_ld, 16)
            sp.dma_start(rb[:, 4:20], A["re_b"][0].rearrange("g e -> (g e)").partition_broadcast(P)).then_inc(q_ld, 16)

        @block.gpsimd
        def _(pool):
            nc.gpsimd.memset(ones[:, :], 1.0)
            nc.gpsimd.memset(r16[:, 5, 0, :], 1.0)
            pool.drain().then_inc(q_x, 1)

        @block.scalar
        def _(act):
            for b in range(TB):
                nc.scalar.activation(hfT[:, 2 * b:2 * b + 2, :].rearrange("p a n -> p (a n)"), xtok[:, b, :], ACT.Square, accum_out=ssum[:, b:b + 1])
            act.drain()
            nc.scalar.activation(ssum[:, 0:TB], ssum[:, 0:TB], ACT.Sqrt, bias=eps6[:, 0:1], scale=1.0 / D).then_inc(q_ss, 1)
            act.wait_ge(q_n, 1)
            nc.scalar.activation(xn_hi, xn2[:, :, :], ACT.Copy).then_inc(q_hi, 1)
            for kc in range(KC):
                act.wait_ge(q_tr, kc + 1)
                nc.scalar.activation(hfT[:, kc, :], PS[:, kc, :], ACT.Identity, bias=modT[:, 2, kc, 0:1], scale=modT[:, 3, kc, 0:1]).then_inc(q_ev, 1)
            act.wait_ge(q_e1, 1)
            nc.scalar.activation(r4[:, 1, :, :], r4[:, 0, :, :], ACT.Exp).then_inc(q_e2, 1)
            act.wait_ge(q_e1, 2)
            nc.scalar.activation(r1[:, 6, :], r1[:, 5, :], ACT.Exp).then_inc(q_e2, 1)

        @block.tensor
        def _(pe):
            pe.wait_ge(q_n, 1)
            for kc in range(KC):
                for b in range(TB):
                    last = nc.tensor.transpose(PS[:, kc, b * P:(b + 1) * P], xn2[:, b, kc * P:(kc + 1) * P], ident[:, :])
                last.then_inc(q_tr, 1)
            pe.wait_ge(q_ev, KC)
            pe.wait_ge(q_ld, 112)
            for b in range(TB):
                for kc in range(KC):
                    last = nc.tensor.matmul(PS[:, b, 0:20], hfT[:, kc, b * P:(b + 1) * P], rw[:, kc, :], start=kc == 0, stop=kc == KC - 1)
            last.then_inc(q_lg, 1)
            pe.wait_ge(q_m, 1)
            for b in range(TB):
                for a in range(b):
                    nc.tensor.matmul(PS[:, 4 + b, 0:16], ones[:, :], r16[:, 2, a, :], start=a == 0, stop=False)
                nc.tensor.matmul(PS[:, 4 + b, 0:16], lower[:, :], r16[:, 2, b, :], start=b == 0, stop=True)
            for b in range(TB):
                last = nc.tensor.matmul(PS[:, 0, 0:16], ones[:, :], r16[:, 2, b, :], start=b == 0, stop=b == TB - 1)
            last.then_inc(q_rk, 1)

        @block.vector
        def _(dve):
            V = nc.vector
            TT, TS = V.tensor_tensor, V.tensor_scalar
            dr = dve.drain
            dve.wait_ge(q_ss, 1)
            V.reciprocal(ssum[:, 0:TB], ssum[:, 0:TB])
            dr()
            for b in range(TB):
                TS(xn2[:, b, :], xtok[:, b, :], ssum[:, b:b + 1], None, ALU.mult)
            dr().then_inc(q_n, 1)
            dve.wait_ge(q_hi, 1)
            TT(xn_lo, xn2[:, :, :], xn_hi.bitcast(f32), ALU.subtract)
            dve.wait_ge(q_x, 1)
            dve.wait_ge(q_ld, 112)
            dve.wait_ge(q_lg, 1)
            TT(lg[:, :, :], PS[:, 0:TB, 0:20], rb[:, :].unsqueeze(1).to_broadcast([P, TB, 20]), ALU.add)
            dr()
            b4 = lambda a: a.unsqueeze(2).to_broadcast([P, TB, 4])

            def first_max(src, top, hot, t):
                V.tensor_reduce(top, src, AX.X, ALU.max)
                dr()
                TT(t, src, b4(top), ALU.is_equal)
                dr()
                TT(t, t, first4[:, :].unsqueeze(1).to_broadcast([P, TB, 4]), ALU.mult)
                dr()
                V.tensor_reduce(r1[:, 11, :], t, AX.X, ALU.max)
                dr()
                TT(hot, t, b4(r1[:, 11, :]), ALU.is_equal)
                dr()
            first_max(lg[:, :, 0:4], r1[:, 0, :], r4[:, 2, :, :], r4[:, 7, :, :])
            TT(r4[:, 0, :, :], lg[:, :, 0:4], b4(r1[:, 0, :]), ALU.subtract)
            dr().then_inc(q_e1, 1)
            for g in range(GROUPS):
                hot_g = r4[:, 2, :, g:g + 1].to_broadcast([P, TB, 4])
                TT(r4[:, 3 if g == 0 else 7, :, :], lg[:, :, 4 + 4 * g:8 + 4 * g], hot_g, ALU.mult)
                dr()
                if g:
                    TT(r4[:, 3, :, :], r4[:, 3, :, :], r4[:, 7, :, :], ALU.add)
                    dr()
            first_max(r4[:, 3, :, :], r1[:, 1, :], r4[:, 4, :, :], r4[:, 7, :, :])
            TS(r4[:, 5, :, :], r4[:, 4, :, :], NEG, None, ALU.mult)
            dr()
            TT(r4[:, 5, :, :], r4[:, 5, :, :], r4[:, 3, :, :], ALU.add)
            dr()
            first_max(r4[:, 5, :, :], r1[:, 2, :], r4[:, 6, :, :], r4[:, 7, :, :])
            TT(r1[:, 5, :], r1[:, 2, :], r1[:, 1, :], ALU.subtract)
            dr().then_inc(q_e1, 1)
            for k, hot_e in ((0, 4), (1, 6)):
                for g in range(GROUPS):
                    TT(r16[:, k, :, 4 * g:4 * g + 4], r4[:, hot_e, :, :], r4[:, 2, :, g:g + 1].to_broadcast([P, TB, 4]), ALU.mult)
            dr()
            TT(r16[:, 2, :, :], r16[:, 0, :, :], r16[:, 1, :, :], ALU.add)
            dr().then_inc(q_m, 1)
            dve.wait_ge(q_e2, 2)
            V.tensor_reduce(r1[:, 7, :], r4[:, 1, :, :], AX.X, ALU.add)
            TS(r1[:, 8, :], r1[:, 6, :], 1.0, None, ALU.add)
            dr()
            TT(r1[:, 8, :], r1[:, 8, :], r1[:, 7, :], ALU.mult)
            dr()
            V.reciprocal(gates[:, 0, :], r1[:, 8, :])
            dr()
            TT(gates[:, 1, :], gates[:, 0, :], r1[:, 6, :], ALU.mult)
            dve.wait_ge(q_rk, 1)
            V.tensor_copy(cnt[:, 0, :], PS[:, 0, 0:16])
            dr()
            for k in range(4):
                TS(cnt[:, 1 + k, :], cnt[:, 0, :], float(P * k), None, ALU.is_gt)
            dr()
            for k in range(1, 4):
                TT(cnt[:, 1, :], cnt[:, 1, :], cnt[:, 1 + k, :], ALU.add)
                dr()
            V.tensor_tensor_scan(cnt[:, 5, :], r16[:, 5, 0, :], cnt[:, 1, :], 0.0, ALU.mult, ALU.add)
            dr()
            TT(cnt[:, 6, :], cnt[:, 5, :], cnt[:, 1, :], ALU.subtract)
            dr()
            TS(cnt[:, 6, :], cnt[:, 6, :], float(P), None, ALU.mult)
            dr()
            TT(r16[:, 3, :, :], PS[:, 4:8, 0:16], cnt[:, 6, :].unsqueeze(1).to_broadcast([P, TB, 16]), ALU.add)
            dr()
            for k in range(2):
                TT(r16[:, 4, :, :], r16[:, 3, :, :], r16[:, k, :, :], ALU.mult)
                dr()
                V.tensor_reduce(slots[:, k, :], r16[:, 4, :, :], AX.X, ALU.add)
                dr()
            V.tensor_copy(slot_i[:, :, :], slots[:, :, :])
            TT(bj[:, :, :], cnt[:, 5, :].unsqueeze(1).to_broadcast([P, 24, 16]), jrow[:, :].unsqueeze(2).to_broadcast([P, 24, 16]), ALU.is_le)
            dr()
            V.tensor_reduce(bjf[:, 0:24], bj[:, :, :], AX.X, ALU.add)
            dr()
            TS(bjf[:, 0:24], bjf[:, 0:24], float(EXPERTS - 1), None, ALU.min)
            V.tensor_copy(bjf[:, 24:25], cnt[:, 5, 15:16])
            dr()
            V.tensor_copy(plan[:, 0:25], bjf[:, 0:25])
    rt.close()

    ex = ExitStack()
    w1b = sb(ex, "w1_buf", [P, KC, D_EXP])
    w3b = sb(ex, "w3_buf", [P, KC, D_EXP])
    w2b = sb(ex, "w2_buf", [P, D_EXP // P, D])
    pick = sb(ex, "pick", [P, TB, P], f32r)
    xs = sb(ex, "rows_T", [P, KC, P])
    sl = sb(ex, "silu_e", [P, D_EXP])
    hid = sb(ex, "hidden_e", [P, D_EXP])
    hT = sb(ex, "hidden_T", [P, D_EXP // P, P])
    yb = sb(ex, "y_buf", [P, D])
    KE = D_EXP // P
    e_w1, e_w3, e_w2, e_pk, e_gt, e_xs, e_u1, e_u3, e_sl, e_hd, e_tr, e_hT, e_dn, e_y, e_st, e_yf = [
        sem("ex_" + n) for n in ("w1", "w3", "w2", "pick", "gather", "rows", "up1", "up3", "silu", "hid", "tr", "hT", "down", "y", "store", "y_free")]
    with nc.Block() as block:
        @block.sync
        def _(sp):
            n_blocks = sp.value_load(plan[0:1, 24:25], min_val=8, max_val=MAX_BLOCKS)
            with sp.Fori(0, n_blocks) as j:
                e = sp.value_load(plan[0:1, ds(j, 1)], min_val=0, max_val=EXPERTS - 1)
                sp.wait_ge(e_u1, j + 1)
                sp.dma_start(w1b[:, :, :], A["w1"][0, ds(e, 1)].rearrange("a (k p) n -> p (a k) n", p=P)).then_inc(e_w1, 16)
                sp.wait_ge(e_u3, j + 1)
                sp.dma_start(w3b[:, :, :], A["w3"][0, ds(e, 1)].rearrange("a (k p) n -> p (a k) n", p=P)).then_inc(e_w3, 16)
                sp.wait_ge(e_dn, j + 1)
                sp.dma_start(w2b[:, :, :], A["w2"][0, ds(e, 1)].rearrange("a (k p) n -> p (a k) n", p=P)).then_inc(e_w2, 16)

        @block.gpsimd
        def _(pool):
            n_blocks = pool.value_load(plan[0:1, 24:25], min_val=8, max_val=MAX_BLOCKS)
            with pool.Fori(0, n_blocks) as j:
                pool.wait_ge(e_y, j + 2)
                pool.dma_start(ys[ds(j * P, P), :], yb[:, :]).then_inc(e_st, 16)
                pool.wait_ge(e_st, 16 * (j + 1))
                pool.sem_inc(e_yf, 1)

        @block.tensor
        def _(pe):
            pe.sem_inc(e_u1, 1)
            pe.sem_inc(e_u3, 1)
            pe.sem_inc(e_dn, 1)
            n_blocks = pe.value_load(plan[0:1, 24:25], min_val=8, max_val=MAX_BLOCKS)

            def gather():
                for kc in range(KC):
                    for b in range(TB):
                        at = (slice(None), b, slice(kc * P, (kc + 1) * P))
                        for part, x in enumerate((xn_hi, xn_lo)):
                            last = nc.tensor.matmul(PS[:, kc // 4, (kc % 4) * P:(kc % 4 + 1) * P], x[at], pick[:, b, :], start=b == 0 and part == 0, stop=b == TB - 1 and part == 1, skip_group_check=True)
                last.then_inc(e_gt, 1)
            pe.wait_ge(e_pk, 1)
            gather()
            with pe.Fori(0, n_blocks) as j:
                pe.wait_ge(e_xs, j + 1)
                pe.wait_ge(e_w1, 16 * (j + 1))
                pe.wait_ge(e_hd, j + 1)
                for kc in range(KC):
                    last = nc.tensor.matmul(PS[:, 2, :], xs[:, kc, :], w1b[:, kc, :], start=kc == 0, stop=kc == KC - 1)
                last.then_inc(e_u1, 1)
                pe.wait_ge(e_w3, 16 * (j + 1))
                for kc in range(KC):
                    last = nc.tensor.matmul(PS[:, 3, :], xs[:, kc, :], w3b[:, kc, :], start=kc == 0, stop=kc == KC - 1)
                last.then_inc(e_u3, 1)
                pe.wait_ge(e_pk, j + 2)
                gather()
                pe.wait_ge(e_hd, j + 2)
                for k in range(KE):
                    last = nc.tensor.transpose(PS[:, 4, k * P:(k + 1) * P], hid[:, k * P:(k + 1) * P], ident[:, :])
                last.then_inc(e_tr, 1)
                pe.wait_ge(e_hT, j + 1)
                pe.wait_ge(e_w2, 16 * (j + 1))
                pe.wait_ge(e_y, j + 1)
                for h in range(2):
                    for k in range(KE):
                        last = nc.tensor.matmul(PS[:, 5 + h, :], hT[:, k, :], w2b[:, k, h * HALF:(h + 1) * HALF], start=k == 0, stop=k == KE - 1)
                last.then_inc(e_dn, 1)

        @block.scalar
        def _(act):
            act.sem_inc(e_yf, 1)
            n_blocks = act.value_load(plan[0:1, 24:25], min_val=8, max_val=MAX_BLOCKS)
            with act.Fori(0, n_blocks) as j:
                act.wait_ge(e_u1, j + 2)
                nc.scalar.activation(sl[:, :], PS[:, 2, :], ACT.Silu).then_inc(e_sl, 1)
                act.wait_ge(e_tr, j + 1)
                nc.scalar.activation(hT[:, :, :].rearrange("p k n -> p (k n)"), PS[:, 4, :], ACT.Copy).then_inc(e_hT, 1)
                act.wait_ge(e_dn, j + 2)
                act.wait_ge(e_yf, j + 1)
                nc.scalar.activation(yb[:, :], PS[:, 5:7, :].rearrange("p a n -> p (a n)"), ACT.Copy).then_inc(e_y, 1)

        @block.vector
        def _(dve):
            V = nc.vector
            V.sem_inc(e_hd, 1)
            V.sem_inc(e_y, 1)
            n_blocks = dve.value_load(plan[0:1, 24:25], min_val=8, max_val=MAX_BLOCKS)

            def picks():
                for b in range(TB):
                    V.tensor_scalar(pick[:, b, :], iota[:, :], slots[:, 0, b:b + 1], None, ALU.is_equal)
                dve.drain()
                for b in range(TB):
                    V.scalar_tensor_tensor(pick[:, b, :], iota[:, :], slots[:, 1, b:b + 1], pick[:, b, :].bitcast(f32), ALU.is_equal, ALU.add)
                dve.drain()
                V.tensor_scalar(slots[:, :, :], slots[:, :, :], float(-P), None, ALU.add)
                dve.drain().then_inc(e_pk, 1)

            def rows():
                g = PS[:, 0:2, :].rearrange("p a (k s) -> p (a k) s", s=P)
                V.tensor_tensor(xs[:, :, :], g, modT[:, 3, :, 0:1].to_broadcast([P, KC, P]), ALU.mult)
                dve.drain()
                V.tensor_tensor(xs[:, :, :], xs[:, :, :], modT[:, 2, :, 0:1].to_broadcast([P, KC, P]), ALU.add).then_inc(e_xs, 1)
            picks()
            dve.wait_ge(e_gt, 1)
            rows()
            with dve.Fori(0, n_blocks) as j:
                picks()
                dve.wait_ge(e_sl, j + 1)
                dve.wait_ge(e_u3, j + 2)
                V.tensor_tensor(hid[:, :], sl[:, :], PS[:, 3, :], ALU.mult).then_inc(e_hd, 1)
                dve.wait_ge(e_gt, j + 2)
                rows()
    ex.close()

    fn = ExitStack()
    yA = sb(fn, "y_first", [P, TB, D])
    yB = sb(fn, "y_second", [P, TB, D])
    s_ga = [sem(f"y_rows{b}") for b in range(TB)]
    with nc.Block() as block:
        @block.gpsimd
        def _(pool):
            for b in range(TB):
                for k, d in ((0, yA), (1, yB)):
                    nc.gpsimd.indirect_dma_start(out=d[:, b, :], out_offset=None, in_=ys[:, :], in_offset=bass.IndirectOffsetOnAxis(ap=slot_i[:, k, b:b + 1], axis=0)).then_inc(s_ga[b], 16)

        @block.vector
        def _(dve):
            V = nc.vector
            for b in range(TB):
                dve.wait_ge(s_ga[b], 32)
                V.tensor_scalar(yA[:, b, :], yA[:, b, :], gates[:, 0, b:b + 1], None, ALU.mult)
                dve.drain()
                V.scalar_tensor_tensor(yA[:, b, :], yB[:, b, :], gates[:, 1, b:b + 1], yA[:, b, :], ALU.mult, ALU.add)
                dve.drain()
                V.tensor_tensor(yA[:, b, :], yA[:, b, :], gf_row[:, :], ALU.mult)
                dve.drain()
                V.tensor_tensor(xtok[:, b, :], xtok[:, b, :], yA[:, b, :], ALU.add)
    fn.close()
    moe.close()
    ctx.close()


def second_block(nc, ctx, T0, S, A):
    xtok, xT_hi, xT_lo, raw, whi, wlo, ident, PS = S.xtok, S.xT_hi, S.xT_lo, S.raw, S.whi, S.wlo, S.ident, S.PS
    w_loaded, w_hi, w_lo, w_used = S.w_loaded, S.w_hi, S.w_lo, S.w_used

    def sem(n):
        return ctx.enter_context(nc.semaphore(n))

    def sb(c, n, shape, dt=f32):
        return c.enter_context(nc.sbuf_tensor(n, shape, dt))

    def load_tile(sp, t, src):
        sp.wait_ge(w_lo, t.plus(-1))
        sp.dma_start(raw[:, t.slot, :].rearrange("p (a n) -> p a n", n=src.shape[-1]), src).then_inc(w_loaded[t.slot], 16)

    def split_hi(t):
        nc.scalar.wait_ge(w_loaded[t.slot], t.loads())
        nc.scalar.wait_ge(w_used, t.plus(-1))
        nc.scalar.activation(whi[:, t.slot, :], raw[:, t.slot, :], ACT.Copy).then_inc(w_hi, 1)

    def split_lo(t):
        nc.vector.wait_ge(w_hi, t.plus(1))
        nc.vector.tensor_tensor(wlo[:, t.slot, :], raw[:, t.slot, :], whi[:, t.slot, :].bitcast(f32), ALU.subtract).then_inc(w_lo, 1)

    def product(out, a, a_at, b, b_at, first, last):
        nc.tensor.matmul(out, a[0][a_at], b[0][b_at], start=first, stop=False)
        nc.tensor.matmul(out, a[0][a_at], b[1][b_at], start=False, stop=False)
        return nc.tensor.matmul(out, a[1][a_at], b[0][b_at], start=False, stop=last)

    W = (whi, wlo)
    XT = (xT_hi, xT_lo)

    lnT = sb(ctx, "lnT", [P, 3, 2, KC])
    g_row = sb(ctx, "ln_g_row", [P, D])
    b_row = sb(ctx, "ln_b_row", [P, D])
    stats = sb(ctx, "ln_stats", [P, TB, 2, 6])
    meanvar = sb(ctx, "ln_meanvar", [P, TB, 2])
    rstd = sb(ctx, "ln_rstd", [P, TB])
    eps = sb(ctx, "ln_eps", [P, 1])
    tmp = sb(ctx, "evac_tmp", [P, 2, SEQ])

    def layer_norm_dve(dve, after_max, var_ready, rstd_ready, n):
        for b in range(TB):
            for h in range(2):
                nc.vector.bn_stats(stats[:, b, h, :], xtok[:, b, h * HALF:(h + 1) * HALF])
        dve.drain()
        for b in range(TB):
            last = nc.vector.bn_aggr(meanvar[:, b, :], stats[:, b, :, :])
        last.then_inc(var_ready, 1)
        dve.wait_ge(rstd_ready, n)
        nc.vector.reciprocal(rstd[:, :], rstd[:, :])
        dve.drain()
        for b in range(TB):
            nc.vector.tensor_scalar(xtok[:, b, :], xtok[:, b, :], meanvar[:, b, 0:1], rstd[:, b:b + 1], ALU.subtract, ALU.mult)

    def layer_norm_act(act, var_ready, rstd_ready, n):
        act.wait_ge(var_ready, n)
        nc.scalar.activation(rstd[:, :], meanvar[:, :, 1], ACT.Sqrt, bias=eps[:, 0:1]).then_inc(rstd_ready, 1)

    def transposes(tr_done):
        for kc in range(KC):
            for b in range(TB):
                last = nc.tensor.transpose(PS[:, kc, b * P:(b + 1) * P], xtok[:, b, kc * P:(kc + 1) * P], ident[:, :])
            last.then_inc(tr_done, 1)

    F = [{n: sem(f"ffn{j}_{n}") for n in (
        "tr_done", "hi_ready", "xT_ready", "silu_done", "sum_done", "h_hi_ready", "h_ready", "var_ready", "rstd_ready")} for j in range(2)]
    ln_loaded = sem("ln_loaded")
    rows_loaded = sem("rows_loaded")
    residual_ready = sem("residual_ready")

    with nc.Block() as block:
        @block.gpsimd
        def _(pool):
            nc.gpsimd.memset(eps[:, :], LN_EPS)

    def ffn(j, l, T, post, pre):
        f = F[j]
        wg, wu, wd = A["ffn_w_gate_2"], A["ffn_w_up_2"], A["ffn_w_down_2"]
        with ExitStack() as c:
            h_hi = sb(c, f"h_hi{j}", [P, FC, SEQ], f32r)
            h_lo = sb(c, f"h_lo{j}", [P, FC, SEQ], f32r)
            silu = sb(c, f"silu{j}", [P, 2, SEQ])
            hsum = sb(c, f"hsum{j}", [P, 2, SEQ])
            H = (h_hi, h_lo)

            def up_src(w, i):
                return w[l, j, :, ds(i * P, P)].rearrange("(k p) n -> p k n", p=P)

            with nc.Block() as block:
                @block.sync
                def _(sp):
                    if j == 0:
                        sp.dma_start(lnT[:, :, :, :], A["lnT_2"][l]).then_inc(ln_loaded, 16)
                    else:
                        sp.dma_start(g_row[:, :], A["ln_g_2"][l, 1, :].partition_broadcast(P)).then_inc(rows_loaded, 16)
                        sp.dma_start(b_row[:, :], A["ln_b_2"][l, 1, :].partition_broadcast(P)).then_inc(rows_loaded, 16)
                    with sp.Fori(0, FC) as i:
                        load_tile(sp, T(0, i), up_src(wg, i))
                        load_tile(sp, T(1, i), up_src(wu, i))
                    for n in range(N_DOWN):
                        half, kp = n // (FC // 2), n % (FC // 2)
                        load_tile(sp, T(N_UP + n), wd[l, j, kp * 2 * P:(kp + 1) * 2 * P, half * HALF:(half + 1) * HALF].rearrange("(k p) n -> p k n", p=P))

                @block.scalar
                def _(act):
                    split_hi(T(0))
                    split_hi(T(1))
                    if j == 1:
                        act.wait_ge(ln_loaded, 16 * (l + 1))
                    for kc in range(KC):
                        act.wait_ge(f["tr_done"], l * KC + kc + 1)
                        if j == 0:
                            nc.scalar.activation(xT_hi[:, kc, :], PS[:, kc, :], ACT.Copy).then_inc(f["hi_ready"], 1)
                        else:
                            g, b = lnT[:, 1, 0, kc:kc + 1], lnT[:, 1, 1, kc:kc + 1]
                            if kc >= 2:
                                act.wait_ge(f["xT_ready"], l * KC + kc - 1)
                            nc.scalar.activation(tmp[:, kc % 2, :], PS[:, kc, :], ACT.Identity, bias=b, scale=g)
                            nc.scalar.activation(xT_hi[:, kc, :], PS[:, kc, :], ACT.Identity, bias=b, scale=g).then_inc(f["hi_ready"], 1)
                    with act.Fori(0, FC // 2) as ii:
                        for c2 in range(2):
                            i = 2 * ii + c2
                            split_hi(T(2, i))
                            split_hi(T(3, i))
                            act.wait_ge(w_used, T(0, i).plus(1))
                            act.wait_ge(f["sum_done"], l * (FC + 2) + i + 1)
                            nc.scalar.activation(silu[:, c2, :], PS[:, 2 * c2, :], ACT.Silu).then_inc(f["silu_done"], 1)
                            act.wait_ge(f["sum_done"], l * (FC + 2) + i + 3)
                            nc.scalar.activation(h_hi[:, ds(i, 1), :], hsum[:, c2:c2 + 1, :], ACT.Copy).then_inc(f["h_hi_ready"], 1)
                    for n in range(2, N_DOWN):
                        split_hi(T(N_UP + n))
                    layer_norm_act(act, f["var_ready"], f["rstd_ready"], l + 1)

                @block.vector
                def _(dve):
                    nc.vector.sem_inc(f["sum_done"], 2)
                    split_lo(T(0))
                    split_lo(T(1))
                    for kc in range(KC):
                        dve.wait_ge(f["hi_ready"], l * KC + kc + 1)
                        src = PS[:, kc, :] if j == 0 else tmp[:, kc % 2, :]
                        nc.vector.tensor_tensor(xT_lo[:, kc, :], src, xT_hi[:, kc, :].bitcast(f32), ALU.subtract).then_inc(f["xT_ready"], 1)
                    with dve.Fori(0, FC // 2) as ii:
                        for c2 in range(2):
                            i = 2 * ii + c2
                            split_lo(T(2, i))
                            split_lo(T(3, i))
                            dve.wait_ge(f["silu_done"], l * FC + i + 1)
                            dve.wait_ge(w_used, T(1, i).plus(1))
                            nc.vector.scalar_tensor_tensor(hsum[:, c2, :], silu[:, c2, :], 0.5, PS[:, 2 * c2 + 1, :], ALU.mult, ALU.mult).then_inc(f["sum_done"], 1)
                            dve.wait_ge(f["h_hi_ready"], l * FC + i + 1)
                            nc.vector.tensor_tensor(h_lo[:, ds(i, 1), :], hsum[:, c2:c2 + 1, :], h_hi[:, ds(i, 1), :].bitcast(f32), ALU.subtract).then_inc(f["h_ready"], 1)
                    for n in range(2, FC // 2 + 3):
                        split_lo(T(N_UP + n))
                    dve.wait_ge(w_used, T(N_UP + FC // 2 - 1).plus(1))
                    if post is not None:
                        post(dve)
                    for b in range(TB):
                        nc.vector.scalar_tensor_tensor(xtok[:, b, 0:HALF], xtok[:, b, 0:HALF], ALPHA, PS[:, 4 + b, :], ALU.mult, ALU.add)
                    for n in range(FC // 2 + 3, N_DOWN):
                        split_lo(T(N_UP + n))
                    dve.wait_ge(w_used, T(N_FFN - 1).plus(1))
                    for b in range(TB):
                        nc.vector.scalar_tensor_tensor(xtok[:, b, HALF:D], xtok[:, b, HALF:D], ALPHA, PS[:, b, :], ALU.mult, ALU.add)
                    dve.drain()
                    layer_norm_dve(dve, None, f["var_ready"], f["rstd_ready"], l + 1)

                @block.gpsimd
                def _(pool):
                    if pre is not None:
                        pre(pool)

                @block.tensor
                def _(pe):
                    transposes(f["tr_done"])
                    with pe.Fori(0, FC // 2) as ii:
                        for c2 in range(2):
                            i = 2 * ii + c2
                            for g in range(2):
                                t = T(g, i)
                                pe.wait_ge(w_lo, t.plus(1))
                                pe.wait_ge(f["sum_done"], l * (FC + 2) + i + 1)
                                for kc in range(KC):
                                    if c2 == 0 and g == 0:
                                        pe.wait_ge(f["xT_ready"], l * KC + kc + 1)
                                    last = product(PS[:, 2 * c2 + g, :], W, (slice(None), t.slot, slice(kc * P, (kc + 1) * P)), XT, (slice(None), kc), kc == 0, kc == KC - 1)
                                last.then_inc(w_used, 1)
                    pe.wait_ge(f["sum_done"], l * (FC + 2) + FC + 2)
                    for n in range(N_DOWN):
                        half, kp = n // (FC // 2), n % (FC // 2)
                        t = T(N_UP + n)
                        pe.wait_ge(w_lo, t.plus(1))
                        for kk in range(2):
                            kc = 2 * kp + kk
                            if half == 0:
                                pe.wait_ge(f["h_ready"], l * FC + kc + 1)
                            for b in range(TB):
                                last = product(PS[:, (4 if half == 0 else 0) + b, :], H, (slice(None), kc, slice(b * P, (b + 1) * P)), W,
                                               (slice(None), t.slot, slice(kk * HALF, (kk + 1) * HALF)), kc == 0, kc == FC - 1)
                        last.then_inc(w_used, 1)

    M = {n: sem(f"mix_{n}") for n in (
        "tr_done", "hi_ready", "xT_ready", "pads_set", "small_loaded", "gates_loaded", "lru_conv_done", "gates_done", "gates_out", "scan_out",
        "mean_done", "sq_done", "var_done", "std_out", "norm_out", "silu_out", "evac", "y_hi", "y_ready", "q_staged", "scores_done", "max_out",
        "probs_out", "ptr_done", "pt_out", "o_done", "o_out", "otr_done", "var_ready", "rstd_ready", "chain_a", "chain_b")}
    bias_tab = sb(ctx, "rel_bias_table", [P, QH, BAND])
    sinks = sb(ctx, "sinks", [P, QH])
    ones_ch = sb(ctx, "ones_channels", [P, P])

    OFF = 3 * P
    dist_rows = nc.dram_tensor("dist_rows", [QH, P, OFF], f32, kind="Internal").ap()
    setup = {n: sem(f"setup_{n}") for n in ("in", "mm", "out", "rows", "tab")}
    with ExitStack() as c:
        bucket_hot = sb(c, "bucket_hot", [32, OFF])
        relb = sb(c, "relb", [32, QH])
        by_dist = sb(c, "by_dist", [QH, OFF])
        maskc = sb(c, "band_mask", [P, BAND])
        with nc.Block() as block:
            @block.sync
            def _(sp):
                sp.dma_start(bucket_hot[:, :], A["bucket_hot"]).then_inc(setup["in"], 16)
                sp.dma_start(relb[:, :], A["rel_bias_2"]).then_inc(setup["in"], 16)
                sp.dma_start(maskc[:, :], A["band_mask"]).then_inc(setup["tab"], 16)
                sp.wait_ge(setup["out"], 1)
                for h in range(QH):
                    sp.dma_start(dist_rows[h:h + 1, :, :], by_dist[h:h + 1, :].unsqueeze(1).to_broadcast([1, P, OFF])).then_inc(setup["rows"], 16)
                sp.wait_ge(setup["rows"], 16 * QH)
                skew = bass.AP(dist_rows.tensor, P - 1, [[OFF - 1, P], [P * OFF, QH], [1, BAND]])
                sp.dma_start(bias_tab[:, :, :], skew).then_inc(setup["tab"], 16)

            @block.gpsimd
            def _(pool):
                nc.gpsimd.memset(ones_ch[:, :], 1.0 / 256.0)

            @block.tensor
            def _(pe):
                pe.wait_ge(setup["in"], 32)
                nc.tensor.matmul(PS[0:QH, 0, 0:OFF], relb[:, :], bucket_hot[:, :], start=True, stop=True).then_inc(setup["mm"], 1)

            @block.vector
            def _(dve):
                dve.wait_ge(setup["mm"], 1)
                nc.vector.tensor_copy(by_dist[:, :], PS[0:QH, 0, 0:OFF]).then_inc(setup["out"], 1)
                dve.wait_ge(setup["tab"], 32)
                nc.vector.tensor_tensor(bias_tab[:, :, :], bias_tab[:, :, :], maskc[:, :].unsqueeze(1).to_broadcast([P, QH, BAND]), ALU.add)

    def mixer(l, T):
        m = M
        w_in, w_out = A["w_in_2"], A["w_out_2"]
        N_COLS = 13
        with ExitStack() as c:
            small = sb(c, "mix_small", [P, 2, 48])
            sink_l = sb(c, "sink_l", [P, QH])
            gate_a = sb(c, "lru_wa", [P, 2, P])
            gate_x = sb(c, "lru_wx", [P, 2, P])
            glu = sb(c, "glu_padded", [P, 2, CONV_K - 1 + SEQ])
            sig = sb(c, "conv_gate", [P, 2, SEQ])
            conv = sb(c, "conv_sum", [P, 2, SEQ])
            sq = sb(c, "conv_square", [P, 2, SEQ])
            xb = sb(c, "lru_padded", [P, 2, LRU_K - 1 + SEQ])
            gb = sb(c, "lru_gate", [P, 2, SEQ])
            xc = sb(c, "lru_conv", [P, 2, SEQ])
            r_g = sb(c, "gate_r", [P, 2, SEQ])
            i_g = sb(c, "gate_i", [P, 2, SEQ])
            th = sb(c, "tanh_t", [P, 2, SEQ])
            lamc = sb(c, "lam_consts", [P, 2, 8])
            qT = sb(c, "qT", [P, 4, SEQ])
            kT = sb(c, "kT_padded", [P, P + SEQ])
            vt = sb(c, "v_padded", [P, TB + 1, P])
            qs = sb(c, "q_stage", [P, SEQ])
            prob = sb(c, "probs", [P, 2, TB, BAND])
            pT = sb(c, "probs_T", [P, 2, TB, P])
            smax = sb(c, "row_max", [P, TB])
            nmax = sb(c, "neg_max", [P, TB])
            dsum = sb(c, "row_sum", [P, TB])
            esink = sb(c, "exp_sink", [P, TB])
            o_tok = sb(c, "attn_out", [P, TB, 8 * HD])
            TAPS, CB, CG, CNB, LT, LB, BA, BX, LAM = 0, 31, 32, 33, 34, 38, 39, 40, 41
            with nc.Block() as block:
                @block.sync
                def _(sp):
                    sp.dma_start(small[:, :, 0:42], A["mix_small_2"][l]).then_inc(m["small_loaded"], 16)
                    sp.dma_start(sink_l[:, :], A["attn_sinks_2"][l, :].partition_broadcast(P)).then_inc(m["small_loaded"], 16)
                    sp.wait_ge(m["pads_set"], l + 1)
                    for ch in range(2):
                        for hh in range(2):
                            for dst, src in ((gate_a, "lru_wa_2"), (gate_x, "lru_wx_2")):
                                sp.dma_start(dst[hh * HD:(hh + 1) * HD, ch, hh * HD:(hh + 1) * HD], A[src][l, 2 * ch + hh]).then_inc(m["gates_loaded"], 16)
                    sp.dma_start(g_row[:, :], A["ln_g_2"][l, 0, :].partition_broadcast(P)).then_inc(rows_loaded, 16)
                    sp.dma_start(b_row[:, :], A["ln_b_2"][l, 0, :].partition_broadcast(P)).then_inc(rows_loaded, 16)
                    for n in range(N_MIN):
                        load_tile(sp, T(n), w_in[l, :, n * P:(n + 1) * P].rearrange("(k p) n -> p k n", p=P))

                @block.gpsimd
                def _(pool):
                    nc.gpsimd.memset(gate_a[:, :, :], 0.0)
                    nc.gpsimd.memset(gate_x[:, :, :], 0.0)
                    nc.gpsimd.memset(glu[:, :, 0:CONV_K - 1], 0.0)
                    nc.gpsimd.memset(xb[:, :, 0:LRU_K - 1], 0.0)
                    nc.gpsimd.memset(kT[:, 0:P], 0.0)
                    nc.gpsimd.memset(vt[:, 0, :], 0.0)
                    pool.drain().then_inc(m["pads_set"], 1)
                    residual_affine(pool, 2 * l + 1, m["tr_done"], KC * (l + 1))

                @block.tensor
                def _(pe):
                    transposes(m["tr_done"])
                    for n in range(N_COLS):
                        t = T(n)
                        pe.wait_ge(w_lo, t.plus(1))
                        if n >= 4:
                            pe.wait_ge(m["evac"], l * N_MIN + n - 3)
                        for kc in range(KC):
                            if n == 0:
                                pe.wait_ge(m["xT_ready"], l * KC + kc + 1)
                            last = product(PS[:, n % 4, :], W, (slice(None), t.slot, slice(kc * P, (kc + 1) * P)), XT, (slice(None), kc), kc == 0, kc == KC - 1)
                        last.then_inc(w_used, 1)
                    t = T(N_COLS)
                    pe.wait_ge(w_lo, t.plus(1))
                    for b in range(TB):
                        for kc in range(KC):
                            last = product(PS[:, 4 + b, 0:P], XT, (slice(None), kc, slice(b * P, (b + 1) * P)), W, (slice(None), t.slot, slice(kc * P, (kc + 1) * P)), kc == 0, kc == KC - 1)
                    last.then_inc(w_used, 1)

                @block.scalar
                def _(act):
                    split_hi(T(0))
                    split_hi(T(1))
                    act.wait_ge(ln_loaded, 16 * (l + 1))
                    for kc in range(KC):
                        act.wait_ge(m["tr_done"], l * KC + kc + 1)
                        g, b = lnT[:, 0, 0, kc:kc + 1], lnT[:, 0, 1, kc:kc + 1]
                        if kc >= 2:
                            act.wait_ge(m["xT_ready"], l * KC + kc - 1)
                        nc.scalar.activation(tmp[:, kc % 2, :], PS[:, kc, :], ACT.Identity, bias=b, scale=g)
                        nc.scalar.activation(xT_hi[:, kc, :], PS[:, kc, :], ACT.Identity, bias=b, scale=g).then_inc(m["hi_ready"], 1)
                    act.wait_ge(m["pads_set"], l + 1)
                    for n in range(N_COLS):
                        if n + 2 < N_MIN:
                            split_hi(T(n + 2))
                        act.wait_ge(w_used, T(n).plus(1))
                        ps = PS[:, n % 4, :]
                        if n < 2:
                            op = nc.scalar.activation(glu[:, n, CONV_K - 1:], ps, ACT.Copy)
                        elif n < 4:
                            op = nc.scalar.activation(sig[:, n - 2, :], ps, ACT.Sigmoid)
                        elif n < 6:
                            op = nc.scalar.activation(xb[:, n - 4, LRU_K - 1:], ps, ACT.Copy)
                        elif n < 8:
                            op = nc.scalar.activation(gb[:, n - 6, :], ps, ACT.Gelu_apprx_tanh)
                        elif n < 12:
                            op = nc.scalar.activation(qT[:, n - 8, :], ps, ACT.Copy, scale=HD ** -0.5)
                        else:
                            op = nc.scalar.activation(kT[:, P:], ps, ACT.Copy)
                        op.then_inc(m["evac"], 1)
                    act.wait_ge(w_used, T(N_COLS).plus(1))
                    nc.scalar.activation(vt[:, 1:, :], PS[:, 4:8, 0:P], ACT.Copy).then_inc(m["evac"], 1)

                @block.vector
                def _(dve):
                    split_lo(T(0))
                    split_lo(T(1))
                    for kc in range(KC):
                        dve.wait_ge(m["hi_ready"], l * KC + kc + 1)
                        nc.vector.tensor_tensor(xT_lo[:, kc, :], tmp[:, kc % 2, :], xT_hi[:, kc, :].bitcast(f32), ALU.subtract).then_inc(m["xT_ready"], 1)
                    for n in range(4):
                        split_lo(T(n + 2))
                    dve.wait_ge(m["small_loaded"], 32 * (l + 1))
                    dve.wait_ge(m["evac"], l * N_MIN + 4)
                    nc.vector.tensor_tensor(glu[:, :, CONV_K - 1:], glu[:, :, CONV_K - 1:], sig[:, :, :], ALU.mult)
                    dve.drain()
                    for k in range(CONV_K):
                        if k % 3 == 2 and 4 + k // 3 + 2 < N_MIN:
                            split_lo(T(4 + k // 3 + 2))
                        for ch in range(2):
                            if k == 0:
                                nc.vector.tensor_scalar(conv[:, ch, :], glu[:, ch, 0:SEQ], small[:, ch, TAPS:TAPS + 1], small[:, ch, CB:CB + 1], ALU.mult, ALU.add)
                            else:
                                nc.vector.scalar_tensor_tensor(conv[:, ch, :], glu[:, ch, k:k + SEQ], small[:, ch, TAPS + k:TAPS + k + 1], conv[:, ch, :], ALU.mult, ALU.add)
                        dve.drain()

            with nc.Block() as block:
                @block.tensor
                def _(pe):
                    for ch in range(2):
                        nc.tensor.matmul(PS[:, 7, :], ones_ch[:, :], conv[:, ch, :], start=ch == 0, stop=ch == 1)
                    pe.drain().then_inc(m["mean_done"], 1)
                    pe.wait_ge(m["sq_done"], l + 1)
                    for ch in range(2):
                        nc.tensor.matmul(PS[:, 6, :], ones_ch[:, :], sq[:, ch, :], start=ch == 0, stop=ch == 1)
                    pe.drain().then_inc(m["var_done"], 1)
                    pe.wait_ge(m["gates_loaded"], 128 * (l + 1))
                    pe.wait_ge(m["lru_conv_done"], l + 1)
                    for ch in range(2):
                        for q, gw in enumerate((gate_a, gate_x)):
                            last = nc.tensor.matmul(PS[:, 2 * ch + q, :], gw[:, ch, :], xc[:, ch, :], start=True, stop=True)
                    last.then_inc(m["gates_done"], 1)

                @block.scalar
                def _(act):
                    act.wait_ge(m["chain_a"], 4 * l + 1)
                    nc.scalar.activation(lamc[:, :, 1], lamc[:, :, 0], ACT.Exp).then_inc(m["chain_b"], 1)
                    act.wait_ge(m["chain_a"], 4 * l + 2)
                    nc.scalar.activation(lamc[:, :, 3], lamc[:, :, 2], ACT.Ln).then_inc(m["chain_b"], 1)
                    act.wait_ge(m["gates_done"], l + 1)
                    for ch in range(2):
                        nc.scalar.activation(r_g[:, ch, :], PS[:, 2 * ch, :], ACT.Sigmoid, bias=small[:, ch, BA:BA + 1])
                        nc.scalar.activation(i_g[:, ch, :], PS[:, 2 * ch + 1, :], ACT.Sigmoid, bias=small[:, ch, BX:BX + 1])
                    act.drain().then_inc(m["gates_out"], 1)
                    act.wait_ge(m["chain_a"], 4 * l + 3)
                    for ch in range(2):
                        nc.scalar.activation(th[:, ch, :], r_g[:, ch, :], ACT.Tanh, scale=lamc[:, ch, 7:8])
                        nc.scalar.activation(sig[:, ch, :], r_g[:, ch, :], ACT.Exp, scale=lamc[:, ch, 6:7])
                    act.drain().then_inc(m["chain_b"], 1)
                    act.wait_ge(m["chain_a"], 4 * l + 4)
                    nc.scalar.activation(th[:, :, :], th[:, :, :], ACT.Sqrt).then_inc(m["chain_b"], 1)
                    act.wait_ge(m["var_done"], l + 1)
                    nc.scalar.activation(xb[:, 0, 0:SEQ], PS[:, 6, :], ACT.Sqrt, bias=eps[:, 0:1]).then_inc(m["std_out"], 1)
                    act.wait_ge(m["norm_out"], l + 1)
                    for ch in range(2):
                        nc.scalar.activation(sq[:, ch, :], conv[:, ch, :], ACT.Silu, bias=small[:, ch, CNB:CNB + 1], scale=small[:, ch, CG:CG + 1])
                    act.drain()
                    nc.scalar.activation(xT_hi[:, 0:2, :], sq[:, :, :], ACT.Copy).then_inc(m["silu_out"], 1)
                    act.wait_ge(m["scan_out"], l + 1)
                    nc.scalar.activation(xT_hi[:, 2:4, :], xc[:, :, :], ACT.Copy).then_inc(m["y_hi"], 1)

                @block.vector
                def _(dve):
                    V = nc.vector
                    V.tensor_scalar(lamc[:, :, 0], small[:, :, LAM], -1.0, None, ALU.mult)
                    dve.drain()
                    V.tensor_tensor(lamc[:, :, 0], lamc[:, :, 0], small[:, :, LAM], ALU.min)
                    dve.drain().then_inc(m["chain_a"], 1)
                    dve.wait_ge(m["chain_b"], 4 * l + 1)
                    V.tensor_scalar(lamc[:, :, 2], lamc[:, :, 1], 1.0, None, ALU.add)
                    dve.drain().then_inc(m["chain_a"], 1)
                    V.tensor_scalar(lamc[:, :, 4], lamc[:, :, 2], -1.0, None, ALU.add)
                    dve.drain()
                    V.tensor_scalar(lamc[:, :, 5], lamc[:, :, 4], 0.0, None, ALU.is_equal)
                    V.tensor_scalar(lamc[:, :, 4], lamc[:, :, 4], 1e-30, None, ALU.max)
                    dve.drain()
                    V.tensor_tensor(lamc[:, :, 5], lamc[:, :, 5], lamc[:, :, 1], ALU.mult)
                    V.reciprocal(lamc[:, :, 4], lamc[:, :, 4])
                    dve.drain()
                    V.tensor_tensor(lamc[:, :, 4], lamc[:, :, 4], lamc[:, :, 1], ALU.mult)
                    dve.drain()
                    dve.wait_ge(m["chain_b"], 4 * l + 2)
                    V.tensor_tensor(lamc[:, :, 4], lamc[:, :, 4], lamc[:, :, 3], ALU.mult)
                    dve.drain()
                    V.tensor_tensor(lamc[:, :, 4], lamc[:, :, 4], lamc[:, :, 5], ALU.add)
                    V.tensor_scalar(lamc[:, :, 6], small[:, :, LAM], 0.0, None, ALU.min)
                    dve.drain()
                    V.tensor_tensor(lamc[:, :, 6], lamc[:, :, 6], lamc[:, :, 4], ALU.subtract)
                    dve.drain()
                    V.tensor_scalar(lamc[:, :, 7], lamc[:, :, 6], -LRU_C, None, ALU.mult)
                    V.tensor_scalar(lamc[:, :, 6], lamc[:, :, 6], LRU_C, None, ALU.mult)
                    dve.drain().then_inc(m["chain_a"], 1)
                    for k in range(LRU_K):
                        for ch in range(2):
                            if k == 0:
                                V.tensor_scalar(xc[:, ch, :], xb[:, ch, 0:SEQ], small[:, ch, LT:LT + 1], small[:, ch, LB:LB + 1], ALU.mult, ALU.add)
                            else:
                                V.scalar_tensor_tensor(xc[:, ch, :], xb[:, ch, k:k + SEQ], small[:, ch, LT + k:LT + k + 1], xc[:, ch, :], ALU.mult, ALU.add)
                        dve.drain()
                    dve.drain().then_inc(m["lru_conv_done"], 1)
                    dve.wait_ge(m["mean_done"], l + 1)
                    for ch in range(2):
                        V.tensor_tensor(conv[:, ch, :], conv[:, ch, :], PS[:, 7, :], ALU.subtract)
                    dve.drain()
                    V.tensor_tensor(sq[:, :, :], conv[:, :, :], conv[:, :, :], ALU.mult).then_inc(m["sq_done"], 1)
                    dve.wait_ge(m["gates_out"], l + 1)
                    V.tensor_tensor(xc[:, :, :], xc[:, :, :], i_g[:, :, :], ALU.mult)
                    dve.drain()
                    dve.wait_ge(m["chain_b"], 4 * l + 3)
                    V.tensor_scalar(i_g[:, :, :], th[:, :, :], 1.0, None, ALU.add)
                    dve.drain()
                    V.reciprocal(i_g[:, :, :], i_g[:, :, :])
                    dve.drain()
                    V.scalar_tensor_tensor(th[:, :, :], th[:, :, :], 2.0, i_g[:, :, :], ALU.mult, ALU.mult)
                    dve.drain().then_inc(m["chain_a"], 1)
                    dve.wait_ge(m["chain_b"], 4 * l + 4)
                    V.tensor_tensor(xc[:, :, :], xc[:, :, :], th[:, :, :], ALU.mult)
                    dve.drain()
                    for ch in range(2):
                        V.tensor_tensor_scan(th[:, ch, :], sig[:, ch, :], xc[:, ch, :], 0.0, ALU.mult, ALU.add)
                    dve.drain()
                    V.tensor_tensor(xc[:, :, :], th[:, :, :], gb[:, :, :], ALU.mult).then_inc(m["scan_out"], 1)
                    dve.wait_ge(m["std_out"], l + 1)
                    V.reciprocal(xb[:, 0, 0:SEQ], xb[:, 0, 0:SEQ])
                    dve.drain()
                    for ch in range(2):
                        V.tensor_tensor(conv[:, ch, :], conv[:, ch, :], xb[:, 0, 0:SEQ], ALU.mult)
                    dve.drain().then_inc(m["norm_out"], 1)
                    dve.wait_ge(m["silu_out"], l + 1)
                    V.tensor_tensor(xT_lo[:, 0:2, :], sq[:, :, :], xT_hi[:, 0:2, :].bitcast(f32), ALU.subtract)
                    dve.wait_ge(m["y_hi"], l * 5 + 1)
                    V.tensor_tensor(xT_lo[:, 2:4, :], xc[:, :, :], xT_hi[:, 2:4, :].bitcast(f32), ALU.subtract)

            with nc.Block() as block:
                @block.vector
                def _(dve):
                    V = nc.vector
                    with dve.Fori(0, 4) as c4:
                        V.tensor_copy(qs[:, :], qT[:, ds(c4, 1), :]).then_inc(m["q_staged"], 1)
                        for p in range(2):
                            u = l * 8 + 2 * c4 + p
                            sc = PS[:, 2 * p:2 * p + 2, :].rearrange("q a (b k) -> q (a b) k", k=BAND)
                            dve.wait_ge(m["scores_done"], u + 1)
                            V.tensor_tensor(prob[:, p, :, :], sc, bias_tab[:, ds(2 * c4 + p, 1), :].to_broadcast([P, TB, BAND]), ALU.add)
                            dve.drain()
                            V.memset(prob[:, p, 0, 0:P], NEG)
                            dve.drain()
                            V.tensor_reduce(smax[:, :], prob[:, p, :, :], AX.X, ALU.max)
                            dve.drain()
                            V.tensor_scalar(nmax[:, :], smax[:, :], sink_l[:, ds(2 * c4 + p, 1)], -1.0, ALU.max, ALU.mult)
                            dve.drain()
                            V.tensor_scalar(smax[:, :], nmax[:, :], sink_l[:, ds(2 * c4 + p, 1)], None, ALU.add)
                            dve.drain().then_inc(m["max_out"], 1)
                            dve.wait_ge(m["ptr_done"], u + 1)
                            V.tensor_copy(pT[:, :, :, :], PS[:, 4:6, :].rearrange("k a (b q) -> k a b q", q=P)).then_inc(m["pt_out"], 1)
                            V.tensor_tensor(dsum[:, :], dsum[:, :], esink[:, :], ALU.add)
                            dve.drain()
                            V.reciprocal(dsum[:, :], dsum[:, :])
                            dve.drain()
                            dve.wait_ge(m["o_done"], u + 1)
                            V.tensor_tensor(o_tok[:, :, ds((c4 + 4 * p) * HD, HD)], PS[:, 6, 0:TB * HD].rearrange("q (b d) -> q b d", d=HD),
                                            dsum[:, :].unsqueeze(2).to_broadcast([P, TB, HD]), ALU.mult).then_inc(m["o_out"], 1)

                @block.scalar
                def _(act):
                    with act.Fori(0, 4) as c4:
                        for p in range(2):
                            u = l * 8 + 2 * c4 + p
                            act.wait_ge(m["max_out"], u + 1)
                            nc.scalar.activation(esink[:, :], smax[:, :], ACT.Exp)
                            for b in range(TB):
                                nc.scalar.activation(prob[:, p, b, :], prob[:, p, b, :], ACT.Exp, bias=nmax[:, b:b + 1], accum_out=dsum[:, b:b + 1])
                            act.drain().then_inc(m["probs_out"], 1)

                @block.tensor
                def _(pe):
                    with pe.Fori(0, 4) as c4:
                        pe.wait_ge(m["q_staged"], l * 4 + c4 + 1)
                        for p in range(2):
                            hp = slice(p * HD, (p + 1) * HD)
                            for b in range(TB):
                                last = nc.tensor.matmul(PS[:, 2 * p + b // 2, (b % 2) * BAND:(b % 2 + 1) * BAND], qs[hp, b * P:(b + 1) * P], kT[hp, b * P:b * P + BAND], start=b % 2 == 0, stop=b % 2 == 1, skip_group_check=True)
                            last.then_inc(m["scores_done"], 1)
                        for p in range(2):
                            u = l * 8 + 2 * c4 + p
                            pe.wait_ge(m["probs_out"], u + 1)
                            for j in range(2):
                                for b in range(TB):
                                    last = nc.tensor.transpose(PS[:, 4 + j, b * P:(b + 1) * P], prob[:, p, b, j * P:(j + 1) * P], ident[:, :])
                            last.then_inc(m["ptr_done"], 1)
                            pe.wait_ge(m["pt_out"], u + 1)
                            for b in range(TB):
                                for j in range(2):
                                    last = nc.tensor.matmul(PS[:, 6, b * HD:(b + 1) * HD], pT[:, j, b, :], vt[:, b + j, p * HD:(p + 1) * HD], start=j == 0, stop=j == 1, skip_group_check=True)
                            last.then_inc(m["o_done"], 1)
                            pe.wait_ge(m["o_out"], u + 1)

            with nc.Block() as block:
                @block.sync
                def _(sp):
                    for n in range(N_MOUT):
                        half, kp = n // 4, n % 4
                        load_tile(sp, T(N_MIN + n), w_out[l, kp * 2 * P:(kp + 1) * 2 * P, half * HALF:(half + 1) * HALF].rearrange("(k p) n -> p k n", p=P))

                @block.scalar
                def _(act):
                    split_hi(T(N_MIN))
                    split_hi(T(N_MIN + 1))
                    for kc in range(4):
                        act.wait_ge(m["otr_done"], l * 4 + kc + 1)
                        nc.scalar.activation(xT_hi[:, 4 + kc, :], PS[:, 4 + kc, :], ACT.Copy).then_inc(m["y_hi"], 1)
                    for n in range(2, N_MOUT):
                        split_hi(T(N_MIN + n))
                    layer_norm_act(act, m["var_ready"], m["rstd_ready"], l + 1)

                @block.vector
                def _(dve):
                    split_lo(T(N_MIN))
                    split_lo(T(N_MIN + 1))
                    for kc in range(4):
                        dve.wait_ge(m["y_hi"], l * 5 + kc + 2)
                        nc.vector.tensor_tensor(xT_lo[:, 4 + kc, :], PS[:, 4 + kc, :], xT_hi[:, 4 + kc, :].bitcast(f32), ALU.subtract).then_inc(m["y_ready"], 1)
                    for n in range(2, N_MOUT):
                        split_lo(T(N_MIN + n))
                        if n == 5:
                            dve.wait_ge(w_used, T(N_MIN + 3).plus(1))
                            for b in range(TB):
                                nc.vector.scalar_tensor_tensor(xtok[:, b, 0:HALF], xtok[:, b, 0:HALF], ALPHA, PS[:, b, :], ALU.mult, ALU.add)
                    dve.wait_ge(w_used, T(N_MIN + 7).plus(1))
                    for b in range(TB):
                        nc.vector.scalar_tensor_tensor(xtok[:, b, HALF:D], xtok[:, b, HALF:D], ALPHA, PS[:, 4 + b, :], ALU.mult, ALU.add)
                    dve.drain()
                    layer_norm_dve(dve, None, m["var_ready"], m["rstd_ready"], l + 1)

                @block.tensor
                def _(pe):
                    for kc in range(4):
                        for b in range(TB):
                            last = nc.tensor.transpose(PS[:, 4 + kc, b * P:(b + 1) * P], o_tok[:, b, kc * P:(kc + 1) * P], ident[:, :])
                        last.then_inc(m["otr_done"], 1)
                    for n in range(N_MOUT):
                        half, kp = n // 4, n % 4
                        t = T(N_MIN + n)
                        pe.wait_ge(w_lo, t.plus(1))
                        if kp >= 2 and half == 0:
                            pe.wait_ge(m["y_ready"], l * 4 + 2 * (kp - 1))
                        for kk in range(2):
                            kc = 2 * kp + kk
                            for b in range(TB):
                                last = product(PS[:, 4 * half + b, :], XT, (slice(None), kc, slice(b * P, (b + 1) * P)), W, (slice(None), t.slot, slice(kk * HALF, (kk + 1) * HALF)), kc == 0, kc == KC - 1)
                        last.then_inc(w_used, 1)

    def residual_affine(pool, n_rows, read_sem, read_value):
        pool.wait_ge(rows_loaded, 32 * n_rows)
        pool.wait_ge(read_sem, read_value)
        row = lambda r: r[:, :].unsqueeze(1).to_broadcast([P, TB, D])
        nc.gpsimd.tensor_tensor(xtok[:, :, :], xtok[:, :, :], row(g_row), ALU.mult)
        pool.drain()
        nc.gpsimd.tensor_tensor(xtok[:, :, :], xtok[:, :, :], row(b_row), ALU.add).then_inc(residual_ready, 1)

    fin_rows = sem("final_rows_loaded")

    with nc.Fori(0, LAYERS) as l:
        def tiles(off):
            return lambda at, i=0: Tile(T0 + off + at, l * (N_LAYER // 2) + i)
        ffn(0, l, tiles(0), None, None)
        mixer(l, tiles(N_FFN))
        ffn(1, l, tiles(N_FFN + N_MIN + N_MOUT), lambda dve: dve.wait_ge(residual_ready, 2 * l + 2), lambda pool: residual_affine(pool, 2 * l + 2, F[1]["tr_done"], KC * (l + 1)))
        with nc.Block() as block:
            @block.sync
            def _(sp):
                sp.dma_start(g_row[:, :], A["ln_g_2"][l, 2, :].partition_broadcast(P)).then_inc(fin_rows, 16)
                sp.dma_start(b_row[:, :], A["ln_b_2"][l, 2, :].partition_broadcast(P)).then_inc(fin_rows, 16)

            @block.vector
            def _(dve):
                dve.wait_ge(fin_rows, 32 * (l + 1))
                for b in range(TB):
                    nc.vector.tensor_tensor(xtok[:, b, :], xtok[:, b, :], g_row[:, :], ALU.mult)
                dve.drain()
                for b in range(TB):
                    nc.vector.tensor_tensor(xtok[:, b, :], xtok[:, b, :], b_row[:, :], ALU.add)


def constants():
    i = np.arange(P)
    at = np.arange(3 * P)
    distance = np.maximum(2 * P - 1 - at, 0)
    exact = REL_BUCKETS // 2
    large = exact + (np.log(np.maximum(distance, 1).astype(np.float32) / exact) / math.log(REL_MAX_DIST / exact) * (REL_BUCKETS - exact)).astype(np.int32)
    bucket = np.where(distance < exact, distance, np.minimum(large, REL_BUCKETS - 1))
    q, k = np.arange(P)[:, None], np.arange(2 * P)[None, :]
    back = q - k + P
    col, kcol = (np.arange(P) % GRID)[:, None], np.arange(GRID)[None, :]
    start = np.clip(col - KW // 2, 0, GRID - KW)
    wide = lambda row: np.ascontiguousarray(np.broadcast_to(row.astype(np.float32), (P, row.size)))
    return {
        "ident": np.eye(P, dtype=np.float32),
        "before": (i[:, None] < i[None, :]).astype(np.float32),
        "iota": wide(i),
        "first4": wide(np.array([4, 3, 2, 1])),
        "jrow": wide(np.arange(24)),
        "nb_mask": np.where((kcol >= start) & (kcol < start + KW), 0, NEG).astype(np.float32),
        "band_mask": np.where((back >= 0) & (back < P), 0, NEG).astype(np.float32),
        "bucket_hot": (bucket[None, :] == np.arange(REL_BUCKETS)[:, None]).astype(np.float32),
    }


PAIRS = [h for c in range(4) for h in (c, c + 4)]


def laid_out(inputs):
    g = lambda n: np.asarray(inputs[n])
    c = np.ascontiguousarray
    A = {n: g(n) for n in (
        "x", "ctx", "w_ada", "b_ada", "w_in", "rpb", "sgu_ln", "w_out", "rg_b", "re_b", "w1", "w3", "w2", "ffn_w_gate_2", "ffn_w_up_2",
        "ffn_w_down_2", "ln_g_2", "ln_b_2", "lru_wa_2", "lru_wx_2", "w_out_2")}
    A["cT"] = c(np.stack([g("c")[0], g("c_ctx")], 0).reshape(2, KC, P).transpose(2, 1, 0))
    A["b_adaT"] = c(g("b_ada")[0].reshape(6, KC, P).transpose(2, 0, 1))
    A["out_gainT"] = c(g("out_gain")[0].reshape(KC, P).T)
    A["qk_gainT"] = c(np.stack([np.tile(g("q_gain")[0], 2), np.tile(g("k_gain")[0], 2)], 1))
    A["sgu_wT"] = c(g("sgu_w")[0].transpose(2, 0, 1))
    A["sgu_bT"] = c(g("sgu_b")[0].T)
    A["router_w"] = c(np.concatenate([g("rg_w")[0], g("re_w")[0].transpose(1, 0, 2).reshape(D, EXPERTS)], 1).reshape(KC, P, GROUPS + EXPERTS).transpose(1, 0, 2))
    A["lnT_2"] = c(np.stack([g("ln_g_2"), g("ln_b_2")], 2).reshape(LAYERS, 3, 2, KC, P).transpose(0, 4, 1, 2, 3))
    w = g("w_in_2")
    wq = w[:, :, 1024:1536].reshape(LAYERS, D, QH, HD)[:, :, PAIRS].reshape(LAYERS, D, QH * HD)
    A["w_in_2"] = c(np.concatenate([w[:, :, :1024], wq, w[:, :, 1536:]], 2))
    A["rel_bias_2"] = c(g("rel_bias_2")[:, PAIRS])
    A["attn_sinks_2"] = c(g("attn_sinks_2")[:, PAIRS])
    rows = [g("conv_dw_w_2")] + [g(n)[:, None] for n in ("conv_dw_b_2", "conv_ln_g_2", "conv_ln_b_2")] + [g("lru_conv_w_2")] + [
        g(n)[:, None] for n in ("lru_conv_b_2", "lru_ba_2", "lru_bx_2", "lru_lambda_2")]
    A["mix_small_2"] = c(np.concatenate(rows, 1).reshape(LAYERS, 42, 2, P).transpose(0, 3, 2, 1))
    A.update(constants())
    return A


def build(nc, A, out):
    with ExitStack() as ctx:
        S = shared(nc, ctx)
        first_block(nc, ctx, S, A)
        second_block(nc, ctx, N_FIRST, S, A)
        stored = ctx.enter_context(nc.semaphore("stored"))
        with nc.Block() as block:
            @block.sync
            def _(sp):
                sp.dma_start(out[0].rearrange("(b p) d -> p b d", p=P), S.xtok[:, :, :]).then_inc(stored, 16)
                sp.wait_ge(stored, 16)


def kernel(**inputs):
    import concourse.bacc as bacc
    from concourse.bass_utils import run_bass_kernel_spmd as run

    nc = bacc.Bacc("TRN2", target_bir_lowering=False, num_devices=1)
    arrays, A = {}, {}
    for name, a in laid_out(inputs).items():
        arrays["in_" + name] = a
        A[name] = nc.dram_tensor("in_" + name, a.shape, mybir.dt.from_np(a.dtype), kind="ExternalInput").ap()
    out = nc.dram_tensor("out_x", (1, SEQ, D), f32, kind="ExternalOutput").ap()
    build(nc, A, out)
    return run(nc, [arrays], core_ids=[0]).results[0]["out_x"]
```

```python
import concourse.bass as bass
from concourse import mybir
from contextlib import ExitStack
import numpy as np
import math

f32 = mybir.dt.float32
f32r = mybir.dt.float32r
ALU = mybir.AluOpType
ACT = mybir.ActivationFunctionType
AX = mybir.AxisListType
ds = bass.ds

P = 128
SEQ = 512
D = 1024
KC = D // P
TB = SEQ // P
HALF = 512
LAYERS = 2
D_FF = 2816
FC = D_FF // P
ALPHA = (2.0 * LAYERS) ** 0.25
LN_EPS = 1e-5
N_UP = 2 * FC
N_DOWN = FC
N_FFN = N_UP + N_DOWN
N_MIN = 14
N_MOUT = 8
N_LAYER = 2 * N_FFN + N_MIN + N_MOUT
HD = 64
CONV_K = 31
LRU_K = 4
LRU_C = 8.0
QH = 8
BAND = 2 * P
NEG = -1e30
REL_BUCKETS = 32
REL_MAX_DIST = 128
DIST = 3 * P


CTX = 256
CB_ = CTX // P
EPS = 1e-6
NCOL = 5
NB_ROWS = 8
GRID = 64
KW = 16
RP = 2 * GRID - 1
NDR = 15
GROUPS, EPG, EXPERTS = 4, 4, 16
D_EXP = 512
MAX_BLOCKS = 23
N_WIN = 4 * 7
AW = 512
AN = D // AW
N_FIRST = N_WIN + 8


class Tile:

    def __init__(self, at, pairs=0):
        self.at, self.pairs, self.slot = at, pairs, at % 2

    def plus(self, n):
        return self.at + n + 2 * self.pairs

    def loads(self):
        return 16 * (self.at // 2 + 1) + 16 * self.pairs


class DistanceRows:

    def __init__(self, nc, sb, sem, A, PS):
        self.nc, self.A, self.PS = nc, A, PS
        self.rows = nc.dram_tensor("dist_rows", [QH, P, DIST], f32, kind="Internal").ap()
        self.bucket_hot, self.relb = sb("bucket_hot", [32, DIST]), sb("relb", [32, QH])
        self.mask, self.by_dist = sb("distance_mask", [QH, DIST]), sb("by_dist", [QH, DIST])
        self.loaded, self.product, self.ready, self.stored = [sem("dist_" + n) for n in ("loaded", "product", "ready", "stored")]

    def sync(self, sp):
        sp.dma_start(self.bucket_hot[:, :], self.A["bucket_hot"]).then_inc(self.loaded, 16)
        sp.dma_start(self.relb[:, :], self.A["rel_bias_2"]).then_inc(self.loaded, 16)
        sp.dma_start(self.mask[:, :], self.A["distance_mask"]).then_inc(self.loaded, 16)
        sp.wait_ge(self.ready, 1)
        for h in range(QH):
            sp.dma_start(self.rows[h:h + 1, :, :], self.by_dist[h:h + 1, :].unsqueeze(1).to_broadcast([1, P, DIST])).then_inc(self.stored, 16)
        sp.wait_ge(self.stored, 16 * QH)

    def tensor(self, pe):
        pe.wait_ge(self.loaded, 48)
        self.nc.tensor.matmul(self.PS[0:QH, 0, 0:DIST], self.relb[:, :], self.bucket_hot[:, :], start=True, stop=True).then_inc(self.product, 1)

    def vector(self, dve):
        dve.wait_ge(self.product, 1)
        self.nc.vector.tensor_tensor(self.by_dist[:, :], self.PS[0:QH, 0, 0:DIST], self.mask[:, :], ALU.add).then_inc(self.ready, 1)

    def table(self):
        return bass.AP(self.rows.tensor, P - 1, [[DIST - 1, P], [P * DIST, QH], [1, BAND]])


class Shared:
    pass


def shared(nc, ctx):
    S = Shared()
    sb = lambda n, shape, dt=f32: ctx.enter_context(nc.sbuf_tensor(n, shape, dt))
    sem = lambda n: ctx.enter_context(nc.semaphore(n))
    S.xtok = sb("xtok", [P, TB, D])
    S.xT_hi = sb("xT_hi", [P, KC, SEQ], f32r)
    S.xT_lo = sb("xT_lo", [P, KC, SEQ], f32r)
    S.raw = sb("w_raw", [P, 2, D])
    S.whi = sb("w_part_hi", [P, 2, D], f32r)
    S.wlo = sb("w_part_lo", [P, 2, D], f32r)
    S.ident = sb("identity", [P, P])
    S.PS = ctx.enter_context(nc.psum_tensor("PS", [P, 8, 512], f32))
    S.w_loaded = [sem("w_loaded0"), sem("w_loaded1")]
    S.w_hi, S.w_lo, S.w_used = sem("w_hi_ready"), sem("w_lo_ready"), sem("w_used")
    return S


def first_block(nc, ctx0, S, A, stop=None):
    xtok, xT_hi, xT_lo, raw, whi, wlo, ident, PS = S.xtok, S.xT_hi, S.xT_lo, S.raw, S.whi, S.wlo, S.ident, S.PS
    w_loaded, w_hi, w_lo, w_used = S.w_loaded, S.w_hi, S.w_lo, S.w_used
    ctx = ctx0.enter_context(ExitStack())

    own_sems = []

    def sem(n):
        own_sems.append(nc.alloc_semaphore(n))
        return own_sems[-1]

    def sb(c, n, shape, dt=f32):
        return c.enter_context(nc.sbuf_tensor(n, shape, dt))

    def load_tile(sp, t, src):
        if t.plus(-1) > 0:
            sp.wait_ge(w_lo, t.plus(-1))
        sp.dma_start(raw[:, t.slot, :].rearrange("p (a n) -> p a n", n=src.shape[-1]), src).then_inc(w_loaded[t.slot], 16)

    def split_hi(t):
        nc.scalar.wait_ge(w_loaded[t.slot], t.loads())
        if t.plus(-1) > 0:
            nc.scalar.wait_ge(w_used, t.plus(-1))
        nc.scalar.activation(whi[:, t.slot, :], raw[:, t.slot, :], ACT.Copy).then_inc(w_hi, 1)

    def split_lo(t):
        nc.vector.wait_ge(w_hi, t.plus(1))
        nc.vector.tensor_tensor(wlo[:, t.slot, :], raw[:, t.slot, :], whi[:, t.slot, :].bitcast(f32), ALU.subtract).then_inc(w_lo, 1)

    def product(out, a, a_at, b, b_at, first, last):
        nc.tensor.matmul(out, a[0][a_at], b[0][b_at], start=first, stop=False)
        nc.tensor.matmul(out, a[0][a_at], b[1][b_at], start=False, stop=False)
        return nc.tensor.matmul(out, a[1][a_at], b[0][b_at], start=False, stop=last)

    W = (whi, wlo)
    XT = (xT_hi, xT_lo)

    ga_row = sb(ctx, "ga_row", [P, D])
    modT = sb(ctx, "modT", [P, 2, KC, 2])
    eps6 = sb(ctx, "eps6", [P, 1])
    ssum = sb(ctx, "sum_of_squares", [P, 8])
    tmp = sb(ctx, "evac_tmp1", [P, 2, SEQ])
    out_gT = sb(ctx, "out_gainT", [P, KC])
    rpad_rows = nc.dram_tensor("rpb_rows", [8 * NDR, GRID, RP], f32, kind="Internal").ap()
    ys = nc.dram_tensor("expert_rows", [MAX_BLOCKS * P, D], f32, kind="Internal").ap()

    s_in, s_c, s_cb, s_scb = sem("x_loaded"), sem("c_loaded"), sem("c_silu"), sem("c_bcast")
    s_aw = [sem(f"ada_w{k}") for k in range(5)]
    s_brow, s_x = sem("ada_bias_rows"), sem("x_in")
    s_mtr, s_rpc = sem("ada_tr"), sem("rpb_copied")
    s_mm, s_mod, s_bias = sem("ada_mm"), sem("ada_out"), sem("ada_bias")
    s_rt, s_rpb, s_rpr, s_rps = sem("ssum_root"), sem("rpb_in"), sem("rpb_rows_sem"), sem("rpb_pad")
    ada = ExitStack()
    AR = 5
    wada = sb(ada, "wada", [P, AR, KC, AW])
    sc2 = sb(ada, "silu_c", [P, KC, 2])
    c2 = sb(ada, "c_in", [P, KC, 2])
    scb = sb(ada, "silu_c_wide", [P, KC, P])
    b_adaT = sb(ada, "b_adaT", [P, 6, KC])
    rpad = sb(ada, "rpb_padded", [8 * NDR, RP])
    shf_new, scf_new, gf_new = [sb(ada, n, [P, D]) for n in ("shf_new", "scf_new", "gf_new")]
    late_rows = nc.dram_tensor("late_rows", [3, D], f32, kind="Internal").ap()
    s_late, s_late_out = sem("late_rows_ready"), sem("late_rows_stored")
    RC = 16
    rcopies = sb(ada, "rpb_copies", [8 * NDR, RC, RP])
    two_rows = sb(ada, "two_rows", [2, 2, AW])
    turns = [("f", 0, 0), ("f", 1, 1), ("r", 3, shf_new), ("r", 4, scf_new), ("r", 5, gf_new), ("r", 2, ga_row)]
    with nc.Block() as block:
        @block.sync
        def _(sp):
            sp.dma_start(c2[:, :, :], A["cT"]).then_inc(s_c, 16)
            for n, (_, sec, _) in enumerate(turns):
                for h in range(AN):
                    i = AN * n + h
                    if i == 2:
                        for _, bsec, row in turns[2:]:
                            sp.dma_start(row[:, :], A["b_ada"][0, bsec * D:(bsec + 1) * D].partition_broadcast(P)).then_inc(s_brow, 16)
                    if i == 4:
                        sp.dma_start(xtok[:, :, :], A["x"][0].rearrange("(b p) d -> p b d", p=P)).then_inc(s_x, 16)
                    if i >= AR:
                        sp.wait_ge(s_mm, i - AR + 1)
                    sp.dma_start(wada[:, i % AR, :, :], A["w_ada"][0, :, sec * D + h * AW:sec * D + (h + 1) * AW].rearrange("(k p) n -> p k n", p=P)).then_inc(s_aw[i % AR], 16)

        @block.gpsimd
        def _(pool):
            nc.gpsimd.memset(rpad[:, :], 0.0)
            nc.gpsimd.memset(eps6[:, :], EPS)
            pool.drain().then_inc(s_rps, 1)

        @block.scalar
        def _(act):
            act.dma_start(ident[:, :], A["ident"]).then_inc(s_in, 16)
            act.dma_start(out_gT[:, :], A["out_gainT"]).then_inc(s_x, 16)
            act.wait_ge(s_c, 16)
            nc.scalar.activation(sc2[:, :, :], c2[:, :, :], ACT.Silu).then_inc(s_cb, 1)
            act.dma_start(b_adaT[:, :, :], A["b_adaT"]).then_inc(s_bias, 16)
            act.wait_ge(s_rps, 1)
            act.dma_start(rpad[:, 48:79], A["rpb"][0].rearrange("h r w -> (h r) w")).then_inc(s_rpb, 16)
            act.wait_ge(s_rpb, 16)
            nc.scalar.activation(rcopies[:, :, :], rpad[:, :].unsqueeze(1).to_broadcast([8 * NDR, RC, RP]), ACT.Copy).then_inc(s_rpc, 1)
            act.wait_ge(s_x, 32)
            for b in range(TB):
                nc.scalar.activation(xT_lo[:, 2 * b:2 * b + 2, :].rearrange("p a n -> p (a n)"), xtok[:, b, :], ACT.Square, accum_out=ssum[:, b:b + 1])
            act.drain()
            nc.scalar.activation(ssum[:, 0:TB], ssum[:, 0:TB], ACT.Sqrt, bias=eps6[:, 0:1], scale=1.0 / D).then_inc(s_rt, 1)
            act.wait_ge(s_mm, AN * len(turns) - AR - 1)
            act.wait_ge(s_rpc, 1)
            act.dma_start(rpad_rows.rearrange("a (g r) w -> a g (r w)", r=RC),
                          rcopies[:, :, :].rearrange("a r w -> a (r w)").unsqueeze(1).to_broadcast([8 * NDR, GRID // RC, RC * RP])).then_inc(s_rpr, 16)
            act.wait_ge(s_late, 1)
            for k, row in enumerate((shf_new, scf_new, gf_new)):
                act.dma_start(late_rows[k:k + 1, :], row[0:1, :]).then_inc(s_late_out, 16)
            act.wait_ge(s_late_out, 48)
            act.wait_ge(s_rpr, 16)

        @block.vector
        def _(dve):
            dve.wait_ge(s_cb, 1)
            nc.vector.tensor_copy(scb[:, :, :], sc2[:, :, 0:1].to_broadcast([P, KC, P])).then_inc(s_scb, 1)
            for n, (kind, sec, dst) in enumerate(turns):
                for h in range(AN):
                    i = AN * n + h
                    dve.wait_ge(s_mm, i + 1)
                    if i == 1:
                        dve.wait_ge(s_bias, 16)
                    if i == 2 * AN:
                        dve.wait_ge(s_brow, 64)
                    if kind == "f":
                        if i >= 2:
                            dve.wait_ge(s_mtr, i - 1)
                        nc.vector.tensor_copy(two_rows[:, i % 2, :], PS[0:2, i % 2, 0:AW]).then_inc(s_mod, 1)
                    else:
                        nc.vector.tensor_tensor(dst[:, h * AW:(h + 1) * AW], PS[:, i % 2, 0:AW], dst[:, h * AW:(h + 1) * AW], ALU.add).then_inc(s_mod, 1)
                    if 0 < i <= 2 * AN:
                        k = i - 1
                        dve.wait_ge(s_mtr, k + 1)
                        at = slice(k % AN * (AW // P), (k % AN + 1) * (AW // P))
                        nc.vector.tensor_tensor(modT[:, k // AN, at, :], PS[:, 4 + k, 0:2 * AW // P].rearrange("p (c v) -> p c v", v=2),
                                                b_adaT[:, k // AN, at].unsqueeze(2).to_broadcast([P, AW // P, 2]), ALU.add)
                    if i == 2 * AN:
                        dve.drain()
                        nc.vector.tensor_scalar(modT[:, 1, :, :], modT[:, 1, :, :], 1.0, None, ALU.add)
                        dve.wait_ge(s_rt, 1)
                        nc.vector.reciprocal(ssum[:, 0:TB], ssum[:, 0:TB])
                if sec == 4:
                    dve.drain()
                    nc.vector.tensor_scalar(scf_new[:, :], scf_new[:, :], 1.0, None, ALU.add)
                if sec == 5:
                    dve.drain().then_inc(s_late, 1)

        @block.tensor
        def _(pe):
            pe.wait_ge(s_scb, 1)
            for n, (kind, sec, _) in enumerate(turns):
                for h in range(AN):
                    i = AN * n + h
                    pe.wait_ge(s_aw[i % AR], 16 * (i // AR + 1))
                    if i >= 2:
                        pe.wait_ge(s_mod, i - 1)
                    for kc in range(KC):
                        if kind == "f":
                            last = nc.tensor.matmul(PS[0:2, i % 2, 0:AW], sc2[:, kc, :], wada[:, i % AR, kc, :], start=kc == 0, stop=kc == KC - 1)
                        else:
                            last = nc.tensor.matmul(PS[:, i % 2, 0:AW], scb[:, kc, :], wada[:, i % AR, kc, :], start=kc == 0, stop=kc == KC - 1)
                    last.then_inc(s_mm, 1)
                    if 0 < i <= 2 * AN:
                        pe.wait_ge(s_in, 16)
                        pe.wait_ge(s_mod, i)
                        for c in range(AW // P):
                            last = nc.tensor.transpose(PS[:, 3 + i, 2 * c:2 * c + 2], two_rows[:, (i - 1) % 2, c * P:(c + 1) * P], ident[0:2, 0:2])
                        last.then_inc(s_mtr, 1)
    ada.close()
    keep = ctx.enter_context(ExitStack())
    v_tok = sb(keep, "v_tok", [P, TB + CB_, HALF])
    ug = sb(keep, "u_gelu", [P, TB, HALF])
    vs = sb(keep, "vs_tok", [P, TB, HALF])
    qT = sb(keep, "qT1", [P, 4, SEQ])
    kT = sb(keep, "kT1", [P, 4, SEQ + CTX])
    qk_gain = sb(keep, "qk_gain", [P, 2])
    proj = ExitStack()
    q_tok = sb(proj, "q_tok", [P, TB, HALF])
    k_tok = sb(proj, "k_tok", [P, TB + CB_, HALF])
    sqb = sb(proj, "square_buf", [P, TB, HALF])
    hsum = sb(proj, "head_sums", [P, 3, TB * 8])
    ln_row = sb(proj, "sgu_ln_row", [P, HALF])
    nbt = sb(proj, "nb_bias", [P, 8, 16 * GRID])
    nbm = sb(proj, "nb_mask", [P, GRID])
    s_tab = sem("nb_table")
    xn = nbt[:, 0:TB + CB_, :]
    hcT = ExitStack()
    hc_hi = sb(hcT, "hc_hi", [P, KC, CTX], f32r)
    hc_lo = sb(hcT, "hc_lo", [P, KC, CTX], f32r)
    HC = (hc_hi, hc_lo)

    def chunk(i):
        kc, of_ctx = i % KC, i // KC
        src = PS[:, 4 + kc // 2, kc % 2 * CTX:(kc % 2 + 1) * CTX] if of_ctx else PS[:, kc, :]
        parts = (hc_hi[:, kc, :], hc_lo[:, kc, :]) if of_ctx else (xT_hi[:, kc, :], xT_lo[:, kc, :])
        return src, modT[:, 0, kc, of_ctx:of_ctx + 1], modT[:, 1, kc, of_ctx:of_ctx + 1], parts, tmp[:, kc % 2, 0:src.shape[-1]]

    def modulate_act(act, i):
        src, b, s, (hi, _), full = chunk(i)
        act.wait_ge(tr1, i + 1 if i < KC else i // 2 * 2 + 2)
        if i % 2 == 0:
            if i >= 2:
                act.wait_ge(rd1, i - 1)
            nc.scalar.activation(full, src, ACT.Identity, bias=b, scale=s)
        nc.scalar.activation(hi, src, ACT.Identity, bias=b, scale=s).then_inc(hi1, 1)

    def modulate_dve(dve, i):
        src, b, s, (hi, lo), full = chunk(i)
        if i % 2 == 1:
            dve.drain()
        dve.wait_ge(hi1, i + 1)
        if i % 2 == 1:
            nc.vector.tensor_scalar(full, src, s, b, ALU.mult, ALU.add)
            dve.drain()
        nc.vector.tensor_tensor(lo, full, hi.bitcast(f32), ALU.subtract).then_inc(rd1, 1)

    tr1, hi1, rd1, evac1 = sem("h_tr"), sem("h_hi"), sem("h_ready"), sem("proj_evac")
    nv, nr, lnv = sem("head_sq"), sem("head_root"), sem("vs_norm")
    cols = [0, 1, 2, 3, 4, 1, 2]
    s_nxb = sem("x_normed")
    s_ctx, s_row, s_cr, s_nx = sem("ctx_loaded"), sem("proj_rows"), sem("ctx_root"), sem("ctx_normed")
    with nc.Block() as block:
        @block.sync
        def _(sp):
            w_in_tile = lambda n: load_tile(sp, Tile(n), A["w_in"][0, n % 4 * 2 * P:(n % 4 + 1) * 2 * P, cols[n // 4] * HALF:(cols[n // 4] + 1) * HALF].rearrange("(k p) n -> p k n", p=P))
            w_in_tile(0)
            w_in_tile(1)
            sp.dma_start(xn[:, TB:, :], A["ctx"][0].rearrange("(b p) d -> p b d", p=P)).then_inc(s_ctx, 16)
            sp.dma_start(ln_row[:, :], A["sgu_ln"][0].partition_broadcast(P)).then_inc(s_row, 16)
            sp.dma_start(qk_gain[:, :], A["qk_gainT"]).then_inc(s_row, 16)
            for n in range(2, N_WIN):
                w_in_tile(n)

        @block.gpsimd
        def _(pool):
            pool.dma_start(nbm[:, :], A["nb_mask"]).then_inc(s_tab, 16)
            pool.wait_ge(tr1, 2 * KC)
            for up in range(2):
                for h in range(8):
                    skew = bass.AP(rpad_rows.tensor, h * NDR * GRID * RP + GRID - 1, [[RP - 1, GRID], [GRID * RP, NDR], [1, GRID]])
                    pool.dma_start(nbt[up * GRID:(up + 1) * GRID, h, up * GRID:(up + NDR) * GRID].rearrange("p (r k) -> p r k", k=GRID), skew).then_inc(s_tab, 16)
            pool.wait_ge(s_tab, 16 * 17)
            for up in range(2):
                at = slice(up * GRID, (up + 1) * GRID)
                for h in range(8):
                    t = nbt[at, h, up * GRID:(up + NDR) * GRID].rearrange("p (r k) -> p r k", k=GRID)
                    nc.gpsimd.tensor_tensor(t, t, nbm[at, :].unsqueeze(1).to_broadcast([GRID, NDR, GRID]), ALU.add)

        @block.tensor
        def _(pe):
            for b in range(TB):
                pe.wait_ge(s_nxb, b + 1)
                for kc in range(KC):
                    last = nc.tensor.transpose(PS[:, kc, b * P:(b + 1) * P], xn[:, b, kc * P:(kc + 1) * P], ident[:, :])
                    if b == TB - 1:
                        last.then_inc(tr1, 1)
            pe.wait_ge(rd1, 4)
            for n in range(N_WIN):
                g, kp = n // 4, n % 4
                t = Tile(n)
                if g == 0:
                    pe.wait_ge(rd1, 2 * kp + 2)
                if n == 2:
                    pe.wait_ge(rd1, KC)
                    pe.wait_ge(s_nx, 1)
                    for kc in range(KC):
                        for b in range(CB_):
                            last = nc.tensor.transpose(PS[:, 4 + kc // 2, (kc % 2 * CB_ + b) * P:(kc % 2 * CB_ + b + 1) * P], xn[:, TB + b, kc * P:(kc + 1) * P], ident[:, :])
                        last.then_inc(tr1, 1)
                if n == 4:
                    pe.wait_ge(rd1, 2 * KC)
                pe.wait_ge(w_lo, t.plus(1))
                if kp == 0 and g >= 2:
                    pe.wait_ge(evac1, g - 1)
                src, nb = (XT, TB) if g < NCOL else (HC, CB_)
                for kk in range(2):
                    kc = 2 * kp + kk
                    for b in range(nb):
                        last = product(PS[:, 4 * (g % 2) + b, :], src, (slice(None), kc, slice(b * P, (b + 1) * P)), W, (slice(None), t.slot, slice(kk * HALF, (kk + 1) * HALF)), kc == 0, kc == KC - 1)
                last.then_inc(w_used, 1)

        @block.scalar
        def _(act):
            split_hi(Tile(0))
            split_hi(Tile(1))
            for i in range(KC):
                modulate_act(act, i)
            split_hi(Tile(2))
            act.wait_ge(s_ctx, 16)
            for b in range(CB_):
                nc.scalar.activation(hc_lo[:, 4 * b:4 * b + 4, :].rearrange("p a n -> p (a n)"), xn[:, TB + b, :], ACT.Square, accum_out=ssum[:, TB + b:TB + b + 1])
            act.drain()
            nc.scalar.activation(ssum[:, TB:TB + CB_], ssum[:, TB:TB + CB_], ACT.Sqrt, bias=eps6[:, 0:1], scale=1.0 / D).then_inc(s_cr, 1)
            dst = [(q_tok[:, :, :], ACT.Copy), (k_tok[:, 0:TB, :], ACT.Copy), (v_tok[:, 0:TB, :], ACT.Copy), (ug[:, :, :], ACT.Gelu_apprx_tanh),
                   (vs[:, :, :], ACT.Gelu_apprx_tanh), (k_tok[:, TB:, :], ACT.Copy), (v_tok[:, TB:, :], ACT.Copy)]
            for g in range(7):
                for kp in range(4):
                    n = 4 * g + kp + 2
                    if 2 < n < N_WIN:
                        split_hi(Tile(n))
                    if n == 3:
                        for i in range(KC, 2 * KC):
                            modulate_act(act, i)
                    if kp == 2 and g in (1, 2, 6):
                        r = {1: 0, 2: 1, 6: 2}[g]
                        act.wait_ge(nv, r + 1)
                        w = TB * 8 if g != 6 else CB_ * 8
                        nc.scalar.activation(hsum[:, r, 0:w], hsum[:, r, 0:w], ACT.Sqrt, bias=eps6[:, 0:1], scale=1.0 / HD).then_inc(nr, 1)
                    if kp == 2 and g == 5:
                        act.wait_ge(lnv, 1)
                        nc.scalar.activation(ssum[:, 0:TB], ssum[:, 0:TB], ACT.Sqrt, bias=eps6[:, 0:1]).then_inc(lnv, 1)
                act.wait_ge(w_used, 4 * (g + 1))
                d, fn = dst[g]
                nb = d.shape[1]
                nc.scalar.activation(d, PS[:, 4 * (g % 2):4 * (g % 2) + nb, :], fn).then_inc(evac1, 1)

        @block.vector
        def _(dve):
            V = nc.vector
            for b in range(TB):
                V.tensor_scalar(xn[:, b, :], xtok[:, b, :], ssum[:, b:b + 1], None, ALU.mult).then_inc(s_nxb, 1)
            split_lo(Tile(0))
            split_lo(Tile(1))
            for i in range(KC):
                modulate_dve(dve, i)
            split_lo(Tile(2))
            dve.wait_ge(s_cr, 1)
            V.reciprocal(ssum[:, TB:TB + CB_], ssum[:, TB:TB + CB_])
            dve.drain()
            for b in range(CB_):
                V.tensor_scalar(xn[:, TB + b, :], xn[:, TB + b, :], ssum[:, TB + b:TB + b + 1], None, ALU.mult)
            dve.drain().then_inc(s_nx, 1)

            dve.wait_ge(s_row, 32)
            V.tensor_tensor(qk_gain[:, 0:1], qk_gain[:, 0:1], qk_gain[:, 1:2], ALU.mult)
            dve.drain()
            V.tensor_scalar(qk_gain[:, 0:1], qk_gain[:, 0:1], HD ** -0.5, None, ALU.mult)

            def head_norm(step, src, nb, r):
                s3 = src.rearrange("p b (h d) -> p (b h) d", d=HD)
                q3 = sqb[:, 0:nb, :].rearrange("p b (h d) -> p (b h) d", d=HD)
                if step == 0:
                    V.tensor_tensor(sqb[:, 0:nb, :], src, src, ALU.mult)
                    dve.drain()
                if step == 1:
                    V.tensor_reduce(hsum[:, r, 0:8 * nb], q3, AX.X, ALU.add).then_inc(nv, 1)
                if step == 2:
                    dve.wait_ge(nr, r + 1)
                    V.reciprocal(hsum[:, r, 0:8 * nb], hsum[:, r, 0:8 * nb])
                    dve.drain()
                if step == 3:
                    V.tensor_tensor(s3, s3, hsum[:, r, 0:8 * nb].unsqueeze(2).to_broadcast([P, 8 * nb, HD]), ALU.mult)

            def vs_norm(step):
                if step == 0:
                    for b in range(TB):
                        V.bn_stats(sqb[:, 0, 6 * b:6 * b + 6], vs[:, b, :])
                    dve.drain()
                if step == 1:
                    for b in range(TB):
                        V.bn_aggr(sqb[:, 1, 2 * b:2 * b + 2], sqb[:, 0, 6 * b:6 * b + 6])
                    dve.drain()
                    V.tensor_copy(ssum[:, 0:TB], sqb[:, 1, 0:2 * TB].rearrange("p (b v) -> p b v", v=2)[:, :, 1]).then_inc(lnv, 1)
                if step == 2:
                    dve.wait_ge(lnv, 2)
                    V.reciprocal(ssum[:, 0:TB], ssum[:, 0:TB])
                    dve.drain()
                    for b in range(TB):
                        V.tensor_scalar(vs[:, b, :], vs[:, b, :], sqb[:, 1, 2 * b:2 * b + 1], ssum[:, b:b + 1], ALU.subtract, ALU.mult)
                if step == 3:
                    dve.drain()
                    V.tensor_tensor(vs[:, :, :], vs[:, :, :], ln_row[:, :].unsqueeze(1).to_broadcast([P, TB, HALF]), ALU.mult)
                    dve.drain()

            for g in range(7):
                for kp in range(4):
                    n = 4 * g + kp + 2
                    if 2 < n < N_WIN:
                        split_lo(Tile(n))
                    if n == 3:
                        for i in range(KC, 2 * KC):
                            modulate_dve(dve, i)
                    if g >= 1 and kp == 0:
                        dve.wait_ge(evac1, g)
                    if g == 1:
                        head_norm(kp, q_tok[:, :, :], TB, 0)
                    if g == 2:
                        head_norm(kp, k_tok[:, 0:TB, :], TB, 1)
                    if g == 5:
                        vs_norm(kp)
                    if g == 6:
                        head_norm(kp, k_tok[:, TB:, :], CB_, 2)
    hcT.close()

    table = ctx.enter_context(ExitStack())
    tq, ev3, sg, so = sem("qk_tr"), sem("qk_evac"), sem("sgu_mm"), sem("sgu_out")
    s_w = sem("sgu_w_loaded")
    wsT = sb(proj, "sgu_wT", [P, 8, P])
    bsT = sb(proj, "sgu_bT", [P, 8])
    sgr = sem("sgu_ss")
    with nc.Block() as block:
        @block.sync
        def _(sp):
            sp.dma_start(wsT[:, :, :], A["sgu_wT"]).then_inc(s_w, 16)
            sp.dma_start(bsT[:, :], A["sgu_bT"]).then_inc(s_w, 16)

        @block.tensor
        def _(pe):
            for c in range(4):
                for b in range(TB):
                    last = nc.tensor.transpose(PS[:, c, b * P:(b + 1) * P], q_tok[:, b, c * P:(c + 1) * P], ident[:, :])
                last.then_inc(tq, 1)
                for b in range(TB):
                    last = nc.tensor.transpose(PS[:, 4 + c, b * P:(b + 1) * P], k_tok[:, b, c * P:(c + 1) * P], ident[:, :])
                last.then_inc(tq, 1)
            for c in range(4):
                pe.wait_ge(ev3, 2 * c + 1)
                for b in range(CB_):
                    last = nc.tensor.transpose(PS[:, c, b * P:(b + 1) * P], k_tok[:, TB + b, c * P:(c + 1) * P], ident[:, :])
                last.then_inc(tq, 1)
            pe.wait_ge(s_w, 32)
            pe.wait_ge(ev3, 8)
            for h in range(8):
                last = nc.tensor.matmul(PS[:, 4 + h // 2, (h % 2) * 256:(h % 2 + 1) * 256].rearrange("p (b d) -> p b d", d=HD), wsT[:, h, :], vs[:, :, h * HD:(h + 1) * HD], start=True, stop=True, skip_group_check=True)
                last.then_inc(sg, 1)

        @block.scalar
        def _(act):
            for c in range(4):
                act.wait_ge(tq, 2 * c + 1)
                nc.scalar.activation(qT[:, c, :], PS[:, c, :], ACT.Copy, scale=qk_gain[:, 0:1]).then_inc(ev3, 1)
                act.wait_ge(tq, 2 * c + 2)
                nc.scalar.activation(kT[:, c, 0:SEQ], PS[:, 4 + c, :], ACT.Copy).then_inc(ev3, 1)
            for c in range(4):
                act.wait_ge(tq, 8 + c + 1)
                nc.scalar.activation(kT[:, c, SEQ:], PS[:, c, 0:CTX], ACT.Copy).then_inc(ev3, 1)
            act.wait_ge(so, 8)
            for b in range(TB):
                nc.scalar.activation(vs[:, b, :], ug[:, b, :], ACT.Square, accum_out=ssum[:, b:b + 1])
            act.drain()
            nc.scalar.activation(ssum[:, 0:TB], ssum[:, 0:TB], ACT.Sqrt, bias=eps6[:, 0:1], scale=1.0 / HALF).then_inc(sgr, 1)

        @block.vector
        def _(dve):
            for h in range(8):
                dve.wait_ge(sg, h // 2 * 2 + 2)
                u = ug[:, :, h * HD:(h + 1) * HD]
                nc.vector.scalar_tensor_tensor(u, PS[:, 4 + h // 2, (h % 2) * 256:(h % 2 + 1) * 256].rearrange("p (b d) -> p b d", d=HD), bsT[:, h:h + 1], u, ALU.add, ALU.mult).then_inc(so, 1)
            dve.wait_ge(sgr, 1)
            nc.vector.reciprocal(ssum[:, 0:TB], ssum[:, 0:TB])
            dve.drain()
            for b in range(TB):
                nc.vector.tensor_scalar(ug[:, b, :], ug[:, b, :], ssum[:, b:b + 1], None, ALU.mult)

    att = ExitStack()
    NK = SEQ + CTX
    HPI = 2
    UNITS = HPI * 2 * TB
    flat_hi, flat_lo = (t[:, :, :].rearrange("p k n -> p (k n)") for t in (xT_hi, xT_lo))
    q_parts = flat_hi[:, 0:2 * HPI * SEQ].rearrange("p (h n) -> p h n", n=SEQ)
    k_lo = flat_hi[:, 2 * HPI * SEQ:2 * HPI * SEQ + HPI * NK].rearrange("p (c n) -> p c n", n=NK)
    k_hi = flat_lo[:, 0:2 * HPI * NK].rearrange("p (h n) -> p h n", n=NK)
    own = [slice(0, HD), slice(HD, P)]
    spare = k_tok[:, :, :].rearrange("p b n -> p (b n)")
    prob = spare[:, 0:2 * NK].rearrange("p (s n) -> p s n", s=2)
    pT = spare[:, 2 * NK:4 * NK].rearrange("p (s j q) -> p s j q", s=2, q=P)
    mx = sb(att, "row_max1", [P, 2, 2])
    nmx = sb(att, "neg_max1", [P, 2])
    dn = sb(att, "row_sum1", [P, 2, 2])
    rdn = sb(att, "row_inv1", [P, 4])
    ona = q_tok
    a_q, a_st, a_sc, a_mx, a_pr, a_tr, a_pt, a_ptv, a_o, a_oo = [sem("na_" + n) for n in ("hi_parts", "staged", "scores", "max", "probs", "ptr", "pt", "pt_v", "o", "out")]
    s_z, s_zd = sem("zeros_set"), sem("rows_cleared")
    MIN_BLOCKS = 2 * SEQ // P

    def unit(w):
        return w // (2 * TB), w // TB % 2, w % TB, w % 2
    with nc.Block() as block:
        @block.gpsimd
        def _(pool):
            nc.gpsimd.memset(vs[:, 0:2, :], 0.0).then_inc(s_z, 1)

        @block.sync
        def _(sp):
            sp.wait_ge(s_z, 1)
            sp.dma_start(ys[MIN_BLOCKS * P:, :].rearrange("(j p) d -> p j d", p=P),
                         vs[:, 0:2, :].rearrange("p a n -> p (a n)").unsqueeze(1).to_broadcast([P, MAX_BLOCKS - MIN_BLOCKS, D])).then_inc(s_zd, 16)
            sp.wait_ge(s_zd, 16)

        @block.tensor
        def _(pe):
            with pe.Fori(0, 4 // HPI) as c:
                n = c * UNITS

                def scores(w):
                    ch, p, b, s = unit(w)
                    if w % (2 * TB) == 0:
                        pe.wait_ge(a_st, HPI * c + ch + 1)
                    if w >= 2:
                        pe.wait_ge(a_pr, n + w - 1)
                    h, at = 2 * ch + p, slice(b * P, (b + 1) * P)
                    for out, keys in ((PS[:, 2 * s, :], slice(0, SEQ)), (PS[:, 2 * s + 1, 0:CTX], slice(SEQ, NK))):
                        nc.tensor.matmul(out, q_parts[:, h, at], k_hi[:, h, keys], start=True, stop=False)
                        last = nc.tensor.matmul(out, q_parts[own[p], h, at], k_lo[own[p], ch, keys], start=False, stop=True)
                    last.then_inc(a_sc, 1)

                def outputs(w):
                    ch, p, b, s = unit(w)
                    pe.wait_ge(a_pt, n + w + 1)
                    pe.wait_ge(a_ptv, n + w + 1)
                    if w >= 2:
                        pe.wait_ge(a_oo, n + w - 1)
                    for j in range(NK // P):
                        last = nc.tensor.matmul(PS[:, 6 + s, 0:HD], pT[:, s, j, :], v_tok[:, j, ds((2 * (HPI * c + ch) + p) * HD, HD)], start=j == 0, stop=j == NK // P - 1)
                    last.then_inc(a_o, 1)
                scores(0)
                for w in range(UNITS):
                    ch, p, b, s = unit(w)
                    if w + 1 < UNITS:
                        scores(w + 1)
                    pe.wait_ge(a_pr, n + w + 1)
                    if w >= 1:
                        pe.wait_ge(a_pt, n + w)
                        pe.wait_ge(a_ptv, n + w)
                    for j in range(NK // P):
                        last = nc.tensor.transpose(PS[:, 4 + j // 4, (j % 4) * P:(j % 4 + 1) * P], prob[:, s, j * P:(j + 1) * P], ident[:, :])
                    last.then_inc(a_tr, 1)
                    if w >= 1:
                        outputs(w - 1)
                outputs(UNITS - 1)

        @block.scalar
        def _(act):
            with act.Fori(0, 4 // HPI) as c:
                n = c * UNITS

                def exps(w):
                    s = w % 2
                    act.wait_ge(a_mx, n + w + 1)
                    nc.scalar.activation(prob[:, s, SEQ:], PS[:, 2 * s + 1, 0:CTX], ACT.Exp, bias=nmx[:, s:s + 1], accum_out=dn[:, s, 1:2])
                    nc.scalar.activation(prob[:, s, 0:SEQ], prob[:, s, 0:SEQ], ACT.Exp, bias=nmx[:, s:s + 1], accum_out=dn[:, s, 0:1]).then_inc(a_pr, 1)
                def hi_parts(ch):
                    for p in range(2):
                        nc.scalar.activation(q_parts[own[p], 2 * ch + p, :].unsqueeze(1), qT[own[p], ds(HPI * c + ch, 1), :], ACT.Copy)
                        last = nc.scalar.activation(k_hi[own[p], 2 * ch + p, :].unsqueeze(1), kT[own[p], ds(HPI * c + ch, 1), :], ACT.Copy)
                    last.then_inc(a_q, 1)
                hi_parts(0)
                exps(0)
                for w in range(UNITS):
                    if w % (2 * TB) == 2 and w < UNITS - 2 * TB:
                        hi_parts(w // (2 * TB) + 1)
                    if w + 1 < UNITS:
                        exps(w + 1)
                    act.wait_ge(a_tr, n + w + 1)
                    if w >= 2:
                        act.wait_ge(a_o, n + w - 1)
                    nc.scalar.activation(pT[:, w % 2, 0:4, :].rearrange("p j q -> p (j q)"), PS[:, 4, :], ACT.Copy).then_inc(a_pt, 1)

        @block.vector
        def _(dve):
            V = nc.vector
            with dve.Fori(0, 4 // HPI) as c:
                n = c * UNITS
                def lo_parts(ch):
                    for p in range(2):
                        V.tensor_copy(k_hi[own[1 - p], 2 * ch + p, :].unsqueeze(1), kT[own[p], ds(HPI * c + ch, 1), :])
                    dve.wait_ge(a_q, HPI * c + ch + 1)
                    for p in range(2):
                        h, cc = 2 * ch + p, ds(HPI * c + ch, 1)
                        V.tensor_tensor(q_parts[own[1 - p], h, :].unsqueeze(1), qT[own[p], cc, :], q_parts[own[p], h, :].unsqueeze(1).bitcast(f32), ALU.subtract)
                        V.tensor_tensor(k_lo[own[p], ch, :].unsqueeze(1), kT[own[p], cc, :], k_hi[own[p], h, :].unsqueeze(1).bitcast(f32), ALU.subtract)
                    dve.drain().then_inc(a_st, 1)

                def maxima(w):
                    ch, p, b, s = unit(w)
                    dve.wait_ge(a_sc, n + w + 1)
                    if w >= 2:
                        dve.wait_ge(a_tr, n + w - 1)
                    V.tensor_tensor(prob[:, s, 0:SEQ], PS[:, 2 * s, :], nbt[:, ds(2 * (HPI * c + ch) + p, 1), (7 - 2 * b) * GRID:(15 - 2 * b) * GRID].rearrange("p a n -> p (a n)"), ALU.add)
                    V.tensor_reduce(mx[:, s, 1:2], PS[:, 2 * s + 1, 0:CTX], AX.X, ALU.max)
                    dve.drain()
                    V.tensor_reduce(mx[:, s, 0:1], prob[:, s, 0:SEQ], AX.X, ALU.max)
                    dve.drain()
                    V.tensor_scalar(nmx[:, s:s + 1], mx[:, s, 0:1], mx[:, s, 1:2], -1.0, ALU.max, ALU.mult).then_inc(a_mx, 1)

                def norms(w):
                    s = w % 2
                    dve.wait_ge(a_pr, n + w + 1)
                    r = rdn[:, w % 4:w % 4 + 1]
                    V.tensor_tensor(r, dn[:, s, 0:1], dn[:, s, 1:2], ALU.add)
                    dve.drain()
                    V.reciprocal(r, r)
                    dve.drain()

                def finish(w):
                    ch, p, b, s = unit(w)
                    dve.wait_ge(a_o, n + w + 1)
                    V.tensor_scalar(ona[:, b, ds((2 * (HPI * c + ch) + p) * HD, HD)], PS[:, 6 + s, 0:HD], rdn[:, w % 4:w % 4 + 1], None, ALU.mult).then_inc(a_oo, 1)
                lo_parts(0)
                maxima(0)
                for w in range(UNITS):
                    if w % (2 * TB) == 2 and w < UNITS - 2 * TB:
                        lo_parts(w // (2 * TB) + 1)
                    if w + 1 < UNITS:
                        maxima(w + 1)
                    dve.wait_ge(a_tr, n + w + 1)
                    V.tensor_copy(pT[:, w % 2, 4:, :].rearrange("p j q -> p (j q)"), PS[:, 5, 0:NK - SEQ]).then_inc(a_ptv, 1)
                    norms(w)
                    if w >= 1:
                        finish(w - 1)
                finish(UNITS - 1)

    s_sr, tr5, hi5, rd5 = [sem("mrg_" + n) for n in ("root", "tr", "hi", "ready")]
    s_n = sem("mrg_norm")
    with nc.Block() as block:
        @block.sync
        def _(sp):
            for n in range(8):
                half, kp = n // 4, n % 4
                load_tile(sp, Tile(N_WIN + n), A["w_out"][0, kp * 2 * P:(kp + 1) * 2 * P, half * HALF:(half + 1) * HALF].rearrange("(k p) n -> p k n", p=P))

        @block.scalar
        def _(act):
            for b in range(TB):
                nc.scalar.activation(vs[:, b, :], ona[:, b, :], ACT.Square, accum_out=ssum[:, b:b + 1])
            act.drain()
            nc.scalar.activation(ssum[:, 0:TB], ssum[:, 0:TB], ACT.Sqrt, bias=eps6[:, 0:1], scale=1.0 / HALF).then_inc(s_sr, 1)
            split_hi(Tile(N_WIN))
            split_hi(Tile(N_WIN + 1))
            for i in range(KC):
                kc = (i + 4) % KC
                act.wait_ge(tr5, i + 1)
                if i >= 2:
                    act.wait_ge(rd5, i - 1)
                nc.scalar.activation(tmp[:, i % 2, :], PS[:, kc, :], ACT.Copy, scale=out_gT[:, kc:kc + 1])
                nc.scalar.activation(xT_hi[:, kc, :], PS[:, kc, :], ACT.Copy, scale=out_gT[:, kc:kc + 1]).then_inc(hi5, 1)
            for n in range(2, 8):
                split_hi(Tile(N_WIN + n))

        @block.vector
        def _(dve):
            V = nc.vector
            dve.wait_ge(s_sr, 1)
            V.reciprocal(ssum[:, 0:TB], ssum[:, 0:TB])
            dve.drain()
            for b in range(TB):
                V.tensor_scalar(ona[:, b, :], ona[:, b, :], ssum[:, b:b + 1], None, ALU.mult)
            dve.drain().then_inc(s_n, 1)
            split_lo(Tile(N_WIN))
            split_lo(Tile(N_WIN + 1))
            for i in range(KC):
                kc = (i + 4) % KC
                dve.wait_ge(hi5, i + 1)
                V.tensor_tensor(xT_lo[:, kc, :], tmp[:, i % 2, :], xT_hi[:, kc, :].bitcast(f32), ALU.subtract).then_inc(rd5, 1)

            def residual(half):
                for b in range(TB):
                    x = xtok[:, b, half * HALF:(half + 1) * HALF]
                    V.tensor_tensor(tmp[:, b % 2, :], PS[:, 4 * half + b, :], ga_row[:, half * HALF:(half + 1) * HALF], ALU.mult)
                    dve.drain()
                    V.tensor_tensor(x, x, tmp[:, b % 2, :], ALU.add)
                    dve.drain()
            for n in range(2, 8):
                split_lo(Tile(N_WIN + n))
                if n == 5:
                    dve.wait_ge(w_used, N_WIN + 4)
                    residual(0)
            dve.wait_ge(w_used, N_WIN + 8)
            residual(1)

        @block.tensor
        def _(pe):
            for i in range(KC):
                kc = (i + 4) % KC
                src = ug if kc >= 4 else ona
                if i == 4:
                    pe.wait_ge(s_n, 1)
                for b in range(TB):
                    last = nc.tensor.transpose(PS[:, kc, b * P:(b + 1) * P], src[:, b, (kc % 4) * P:(kc % 4 + 1) * P], ident[:, :])
                last.then_inc(tr5, 1)
            pe.wait_ge(rd5, KC)
            for n in range(8):
                half, kp = n // 4, n % 4
                t = Tile(N_WIN + n)
                pe.wait_ge(w_lo, t.plus(1))
                for kk in range(2):
                    kc = 2 * kp + kk
                    for b in range(TB):
                        last = product(PS[:, 4 * half + b, :], XT, (slice(None), kc, slice(b * P, (b + 1) * P)), W, (slice(None), t.slot, slice(kk * HALF, (kk + 1) * HALF)), kc == 0, kc == KC - 1)
                last.then_inc(w_used, 1)
    att.close()
    proj.close()
    table.close()
    keep.close()
    if stop == "attn":
        ctx.close()
        return

    moe = ExitStack()
    hf_hi = xT_hi[:, :, :].rearrange("p k n -> p (k n)").rearrange("p (b d) -> p b d", d=D)
    hf_lo = xT_lo[:, :, :].rearrange("p k n -> p (k n)").rearrange("p (b d) -> p b d", d=D)
    slots = sb(moe, "slots", [P, 2, TB])
    slot_i = sb(moe, "slot_index", [P, 2, TB], mybir.dt.int32)
    gates = sb(moe, "gates", [P, 2, TB])
    iota = sb(moe, "iota_row", [P, P])
    gf_row = sb(moe, "gf_row", [P, D])
    plan = sb(moe, "plan", [P, 32], mybir.dt.int32)
    rt = ExitStack()
    hf = sb(rt, "h_ffn", [P, TB, D])
    shf_row, scf_row = sb(rt, "shf_row", [P, D]), sb(rt, "scf_row", [P, D])
    late_loaded, gf_loaded = sem("late_rows_loaded"), sem("gf_row_loaded")
    hfT = sb(rt, "hfT", [P, KC, SEQ])
    rw = sb(rt, "router_w", [P, KC, 20])
    rb = sb(rt, "router_b", [P, 20])
    lower = sb(rt, "before", [P, P])
    ones = sb(rt, "ones_rt", [P, P])
    first4 = sb(rt, "first4", [P, 4])
    jrow = sb(rt, "block_numbers", [P, 24])
    lg = sb(rt, "logits", [P, TB, 20])
    r4 = sb(rt, "r4", [P, 8, TB, 4])
    r1 = sb(rt, "r1", [P, 12, TB])
    r16 = sb(rt, "r16", [P, 6, TB, 16])
    cnt = sb(rt, "counts", [P, 8, 16])
    bj = sb(rt, "by_block", [P, 24, 16])
    bjf = sb(rt, "by_block_sum", [P, 32])
    q_ld, q_ss, q_n, q_tr, q_ev, q_lg, q_e1, q_e2, q_m, q_rk, q_x, q_hi, q_ev_v = [sem("rt_" + n) for n in ("loaded", "root", "norm", "tr", "evac", "logits", "exp1", "exp2", "mask", "rank", "in", "hi", "evac_v")]
    with nc.Block() as block:
        @block.sync
        def _(sp):
            for k, row in enumerate((shf_row, scf_row)):
                sp.dma_start(row[:, :], late_rows[k, :].partition_broadcast(P)).then_inc(late_loaded, 16)
            for d, n in ((rw[:, :, :], "router_w"), (lower[:, :], "before"), (iota[:, :], "iota"), (first4[:, :], "first4"), (jrow[:, :], "jrow")):
                sp.dma_start(d, A[n]).then_inc(q_ld, 16)
            sp.dma_start(rb[:, 0:4], A["rg_b"][0].partition_broadcast(P)).then_inc(q_ld, 16)
            sp.dma_start(gf_row[:, :], late_rows[2, :].partition_broadcast(P)).then_inc(gf_loaded, 16)
            sp.dma_start(rb[:, 4:20], A["re_b"][0].rearrange("g e -> (g e)").partition_broadcast(P)).then_inc(q_ld, 16)

        @block.gpsimd
        def _(pool):
            nc.gpsimd.memset(ones[:, :], 1.0)
            nc.gpsimd.memset(r16[:, 5, 0, :], 1.0)
            pool.drain().then_inc(q_x, 1)
            pool.wait_ge(q_hi, 1)
            nc.gpsimd.tensor_tensor(hf_lo, hf[:, :, :], hf_hi.bitcast(f32), ALU.subtract)

        @block.scalar
        def _(act):
            for b in range(TB):
                nc.scalar.activation(hfT[:, 2 * b:2 * b + 2, :].rearrange("p a n -> p (a n)"), xtok[:, b, :], ACT.Square, accum_out=ssum[:, b:b + 1])
            act.drain()
            nc.scalar.activation(ssum[:, 0:TB], ssum[:, 0:TB], ACT.Sqrt, bias=eps6[:, 0:1], scale=1.0 / D).then_inc(q_ss, 1)
            for kc in range(0, KC, 2):
                act.wait_ge(q_tr, kc + 1)
                nc.scalar.activation(hfT[:, kc, :], PS[:, kc, :], ACT.Copy).then_inc(q_ev, 1)
            nc.scalar.activation(hf_hi, hf[:, :, :], ACT.Copy).then_inc(q_hi, 1)
            act.wait_ge(q_e1, 1)
            nc.scalar.activation(r4[:, 1, :, :], r4[:, 0, :, :], ACT.Exp).then_inc(q_e2, 1)
            act.wait_ge(q_e1, 2)
            nc.scalar.activation(r1[:, 6, :], r1[:, 5, :], ACT.Exp).then_inc(q_e2, 1)

        @block.tensor
        def _(pe):
            for b in range(TB):
                pe.wait_ge(q_n, b + 1)
                for kc in range(KC):
                    last = nc.tensor.transpose(PS[:, kc, b * P:(b + 1) * P], hf[:, b, kc * P:(kc + 1) * P], ident[:, :])
                    if b == TB - 1:
                        last.then_inc(q_tr, 1)
            pe.wait_ge(q_ev, KC // 2)
            pe.wait_ge(q_ev_v, KC // 2)
            pe.wait_ge(q_ld, 112)
            for b in range(TB):
                for kc in range(KC):
                    last = nc.tensor.matmul(PS[:, b, 0:20], hfT[:, kc, b * P:(b + 1) * P], rw[:, kc, :], start=kc == 0, stop=kc == KC - 1)
            last.then_inc(q_lg, 1)
            pe.wait_ge(q_m, 1)
            for b in range(TB):
                for a in range(b):
                    nc.tensor.matmul(PS[:, 4 + b, 0:16], ones[:, :], r16[:, 2, a, :], start=a == 0, stop=False)
                nc.tensor.matmul(PS[:, 4 + b, 0:16], lower[:, :], r16[:, 2, b, :], start=b == 0, stop=True)
            for b in range(TB):
                last = nc.tensor.matmul(PS[:, 0, 0:16], ones[:, :], r16[:, 2, b, :], start=b == 0, stop=b == TB - 1)
            last.then_inc(q_rk, 1)

        @block.vector
        def _(dve):
            V = nc.vector
            TT, TS = V.tensor_tensor, V.tensor_scalar
            dr = dve.drain
            dve.wait_ge(q_ss, 1)
            V.reciprocal(ssum[:, 0:TB], ssum[:, 0:TB])
            dr()
            dve.wait_ge(late_loaded, 32)
            for b in range(TB):
                V.scalar_tensor_tensor(hf[:, b, :], xtok[:, b, :], ssum[:, b:b + 1], scf_row[:, :], ALU.mult, ALU.mult)
            dr()
            for b in range(TB):
                TT(hf[:, b, :], hf[:, b, :], shf_row[:, :], ALU.add).then_inc(q_n, 1)
            for kc in range(1, KC, 2):
                dve.wait_ge(q_tr, kc + 1)
                V.tensor_copy(hfT[:, kc, :], PS[:, kc, :]).then_inc(q_ev_v, 1)
            dve.wait_ge(q_x, 1)
            dve.wait_ge(q_ld, 112)
            dve.wait_ge(q_lg, 1)
            TT(lg[:, :, :], PS[:, 0:TB, 0:20], rb[:, :].unsqueeze(1).to_broadcast([P, TB, 20]), ALU.add)
            dr()
            b4 = lambda a: a.unsqueeze(2).to_broadcast([P, TB, 4])

            def first_max(src, top, hot, t):
                V.tensor_reduce(top, src, AX.X, ALU.max)
                dr()
                TT(t, src, b4(top), ALU.is_equal)
                dr()
                TT(t, t, first4[:, :].unsqueeze(1).to_broadcast([P, TB, 4]), ALU.mult)
                dr()
                V.tensor_reduce(r1[:, 11, :], t, AX.X, ALU.max)
                dr()
                TT(hot, t, b4(r1[:, 11, :]), ALU.is_equal)
                dr()
            first_max(lg[:, :, 0:4], r1[:, 0, :], r4[:, 2, :, :], r4[:, 7, :, :])
            TT(r4[:, 0, :, :], lg[:, :, 0:4], b4(r1[:, 0, :]), ALU.subtract)
            dr().then_inc(q_e1, 1)
            for g in range(GROUPS):
                hot_g = r4[:, 2, :, g:g + 1].to_broadcast([P, TB, 4])
                TT(r4[:, 3 if g == 0 else 7, :, :], lg[:, :, 4 + 4 * g:8 + 4 * g], hot_g, ALU.mult)
                dr()
                if g:
                    TT(r4[:, 3, :, :], r4[:, 3, :, :], r4[:, 7, :, :], ALU.add)
                    dr()
            first_max(r4[:, 3, :, :], r1[:, 1, :], r4[:, 4, :, :], r4[:, 7, :, :])
            TS(r4[:, 5, :, :], r4[:, 4, :, :], NEG, None, ALU.mult)
            dr()
            TT(r4[:, 5, :, :], r4[:, 5, :, :], r4[:, 3, :, :], ALU.add)
            dr()
            first_max(r4[:, 5, :, :], r1[:, 2, :], r4[:, 6, :, :], r4[:, 7, :, :])
            TT(r1[:, 5, :], r1[:, 2, :], r1[:, 1, :], ALU.subtract)
            dr().then_inc(q_e1, 1)
            for k, hot_e in ((0, 4), (1, 6)):
                for g in range(GROUPS):
                    TT(r16[:, k, :, 4 * g:4 * g + 4], r4[:, hot_e, :, :], r4[:, 2, :, g:g + 1].to_broadcast([P, TB, 4]), ALU.mult)
            dr()
            TT(r16[:, 2, :, :], r16[:, 0, :, :], r16[:, 1, :, :], ALU.add)
            dr().then_inc(q_m, 1)
            dve.wait_ge(q_e2, 2)
            V.tensor_reduce(r1[:, 7, :], r4[:, 1, :, :], AX.X, ALU.add)
            TS(r1[:, 8, :], r1[:, 6, :], 1.0, None, ALU.add)
            dr()
            TT(r1[:, 8, :], r1[:, 8, :], r1[:, 7, :], ALU.mult)
            dr()
            V.reciprocal(gates[:, 0, :], r1[:, 8, :])
            dr()
            TT(gates[:, 1, :], gates[:, 0, :], r1[:, 6, :], ALU.mult)
            dve.wait_ge(q_rk, 1)
            V.tensor_copy(cnt[:, 0, :], PS[:, 0, 0:16])
            dr()
            for k in range(4):
                TS(cnt[:, 1 + k, :], cnt[:, 0, :], float(P * k), None, ALU.is_gt)
            dr()
            for k in range(1, 4):
                TT(cnt[:, 1, :], cnt[:, 1, :], cnt[:, 1 + k, :], ALU.add)
                dr()
            V.tensor_tensor_scan(cnt[:, 5, :], r16[:, 5, 0, :], cnt[:, 1, :], 0.0, ALU.mult, ALU.add)
            dr()
            TT(cnt[:, 6, :], cnt[:, 5, :], cnt[:, 1, :], ALU.subtract)
            dr()
            TS(cnt[:, 6, :], cnt[:, 6, :], float(P), None, ALU.mult)
            dr()
            TT(r16[:, 3, :, :], PS[:, 4:8, 0:16], cnt[:, 6, :].unsqueeze(1).to_broadcast([P, TB, 16]), ALU.add)
            dr()
            for k in range(2):
                TT(r16[:, 4, :, :], r16[:, 3, :, :], r16[:, k, :, :], ALU.mult)
                dr()
                V.tensor_reduce(slots[:, k, :], r16[:, 4, :, :], AX.X, ALU.add)
                dr()
            V.tensor_copy(slot_i[:, :, :], slots[:, :, :])
            TT(bj[:, :, :], cnt[:, 5, :].unsqueeze(1).to_broadcast([P, 24, 16]), jrow[:, :].unsqueeze(2).to_broadcast([P, 24, 16]), ALU.is_le)
            dr()
            V.tensor_reduce(bjf[:, 0:24], bj[:, :, :], AX.X, ALU.add)
            dr()
            TS(bjf[:, 0:24], bjf[:, 0:24], float(EXPERTS - 1), None, ALU.min)
            V.tensor_copy(bjf[:, 24:25], cnt[:, 5, 15:16])
            dr()
            V.tensor_copy(plan[:, 0:25], bjf[:, 0:25])
            dve.wait_ge(gf_loaded, 16)
    rt.close()

    ex = ExitStack()
    ER, NT = 6, 12
    KE = D_EXP // P
    e_raw = sb(ex, "expert_w_raw", [P, ER, D])
    e_whi = sb(ex, "expert_w_hi", [P, ER, D], f32r)
    e_wlo = sb(ex, "expert_w_lo", [P, ER, D], f32r)
    pick = sb(ex, "pick", [P, TB, P], f32r)
    xs_hi = sb(ex, "rows_T_hi", [P, KC, P], f32r)
    xs_lo = sb(ex, "rows_T_lo", [P, KC, P], f32r)
    sl = sb(ex, "silu_e", [P, D_EXP])
    hid = sb(ex, "hidden_e", [P, D_EXP])
    hT_hi = sb(ex, "hidden_T_hi", [P, KE, P], f32r)
    hT_lo = sb(ex, "hidden_T_lo", [P, KE, P], f32r)
    yb = sb(ex, "y_buf", [P, D])
    EW, XS, HT = (e_whi, e_wlo), (xs_hi, xs_lo), (hT_hi, hT_lo)
    e_ld = [sem(f"ex_loaded{k}") for k in range(ER)]
    e_hi, e_ld_v, e_ld_p, e_used, e_pk, e_ga, e_gb, e_xh, e_xl, e_sl, e_hd, e_tr, e_hh, e_hl, e_y, e_st, e_all = [
        sem("ex_" + n) for n in ("hi", "lo_vector", "lo_gpsimd", "used", "pick", "gather_hi", "gather_lo", "rows_hi", "rows_lo", "silu", "hid", "tr",
                                 "hT_hi", "hT_lo", "y", "store", "all_stored")]
    V_TILES = [n for n in range(NT) if n % 3 != 2]
    P_TILES = [n for n in range(NT) if n % 3 == 2]

    def wait_lo(engine, j, n):
        if n in V_TILES:
            engine.wait_ge(e_ld_v, len(V_TILES) * j + V_TILES.index(n) + 1)
        else:
            engine.wait_ge(e_ld_p, len(P_TILES) * j + P_TILES.index(n) + 1)

    def expert_lo(wait, op, j, n, done):
        wait(e_hi, NT * j + n + 1)
        op(e_wlo[:, n % ER, :], e_raw[:, n % ER, :], e_whi[:, n % ER, :].bitcast(f32), ALU.subtract).then_inc(done, 1)

    with nc.Block() as block:
        @block.sync
        def _(sp):
            def turn(j, first):
                e = sp.value_load(plan[0:1, j:j + 1] if first else plan[0:1, ds(j, 1)], min_val=0, max_val=EXPERTS - 1)
                for n in range(NT):
                    if n >= ER:
                        wait_lo(sp, j, n - ER)
                    elif not first:
                        wait_lo(sp, j - 1, n + ER)
                    if n < 8:
                        src = A["w1" if n < 4 else "w3"][0, ds(e, 1), n % 4 * 2 * P:(n % 4 + 1) * 2 * P, :].rearrange("a (k p) n -> p (a k) n", p=P)
                    else:
                        src = A["w2"][0, ds(e, 1), (n - 8) * P:(n - 7) * P, :].rearrange("a (k p) n -> p (a k) n", p=P)
                    sp.dma_start(e_raw[:, n % ER, :].rearrange("p (a n) -> p a n", n=src.shape[-1]), src).then_inc(e_ld[n % ER], 16)
            n_blocks = sp.value_load(plan[0:1, 24:25], min_val=8, max_val=MAX_BLOCKS)
            turn(0, True)
            with sp.Fori(1, n_blocks) as j:
                turn(j, False)

        @block.gpsimd
        def _(pool):
            n_blocks = pool.value_load(plan[0:1, 24:25], min_val=8, max_val=MAX_BLOCKS)
            with pool.Fori(0, n_blocks) as j:
                for n in P_TILES:
                    expert_lo(pool.wait_ge, nc.gpsimd.tensor_tensor, j, n, e_ld_p)

        @block.tensor
        def _(pe):
            def gather(part, bank, done):
                for kc in range(KC):
                    for b in range(TB):
                        last = nc.tensor.matmul(PS[:, bank + kc // 4, (kc % 4) * P:(kc % 4 + 1) * P], part[:, b, kc * P:(kc + 1) * P], pick[:, b, :],
                                                start=b == 0, stop=b == TB - 1, skip_group_check=True)
                last.then_inc(done, 1)

            def turn(j, first):
                pe.wait_ge(e_xh, j + 1)
                pe.wait_ge(e_xl, j + 1)
                for n in range(8):
                    wait_lo(pe, j, n)
                    for kk in range(2):
                        kc = n % 4 * 2 + kk
                        last = product(PS[:, 2 + n // 4, :], XS, (slice(None), kc), EW, (slice(None), n % ER, slice(kk * D_EXP, (kk + 1) * D_EXP)), kc == 0, kc == KC - 1)
                    last.then_inc(e_used, 1)
                pe.wait_ge(e_pk, j + 2)
                gather(hf_hi, 0, e_ga)
                pe.wait_ge(e_hd, j + 1)
                for k in range(KE):
                    last = nc.tensor.transpose(PS[:, 2, k * P:(k + 1) * P], hid[:, k * P:(k + 1) * P], ident[:, :])
                last.then_inc(e_tr, 1)
                gather(hf_lo, 4, e_gb)
                pe.wait_ge(e_hh, j + 1)
                pe.wait_ge(e_hl, j + 1)
                if not first:
                    pe.wait_ge(e_y, j)
                for k in range(KE):
                    wait_lo(pe, j, 8 + k)
                    for h in range(2):
                        last = product(PS[:, 6 + h, :], HT, (slice(None), k), EW, (slice(None), (8 + k) % ER, slice(h * HALF, (h + 1) * HALF)), k == 0, k == KE - 1)
                    last.then_inc(e_used, 1)
            n_blocks = pe.value_load(plan[0:1, 24:25], min_val=8, max_val=MAX_BLOCKS)
            pe.wait_ge(e_pk, 1)
            gather(hf_hi, 0, e_ga)
            gather(hf_lo, 4, e_gb)
            turn(0, True)
            with pe.Fori(1, n_blocks) as j:
                turn(j, False)

        @block.scalar
        def _(act):
            def store(n):
                act.wait_ge(e_y, n)
                act.dma_start(ys[ds(n * P - P, P), :], yb[:, :]).then_inc(e_st, 16)

            def hi(j, n, first):
                act.wait_ge(e_ld[n % ER], 32 * j + 16 * (n // ER) + 16)
                if n >= ER or not first:
                    act.wait_ge(e_used, NT * j + n - ER + 1)
                nc.scalar.activation(e_whi[:, n % ER, :], e_raw[:, n % ER, :], ACT.Copy).then_inc(e_hi, 1)

            def rows_hi(n):
                act.wait_ge(e_ga, n)
                nc.scalar.activation(xs_hi[:, :, :].rearrange("p k n -> p (k n)"), PS[:, 0:2, :].rearrange("p a n -> p (a n)"), ACT.Copy).then_inc(e_xh, 1)

            def turn(j, first):
                for n in range(ER):
                    hi(j, n, first)
                if not first:
                    store(j)
                for n in range(ER, ER + 3):
                    hi(j, n, first)
                act.wait_ge(e_used, NT * j + 4)
                nc.scalar.activation(sl[:, :], PS[:, 2, :], ACT.Silu).then_inc(e_sl, 1)
                for n in range(ER + 3, NT):
                    hi(j, n, first)
                rows_hi(j + 2)
                act.wait_ge(e_tr, j + 1)
                nc.scalar.activation(hT_hi[:, :, :].rearrange("p k n -> p (k n)"), PS[:, 2, :], ACT.Copy).then_inc(e_hh, 1)

            n_blocks = act.value_load(plan[0:1, 24:25], min_val=8, max_val=MAX_BLOCKS)
            rows_hi(1)
            turn(0, True)
            with act.Fori(1, n_blocks) as j:
                turn(j, False)
            store(n_blocks)
            act.wait_ge(e_st, 16 * n_blocks + 16)
            act.sem_inc(e_all, 1)

        @block.vector
        def _(dve):
            V = nc.vector

            def picks():
                for b in range(TB):
                    V.tensor_scalar(pick[:, b, :], iota[:, :], slots[:, 0, b:b + 1], None, ALU.is_equal)
                dve.drain()
                for b in range(TB):
                    V.scalar_tensor_tensor(pick[:, b, :], iota[:, :], slots[:, 1, b:b + 1], pick[:, b, :].bitcast(f32), ALU.is_equal, ALU.add)
                dve.drain()
                V.tensor_scalar(slots[:, :, :], slots[:, :, :], float(-P), None, ALU.add)
                dve.drain().then_inc(e_pk, 1)

            def rows_lo(n):
                dve.wait_ge(e_gb, n)
                V.tensor_copy(xs_lo[:, :, :].rearrange("p k n -> p (k n)"), PS[:, 4:6, :].rearrange("p a n -> p (a n)")).then_inc(e_xl, 1)

            def gated(n):
                dve.wait_ge(e_used, NT * n)
                dve.wait_ge(e_st, 16 * n)
                V.tensor_tensor(yb[:, :], PS[:, 6:8, :].rearrange("p a n -> p (a n)"), gf_row[:, :], ALU.mult).then_inc(e_y, 1)

            def turn(j, first):
                for n in V_TILES[:4]:
                    expert_lo(dve.wait_ge, V.tensor_tensor, j, n, e_ld_v)
                if not first:
                    gated(j)
                picks()
                for n in V_TILES[4:7]:
                    expert_lo(dve.wait_ge, V.tensor_tensor, j, n, e_ld_v)
                dve.wait_ge(e_sl, j + 1)
                dve.wait_ge(e_used, NT * j + 8)
                V.tensor_tensor(hid[:, :], sl[:, :], PS[:, 3, :], ALU.mult).then_inc(e_hd, 1)
                expert_lo(dve.wait_ge, V.tensor_tensor, j, V_TILES[7], e_ld_v)
                dve.wait_ge(e_hh, j + 1)
                V.tensor_tensor(hT_lo[:, :, :].rearrange("p k n -> p (k n)"), PS[:, 2, :], hT_hi[:, :, :].rearrange("p k n -> p (k n)").bitcast(f32), ALU.subtract).then_inc(e_hl, 1)
                rows_lo(j + 2)

            V.sem_inc(e_st, 16)
            n_blocks = dve.value_load(plan[0:1, 24:25], min_val=8, max_val=MAX_BLOCKS)
            picks()
            rows_lo(1)
            turn(0, True)
            with dve.Fori(1, n_blocks) as j:
                turn(j, False)
            gated(n_blocks)
    ex.close()

    fn = ExitStack()
    yA = sb(fn, "y_first", [P, TB, D])
    yB = sb(fn, "y_second", [P, TB, D])
    s_ga = [sem(f"y_rows{b}") for b in range(TB)]
    S.distance_rows = DistanceRows(nc, lambda n, shape: sb(fn, n, shape), sem, A, PS)
    with nc.Block() as block:
        @block.gpsimd
        def _(pool):
            pool.wait_ge(e_all, 1)
            for b in range(TB):
                for k, d in ((0, yA), (1, yB)):
                    nc.gpsimd.indirect_dma_start(out=d[:, b, :], out_offset=None, in_=ys[:, :], in_offset=bass.IndirectOffsetOnAxis(ap=slot_i[:, k, b:b + 1], axis=0)).then_inc(s_ga[b], 16)

        @block.sync
        def _(sp):
            S.distance_rows.sync(sp)

        @block.tensor
        def _(pe):
            S.distance_rows.tensor(pe)

        @block.vector
        def _(dve):
            V = nc.vector
            S.distance_rows.vector(dve)
            for b in range(TB):
                dve.wait_ge(s_ga[b], 32)
                V.scalar_tensor_tensor(xtok[:, b, :], yA[:, b, :], gates[:, 0, b:b + 1], xtok[:, b, :], ALU.mult, ALU.add)
                dve.drain()
                V.scalar_tensor_tensor(xtok[:, b, :], yB[:, b, :], gates[:, 1, b:b + 1], xtok[:, b, :], ALU.mult, ALU.add)
    fn.close()
    moe.close()
    ctx.close()
    nc.clear_and_free_semaphores(own_sems)
    nc.all_engine_barrier()


def second_block(nc, ctx, T0, S, A):
    xtok, xT_hi, xT_lo, raw, whi, wlo, ident, PS = S.xtok, S.xT_hi, S.xT_lo, S.raw, S.whi, S.wlo, S.ident, S.PS
    w_loaded, w_hi, w_lo, w_used = S.w_loaded, S.w_hi, S.w_lo, S.w_used

    def sem(n):
        return ctx.enter_context(nc.semaphore(n))

    def sb(c, n, shape, dt=f32):
        return c.enter_context(nc.sbuf_tensor(n, shape, dt))

    def load_tile(sp, t, src):
        sp.wait_ge(w_lo, t.plus(-1))
        sp.dma_start(raw[:, t.slot, :].rearrange("p (a n) -> p a n", n=src.shape[-1]), src).then_inc(w_loaded[t.slot], 16)

    def split_hi(t):
        nc.scalar.wait_ge(w_loaded[t.slot], t.loads())
        nc.scalar.wait_ge(w_used, t.plus(-1))
        nc.scalar.activation(whi[:, t.slot, :], raw[:, t.slot, :], ACT.Copy).then_inc(w_hi, 1)

    def split_lo(t):
        nc.vector.wait_ge(w_hi, t.plus(1))
        nc.vector.tensor_tensor(wlo[:, t.slot, :], raw[:, t.slot, :], whi[:, t.slot, :].bitcast(f32), ALU.subtract).then_inc(w_lo, 1)

    def product(out, a, a_at, b, b_at, first, last):
        nc.tensor.matmul(out, a[0][a_at], b[0][b_at], start=first, stop=False)
        nc.tensor.matmul(out, a[0][a_at], b[1][b_at], start=False, stop=False)
        return nc.tensor.matmul(out, a[1][a_at], b[0][b_at], start=False, stop=last)

    W = (whi, wlo)
    XT = (xT_hi, xT_lo)

    lnT = sb(ctx, "lnT", [P, 3, 2, KC])
    g_row = sb(ctx, "ln_g_row", [P, D])
    b_row = sb(ctx, "ln_b_row", [P, D])
    stats = sb(ctx, "ln_stats", [P, TB, 2, 6])
    meanvar = sb(ctx, "ln_meanvar", [P, TB, 2])
    rstd = sb(ctx, "ln_rstd", [P, TB])
    shift = sb(ctx, "ln_shift", [P, TB])
    eps = sb(ctx, "ln_eps", [P, 1])
    tmp = sb(ctx, "evac_tmp", [P, 2, SEQ])

    def half_sums(bank, h):
        def of(b):
            at = xtok[:, b, h * HALF:(h + 1) * HALF]
            nc.vector.scalar_tensor_tensor(at, at, ALPHA, PS[:, bank + b, :], ALU.mult, ALU.add)
        return of

    def half_stats(b, h):
        nc.vector.bn_stats(stats[:, b, h, :], xtok[:, b, h * HALF:(h + 1) * HALF])

    def layer_norm_dve(dve, bank, rows_done, all_done, f, l, finish):
        sums = half_sums(bank, 1)
        for b in range(TB):
            if b < TB - 1:
                dve.wait_ge(f[rows_done], (TB - 1) * l + b + 1)
            else:
                all_done()
            sums(b)
            dve.drain()
            half_stats(b, 1)
            dve.drain()
            nc.vector.bn_aggr(meanvar[:, b, :], stats[:, b, :, :]).then_inc(f["var_ready"], 1)
            pair = {2: 0, 3: 1}.get(b)
            if pair is None:
                continue
            dve.wait_ge(f["rstd_ready"], TB * l + 2 * pair + 2)
            nc.vector.reciprocal(rstd[:, 2 * pair:2 * pair + 2], rstd[:, 2 * pair:2 * pair + 2])
            dve.drain()
            nc.vector.scalar_tensor_tensor(shift[:, 2 * pair:2 * pair + 2], meanvar[:, 2 * pair:2 * pair + 2, 0], -1.0, rstd[:, 2 * pair:2 * pair + 2], ALU.mult, ALU.mult).then_inc(f["shift_ready"], 1)
            dve.drain()
            finish(2 * pair)

    def layer_norm_act(act, f, l, finish):
        for pair in range(2):
            for b in (2 * pair, 2 * pair + 1):
                act.wait_ge(f["var_ready"], TB * l + b + 1)
                nc.scalar.activation(rstd[:, b:b + 1], meanvar[:, b, 1:2], ACT.Sqrt, bias=eps[:, 0:1]).then_inc(f["rstd_ready"], 1)
            act.wait_ge(f["shift_ready"], 2 * l + pair + 1)
            finish(2 * pair + 1)

    def normalise_dve(b):
        nc.vector.tensor_scalar(xtok[:, b, :], xtok[:, b, :], rstd[:, b:b + 1], shift[:, b:b + 1], ALU.mult, ALU.add)

    def normalise_affine_dve(b):
        nc.vector.scalar_tensor_tensor(xtok[:, b, :], xtok[:, b, :], meanvar[:, b, 0:1], g_row[:, :], ALU.subtract, ALU.mult)
        nc.vector.drain()
        nc.vector.scalar_tensor_tensor(xtok[:, b, :], xtok[:, b, :], rstd[:, b:b + 1], b_row[:, :], ALU.mult, ALU.add)

    def affine(engine, b):
        engine.tensor_tensor(xtok[:, b, :], xtok[:, b, :], g_row[:, :], ALU.mult)
        engine.drain()
        engine.tensor_tensor(xtok[:, b, :], xtok[:, b, :], b_row[:, :], ALU.add)

    def normalise_act(b):
        return nc.scalar.activation(xtok[:, b, :], xtok[:, b, :], ACT.Identity, bias=shift[:, b:b + 1], scale=rstd[:, b:b + 1])

    def transposes(tr_done):
        for b in range(TB):
            for kc in range(KC):
                last = nc.tensor.transpose(PS[:, kc, b * P:(b + 1) * P], xtok[:, b, kc * P:(kc + 1) * P], ident[:, :])
                if b == TB - 1:
                    last.then_inc(tr_done, 1)

    F = {n: sem(f"ffn_{n}") for n in (
        "tr_done", "hi_ready", "xT_ready", "silu_done", "sum_done", "h_hi_ready", "h_ready", "rows_done", "var_ready", "rstd_ready", "shift_ready")}
    ln_loaded = sem("ln_loaded")
    rows_loaded = sem("rows_loaded")
    odd_normalised = sem("odd_normalised")
    residual_ready = sem("residual_ready")

    with nc.Block() as block:
        @block.gpsimd
        def _(pool):
            nc.gpsimd.memset(eps[:, :], LN_EPS)

    def up_src(l, j, g, i):
        w = (A["ffn_w_gate_2"], A["ffn_w_up_2"])[g]
        return w[l, j, :, ds(i * P, P)].rearrange("(k p) n -> p k n", p=P)

    def mix_src(l, n):
        return A["w_in_2"][l, :, n * P:(n + 1) * P].rearrange("(k p) n -> p k n", p=P)

    MOUT_ORDER = [2, 3, 0, 1]

    def mout_src(l, n):
        half, kp = n // 4, MOUT_ORDER[n % 4]
        return A["w_out_2"][l, kp * 2 * P:(kp + 1) * 2 * P, half * HALF:(half + 1) * HALF].rearrange("(k p) n -> p k n", p=P)

    class Ahead:

        def __init__(self, tiles, src):
            self.tiles, self.src = tiles, src

        def load(self, sp):
            for t, src in zip(self.tiles, self.src):
                load_tile(sp, t, src)

        def hi(self, i):
            if self.tiles:
                split_hi(self.tiles[i])

        def lo(self, i):
            if self.tiles:
                split_lo(self.tiles[i])

    def ffn(j, l, T, T_next):
        ahead = Ahead([T_next(0), T_next(1)], [mix_src(l, 0), mix_src(l, 1)]) if j == 0 else Ahead([], [])
        f, v = F, 2 * l + j
        wd = A["ffn_w_down_2"]
        with ExitStack() as c:
            h_hi = sb(c, f"h_hi{j}", [P, FC, SEQ], f32r)
            h_lo = sb(c, f"h_lo{j}", [P, FC, SEQ], f32r)
            silu = sb(c, f"silu{j}", [P, 2, SEQ])
            hsum = sb(c, f"hsum{j}", [P, 2, SEQ])
            H = (h_hi, h_lo)

            with nc.Block() as block:
                @block.sync
                def _(sp):
                    if j == 0:
                        load_tile(sp, T(0), up_src(l, 0, 0, 0))
                        load_tile(sp, T(1), up_src(l, 0, 1, 0))
                        sp.dma_start(lnT[:, :, :, :], A["lnT_2"][l]).then_inc(ln_loaded, 16)
                    else:
                        sp.dma_start(g_row[:, :], A["ln_g_2"][l, 1, :].partition_broadcast(P)).then_inc(rows_loaded, 16)
                        sp.dma_start(b_row[:, :], A["ln_b_2"][l, 1, :].partition_broadcast(P)).then_inc(rows_loaded, 16)
                    with sp.Fori(1, FC) as i:
                        load_tile(sp, T(0, i), up_src(l, j, 0, i))
                        load_tile(sp, T(1, i), up_src(l, j, 1, i))
                    for n in range(N_DOWN):
                        half, kp = n // (FC // 2), n % (FC // 2)
                        load_tile(sp, T(N_UP + n), wd[l, j, kp * 2 * P:(kp + 1) * 2 * P, half * HALF:(half + 1) * HALF].rearrange("(k p) n -> p k n", p=P))
                    ahead.load(sp)
                    if j == 1:
                        sp.wait_ge(residual_ready, 2 * l + 2)
                        sp.dma_start(g_row[:, :], A["ln_g_2"][l, 2, :].partition_broadcast(P)).then_inc(rows_loaded, 16)
                        sp.dma_start(b_row[:, :], A["ln_b_2"][l, 2, :].partition_broadcast(P)).then_inc(rows_loaded, 16)

                @block.scalar
                def _(act):
                    if j == 0:
                        split_hi(T(0))
                    split_hi(T(1))
                    if j == 1:
                        act.wait_ge(ln_loaded, 16 * (l + 1))
                    for kc in range(KC):
                        act.wait_ge(f["tr_done"], v * KC + kc + 1)
                        if j == 0:
                            nc.scalar.activation(xT_hi[:, kc, :], PS[:, kc, :], ACT.Copy).then_inc(f["hi_ready"], 1)
                        else:
                            g, b = lnT[:, 1, 0, kc:kc + 1], lnT[:, 1, 1, kc:kc + 1]
                            if kc >= 2:
                                act.wait_ge(f["xT_ready"], v * KC + kc - 1)
                            nc.scalar.activation(tmp[:, kc % 2, :], PS[:, kc, :], ACT.Identity, bias=b, scale=g)
                            nc.scalar.activation(xT_hi[:, kc, :], PS[:, kc, :], ACT.Identity, bias=b, scale=g).then_inc(f["hi_ready"], 1)
                    with act.Fori(0, FC // 2) as ii:
                        for c2 in range(2):
                            i = 2 * ii + c2
                            split_hi(T(2, i))
                            split_hi(T(3, i))
                            act.wait_ge(w_used, T(0, i).plus(1))
                            act.wait_ge(f["sum_done"], v * (FC + 2) + i + 1)
                            nc.scalar.activation(silu[:, c2, :], PS[:, 2 * c2, :], ACT.Silu).then_inc(f["silu_done"], 1)
                            act.wait_ge(f["sum_done"], v * (FC + 2) + i + 3)
                            nc.scalar.activation(h_hi[:, ds(i, 1), :], hsum[:, c2:c2 + 1, :], ACT.Copy).then_inc(f["h_hi_ready"], 1)
                    for n in range(2, N_DOWN):
                        split_hi(T(N_UP + n))
                    ahead.hi(0)
                    if j == 0:
                        layer_norm_act(act, f, v, normalise_act)
                    else:
                        layer_norm_act(act, f, v, lambda b: normalise_act(b).then_inc(odd_normalised, 1))

                @block.vector
                def _(dve):
                    nc.vector.sem_inc(f["sum_done"], 2)
                    if j == 0:
                        split_lo(T(0))
                    split_lo(T(1))
                    for kc in range(KC):
                        dve.wait_ge(f["hi_ready"], v * KC + kc + 1)
                        src = PS[:, kc, :] if j == 0 else tmp[:, kc % 2, :]
                        nc.vector.tensor_tensor(xT_lo[:, kc, :], src, xT_hi[:, kc, :].bitcast(f32), ALU.subtract).then_inc(f["xT_ready"], 1)
                    with dve.Fori(0, FC // 2) as ii:
                        for c2 in range(2):
                            i = 2 * ii + c2
                            split_lo(T(2, i))
                            split_lo(T(3, i))
                            dve.wait_ge(f["silu_done"], v * FC + i + 1)
                            dve.wait_ge(w_used, T(1, i).plus(1))
                            nc.vector.scalar_tensor_tensor(hsum[:, c2, :], silu[:, c2, :], 0.5, PS[:, 2 * c2 + 1, :], ALU.mult, ALU.mult).then_inc(f["sum_done"], 1)
                            dve.wait_ge(f["h_hi_ready"], v * FC + i + 1)
                            nc.vector.tensor_tensor(h_lo[:, ds(i, 1), :], hsum[:, c2:c2 + 1, :], h_hi[:, ds(i, 1), :].bitcast(f32), ALU.subtract).then_inc(f["h_ready"], 1)
                    for n in range(2, FC // 2 + 3):
                        split_lo(T(N_UP + n))
                    dve.wait_ge(w_used, T(N_UP + FC // 2 - 1).plus(1))
                    if j == 1:
                        dve.wait_ge(residual_ready, 2 * l + 2)
                    sums = half_sums(4, 0)
                    for b in range(TB):
                        sums(b)
                    dve.drain()
                    for n in range(FC // 2 + 3, N_DOWN):
                        split_lo(T(N_UP + n))
                        if n < FC // 2 + 3 + TB:
                            half_stats(n - FC // 2 - 3, 0)
                    ahead.lo(0)
                    if j == 0:
                        finish = normalise_dve
                    else:
                        dve.wait_ge(rows_loaded, 96 * (l + 1))
                        finish = normalise_affine_dve
                    layer_norm_dve(dve, 0, "rows_done", lambda: dve.wait_ge(w_used, T(N_FFN - 1).plus(1)), f, v, finish)
                    if j == 1:
                        dve.wait_ge(odd_normalised, 2 * l + 2)
                        affine(nc.vector, TB - 1)

                @block.gpsimd
                def _(pool):
                    if j == 1:
                        residual_affine(pool, 3 * l + 2, f["tr_done"], KC * (v + 1))
                        pool.wait_ge(rows_loaded, 96 * (l + 1))
                        pool.wait_ge(odd_normalised, 2 * l + 1)
                        affine(nc.gpsimd, 1)

                @block.tensor
                def _(pe):
                    transposes(f["tr_done"])
                    with pe.Fori(0, FC // 2) as ii:
                        for c2 in range(2):
                            i = 2 * ii + c2
                            for g in range(2):
                                t = T(g, i)
                                pe.wait_ge(w_lo, t.plus(1))
                                pe.wait_ge(f["sum_done"], v * (FC + 2) + i + 1)
                                for kc in range(KC):
                                    if c2 == 0 and g == 0:
                                        pe.wait_ge(f["xT_ready"], v * KC + kc + 1)
                                    last = product(PS[:, 2 * c2 + g, :], W, (slice(None), t.slot, slice(kc * P, (kc + 1) * P)), XT, (slice(None), kc), kc == 0, kc == KC - 1)
                                last.then_inc(w_used, 1)
                    pe.wait_ge(f["sum_done"], v * (FC + 2) + FC + 2)
                    for n in range(N_DOWN):
                        half, kp = n // (FC // 2), n % (FC // 2)
                        t = T(N_UP + n)
                        pe.wait_ge(w_lo, t.plus(1))
                        if half == 0:
                            pe.wait_ge(f["h_ready"], v * FC + 2 * kp + 1)
                        order = [(kk, b) for kk in range(2) for b in range(TB)]
                        if n == N_DOWN - 1:
                            order = [(kk, b) for b in range(TB) for kk in range(2)]
                        for kk, b in order:
                            kc = 2 * kp + kk
                            if half == 0 and kk == 1 and b == 0:
                                pe.wait_ge(f["h_ready"], v * FC + kc + 1)
                            last = product(PS[:, (4 if half == 0 else 0) + b, :], H, (slice(None), kc, slice(b * P, (b + 1) * P)), W,
                                           (slice(None), t.slot, slice(kk * HALF, (kk + 1) * HALF)), kc == 0, kc == FC - 1)
                            if n == N_DOWN - 1 and kk == 1 and b < TB - 1:
                                last.then_inc(f["rows_done"], 1)
                        last.then_inc(w_used, 1)

    M = {n: sem(f"mix_{n}") for n in (
        "tr_done", "hi_ready", "xT_ready", "pads_set", "small_loaded", "gates_loaded", "gates_done", "gates_out", "scan_out",
        "mean_done", "sq_done", "var_done", "std_out", "norm_out", "silu_out", "evac", "y_hi", "y_ready", "scores_done", "max_out",
        "probs_out", "scores_read", "ptr_done", "pt_out0", "pt_out1", "tanh_out", "table_in", "divisor", "glu_ready", "tap_made", "tap_added", "q_lo", "conv_ready", "mult_sq", "mult_out", "o_done", "o_out", "otr_done", "rows_done", "var_ready", "rstd_ready", "shift_ready", "chain_a", "chain_b")}
    bias_tab = sb(ctx, "rel_bias_table", [P, QH, BAND])
    sinks = sb(ctx, "sinks", [P, QH])
    ones_ch = sb(ctx, "ones_channels", [P, P])

    with nc.Block() as block:
        @block.gpsimd
        def _(pool):
            nc.gpsimd.memset(ones_ch[:, :], 1.0 / 256.0)

    def mixer(l, T, T_next):
        m = M
        ahead = Ahead([T_next(0), T_next(1)], [up_src(l, 1, 0, 0), up_src(l, 1, 1, 0)])
        ahead_out = Ahead([T(N_MIN), T(N_MIN + 1)], [mout_src(l, 0), mout_src(l, 1)])
        N_COLS = 13
        with ExitStack() as c:
            small = sb(c, "mix_small", [P, 2, 48])
            sink_l = sb(c, "sink_l", [P, QH])
            gate_a = sb(c, "lru_wa", [P, 2, P])
            gate_x = sb(c, "lru_wx", [P, 2, P])
            glu = sb(c, "glu_padded", [P, 2, CONV_K - 1 + SEQ])
            sig = sb(c, "conv_gate", [P, 2, SEQ])
            conv = sb(c, "conv_sum", [P, 2, SEQ])
            sq = sb(c, "conv_square", [P, 2, SEQ])
            xb = sb(c, "lru_padded", [P, 2, LRU_K - 1 + SEQ])
            gb = sb(c, "lru_gate", [P, 2, SEQ])
            xc = sb(c, "lru_conv", [P, 2, SEQ])
            r_g = sb(c, "gate_r", [P, 2, SEQ])
            i_g = sb(c, "gate_i", [P, 2, SEQ])
            th = sb(c, "tanh_t", [P, 2, SEQ])
            lamc = sb(c, "lam_consts", [P, 2, 8])
            q_parts = sb(c, "q_parts", [P, QH, SEQ], f32r)
            k_hi = sb(c, "k_hi", [P, 2, SEQ], f32r)
            k_lo = sb(c, "k_lo", [P, SEQ], f32r)
            own = [slice(0, HD), slice(HD, P)]
            vt = sb(c, "v_attn", [P, TB, P])
            prob = sb(c, "probs", [P, 2, TB, BAND])
            pT = sb(c, "probs_T", [P, 2, 2, TB, P])
            smax = sb(c, "row_max", [P, 2, TB])
            nmax = sb(c, "neg_max", [P, 2, TB])
            dsum = sb(c, "row_sum", [P, 4, TB])
            esink = sb(c, "exp_sink", [P, 4, TB])
            o_tok = sb(c, "attn_out", [P, TB, 8 * HD])
            TAPS, CB, CG, CNB, LT, LB, BA, BX, LAM = 0, 31, 32, 33, 34, 38, 39, 40, 41
            A_TAPS = 9
            V_TAPS = CONV_K - A_TAPS
            PRODUCTS = sorted([(k == 0, 4 + k, th, glu, V_TAPS + k) for k in range(A_TAPS)] + [(k == 0, 9 + k, xc, xb, k) for k in range(LRU_K)], key=lambda p: p[1])
            with nc.Block() as block:
                @block.sync
                def _(sp):
                    load_tile(sp, T(2), mix_src(l, 2))
                    load_tile(sp, T(3), mix_src(l, 3))
                    sp.dma_start(small[:, :, 0:42], A["mix_small_2"][l]).then_inc(m["small_loaded"], 16)
                    sp.dma_start(sink_l[:, :], A["attn_sinks_2"][l, :].partition_broadcast(P)).then_inc(m["small_loaded"], 16)
                    sp.dma_start(bias_tab[:, :, :], S.distance_rows.table()).then_inc(m["table_in"], 16)
                    sp.wait_ge(m["pads_set"], l + 1)
                    for ch in range(2):
                        for hh in range(2):
                            for dst, src in ((gate_a, "lru_wa_2"), (gate_x, "lru_wx_2")):
                                sp.dma_start(dst[hh * HD:(hh + 1) * HD, ch, hh * HD:(hh + 1) * HD], A[src][l, 2 * ch + hh]).then_inc(m["gates_loaded"], 16)
                    sp.dma_start(g_row[:, :], A["ln_g_2"][l, 0, :].partition_broadcast(P)).then_inc(rows_loaded, 16)
                    sp.dma_start(b_row[:, :], A["ln_b_2"][l, 0, :].partition_broadcast(P)).then_inc(rows_loaded, 16)
                    for n in range(4, N_MIN):
                        load_tile(sp, T(n), mix_src(l, n))

                @block.gpsimd
                def _(pool):
                    nc.gpsimd.memset(gate_a[:, :, :], 0.0)
                    nc.gpsimd.memset(gate_x[:, :, :], 0.0)
                    nc.gpsimd.memset(glu[:, :, 0:CONV_K - 1], 0.0)
                    nc.gpsimd.memset(xb[:, :, 0:LRU_K - 1], 0.0)
                    pool.drain().then_inc(m["pads_set"], 1)
                    residual_affine(pool, 3 * l + 1, m["tr_done"], KC * (l + 1))
                    for k, (first, _, acc, _, _) in enumerate(PRODUCTS):
                        if not first:
                            pool.wait_ge(m["tap_made"], len(PRODUCTS) * l + k + 1)
                            nc.gpsimd.tensor_tensor(acc[:, :, :], acc[:, :, :], (sq, r_g)[k % 2][:, :, :], ALU.add)
                        pool.drain().then_inc(m["tap_added"], 1)

                @block.tensor
                def _(pe):
                    transposes(m["tr_done"])
                    for n in range(N_COLS):
                        t = T(n)
                        pe.wait_ge(w_lo, t.plus(1))
                        if n >= 4:
                            pe.wait_ge(m["evac"], l * N_MIN + n - 3)
                        if n == 12:
                            pe.wait_ge(m["q_lo"], 5 * l + 1)
                        for kc in range(KC):
                            if n == 0:
                                pe.wait_ge(m["xT_ready"], l * KC + kc + 1)
                            last = product(PS[:, n % 4, :], W, (slice(None), t.slot, slice(kc * P, (kc + 1) * P)), XT, (slice(None), kc), kc == 0, kc == KC - 1)
                        last.then_inc(w_used, 1)
                    t = T(N_COLS)
                    pe.wait_ge(w_lo, t.plus(1))
                    for b in range(TB):
                        for kc in range(KC):
                            last = product(PS[:, 4 + b, 0:P], XT, (slice(None), kc, slice(b * P, (b + 1) * P)), W, (slice(None), t.slot, slice(kc * P, (kc + 1) * P)), kc == 0, kc == KC - 1)
                    last.then_inc(w_used, 1)

                @block.scalar
                def _(act):
                    split_hi(T(1))
                    act.wait_ge(ln_loaded, 16 * (l + 1))
                    for kc in range(KC):
                        act.wait_ge(m["tr_done"], l * KC + kc + 1)
                        g, b = lnT[:, 0, 0, kc:kc + 1], lnT[:, 0, 1, kc:kc + 1]
                        if kc >= 2:
                            act.wait_ge(m["xT_ready"], l * KC + kc - 1)
                        nc.scalar.activation(tmp[:, kc % 2, :], PS[:, kc, :], ACT.Identity, bias=b, scale=g)
                        nc.scalar.activation(xT_hi[:, kc, :], PS[:, kc, :], ACT.Identity, bias=b, scale=g).then_inc(m["hi_ready"], 1)
                    act.wait_ge(m["pads_set"], l + 1)
                    for n in range(N_COLS):
                        if n + 2 < N_MIN:
                            split_hi(T(n + 2))
                        act.wait_ge(w_used, T(n).plus(1))
                        ps = PS[:, n % 4, :]
                        if n < 2:
                            op = nc.scalar.activation(glu[:, n, CONV_K - 1:], ps, ACT.Copy)
                        elif n < 4:
                            op = nc.scalar.activation(sig[:, n - 2, :], ps, ACT.Sigmoid)
                        elif n < 6:
                            op = nc.scalar.activation(xb[:, n - 4, LRU_K - 1:], ps, ACT.Copy)
                        elif n < 8:
                            op = nc.scalar.activation(gb[:, n - 6, :], ps, ACT.Gelu_apprx_tanh)
                        elif n < 12:
                            for p in range(2):
                                op = nc.scalar.activation(q_parts[own[p], 2 * (n - 8) + p, :], ps[own[p], :], ACT.Copy, scale=HD ** -0.5)
                        else:
                            for p in range(2):
                                nc.scalar.activation(k_hi[own[p], p, :], ps[own[p], :], ACT.Copy)
                                op = nc.scalar.activation(k_hi[own[1 - p], p, :], ps[own[p], :], ACT.Copy)
                        op.then_inc(m["evac"], 1)
                        if n == 1:
                            act.wait_ge(m["chain_a"], 2 * l + 1)
                            nc.scalar.activation(lamc[:, :, 1], lamc[:, :, 0], ACT.Exp).then_inc(m["chain_b"], 1)
                        elif n == 2:
                            act.wait_ge(m["chain_a"], 2 * l + 2)
                            nc.scalar.activation(lamc[:, :, 3], lamc[:, :, 2], ACT.Ln).then_inc(m["chain_b"], 1)
                        for k, (first, at, acc, src, tap) in enumerate(PRODUCTS):
                            if at != n:
                                continue
                            if k == 0:
                                act.wait_ge(m["glu_ready"], l + 1)
                            if k >= 2:
                                act.wait_ge(m["tap_added"], len(PRODUCTS) * l + k - 1)
                            into = acc if first else (sq, r_g)[k % 2]
                            column = (TAPS if src is glu else LT) + tap
                            for ch in range(2):
                                last = nc.scalar.activation(into[:, ch, :], src[:, ch, tap:tap + SEQ], ACT.Copy, scale=small[:, ch, column:column + 1])
                            last.then_inc(m["tap_made"], 1)
                    act.wait_ge(w_used, T(N_COLS).plus(1))
                    nc.scalar.activation(vt[:, :, :], PS[:, 4:8, 0:P], ACT.Copy).then_inc(m["evac"], 1)

                @block.vector
                def _(dve):
                    split_lo(T(1))
                    for kc in range(KC):
                        dve.wait_ge(m["hi_ready"], l * KC + kc + 1)
                        nc.vector.tensor_tensor(xT_lo[:, kc, :], tmp[:, kc % 2, :], xT_hi[:, kc, :].bitcast(f32), ALU.subtract).then_inc(m["xT_ready"], 1)
                    V = nc.vector
                    split_lo(T(2))
                    dve.wait_ge(m["small_loaded"], 32 * (l + 1))
                    V.tensor_scalar(lamc[:, :, 0], small[:, :, LAM], -1.0, None, ALU.mult)
                    dve.drain()
                    V.tensor_tensor(lamc[:, :, 0], lamc[:, :, 0], small[:, :, LAM], ALU.min).then_inc(m["chain_a"], 1)
                    split_lo(T(3))
                    dve.wait_ge(m["chain_b"], 2 * l + 1)
                    V.tensor_scalar(lamc[:, :, 2], lamc[:, :, 1], 1.0, None, ALU.add)
                    dve.drain().then_inc(m["chain_a"], 1)
                    V.tensor_scalar(lamc[:, :, 4], lamc[:, :, 2], -1.0, None, ALU.add)
                    dve.drain()
                    V.tensor_scalar(lamc[:, :, 5], lamc[:, :, 4], 0.0, None, ALU.is_equal)
                    V.tensor_scalar(lamc[:, :, 4], lamc[:, :, 4], 1e-30, None, ALU.max)
                    dve.drain()
                    V.tensor_tensor(lamc[:, :, 5], lamc[:, :, 5], lamc[:, :, 1], ALU.mult)
                    V.reciprocal(lamc[:, :, 4], lamc[:, :, 4])
                    dve.drain()
                    V.tensor_tensor(lamc[:, :, 4], lamc[:, :, 4], lamc[:, :, 1], ALU.mult)
                    split_lo(T(4))
                    dve.drain()
                    dve.wait_ge(m["chain_b"], 2 * l + 2)
                    V.tensor_tensor(lamc[:, :, 4], lamc[:, :, 4], lamc[:, :, 3], ALU.mult)
                    dve.drain()
                    V.tensor_tensor(lamc[:, :, 4], lamc[:, :, 4], lamc[:, :, 5], ALU.add)
                    V.tensor_scalar(lamc[:, :, 6], small[:, :, LAM], 0.0, None, ALU.min)
                    dve.drain()
                    V.tensor_tensor(lamc[:, :, 6], lamc[:, :, 6], lamc[:, :, 4], ALU.subtract)
                    dve.drain()
                    V.tensor_scalar(lamc[:, :, 7], lamc[:, :, 6], -LRU_C, None, ALU.mult)
                    V.tensor_scalar(lamc[:, :, 6], lamc[:, :, 6], LRU_C, None, ALU.mult)
                    split_lo(T(5))
                    dve.wait_ge(m["evac"], l * N_MIN + 4)
                    nc.vector.tensor_tensor(glu[:, :, CONV_K - 1:], glu[:, :, CONV_K - 1:], sig[:, :, :], ALU.mult)
                    dve.drain().then_inc(m["glu_ready"], 1)

                    def qk_lo(n):
                        dve.wait_ge(m["evac"], l * N_MIN + n + 1)
                        ps = PS[:, n % 4, :]
                        for p in range(2):
                            if n < 12:
                                h = 2 * (n - 8) + p
                                last = V.scalar_tensor_tensor(q_parts[own[1 - p], h, :], ps[own[p], :], HD ** -0.5, q_parts[own[p], h, :].bitcast(f32), ALU.mult, ALU.subtract)
                            else:
                                last = V.tensor_tensor(k_lo[own[p], :], ps[own[p], :], k_hi[own[p], p, :].bitcast(f32), ALU.subtract)
                        last.then_inc(m["q_lo"], 1)
                    for k in range(V_TAPS):
                        if k % 2 == 1 and 6 + k // 2 < N_MIN:
                            split_lo(T(6 + k // 2))
                        if k in (14, 16, 18):
                            qk_lo(8 + (k - 14) // 2)
                        for ch in range(2):
                            if k == 0:
                                nc.vector.tensor_scalar(conv[:, ch, :], glu[:, ch, 0:SEQ], small[:, ch, TAPS:TAPS + 1], small[:, ch, CB:CB + 1], ALU.mult, ALU.add)
                            else:
                                nc.vector.scalar_tensor_tensor(conv[:, ch, :], glu[:, ch, k:k + SEQ], small[:, ch, TAPS + k:TAPS + k + 1], conv[:, ch, :], ALU.mult, ALU.add)
                        dve.drain()
                    qk_lo(11)
                    qk_lo(12)
                    dve.wait_ge(m["tap_added"], len(PRODUCTS) * (l + 1))
                    V.tensor_tensor(conv[:, :, :], conv[:, :, :], th[:, :, :], ALU.add)
                    for ch in range(2):
                        V.tensor_scalar(xc[:, ch, :], xc[:, ch, :], small[:, ch, LB:LB + 1], None, ALU.add)

            U = l * QH
            with nc.Block() as block:
                @block.sync
                def _(sp):
                    ahead_out.load(sp)

                @block.gpsimd
                def _(pool):
                    pool.wait_ge(m["tanh_out"], l + 1)
                    nc.gpsimd.tensor_tensor(xc[:, :, :], xc[:, :, :], i_g[:, :, :], ALU.mult)
                    pool.drain()
                    nc.gpsimd.tensor_scalar(i_g[:, :, :], th[:, :, :], 1.0, None, ALU.add).then_inc(m["divisor"], 1)

                @block.tensor
                def _(pe):
                    def scores(u):
                        p, at = u % 2, 2 * (u % 2)
                        if u >= 2:
                            pe.wait_ge(m["scores_read"], U + u - 1)
                        for b in range(TB):
                            k0 = P if b == 0 else 0
                            out, rows, keys = PS[:, at + b // 2, b % 2 * BAND + k0:(b % 2 + 1) * BAND], slice(b * P, (b + 1) * P), slice(b * P - P + k0, (b + 1) * P)
                            nc.tensor.matmul(out, q_parts[:, u, rows], k_hi[:, p, keys], start=b % 2 == 0, stop=False, skip_group_check=True)
                            last = nc.tensor.matmul(out, q_parts[own[p], u, rows], k_lo[own[p], keys], start=False, stop=b % 2 == 1, skip_group_check=True)
                        last.then_inc(m["scores_done"], 1)

                    def prob_transposes(u):
                        pe.wait_ge(m["probs_out"], U + u + 1)
                        if u >= 1:
                            pe.wait_ge(m["pt_out0"], U + u)
                            pe.wait_ge(m["pt_out1"], U + u)
                        else:
                            pe.wait_ge(m["gates_out"], l + 1)
                        for j in range(2):
                            for b in range(1 - j, TB):
                                last = nc.tensor.transpose(PS[:, 4 + j, b * P:(b + 1) * P], prob[:, u % 2, b, j * P:(j + 1) * P], ident[:, :])
                        last.then_inc(m["ptr_done"], 1)

                    def outputs(u):
                        pe.wait_ge(m["pt_out0"], U + u + 1)
                        pe.wait_ge(m["pt_out1"], U + u + 1)
                        if u >= 2:
                            pe.wait_ge(m["o_out"], U + u - 1)
                        elif u == 1:
                            pe.wait_ge(m["std_out"], l + 1)
                        for b in range(TB):
                            for j in range(1 if b == 0 else 0, 2):
                                last = nc.tensor.matmul(PS[:, 6 + u % 2, b * HD:(b + 1) * HD], pT[:, u % 2, j, b, :], vt[:, b - 1 + j, u % 2 * HD:(u % 2 + 1) * HD],
                                                        start=j == 0 or b == 0, stop=j == 1, skip_group_check=True)
                        last.then_inc(m["o_done"], 1)

                    pe.wait_ge(m["gates_loaded"], 128 * (l + 1))
                    for ch in range(2):
                        for q, gw in enumerate((gate_a, gate_x)):
                            last = nc.tensor.matmul(PS[:, 4 + 2 * ch + q, :], gw[:, ch, :], xc[:, ch, :], start=True, stop=True)
                    last.then_inc(m["gates_done"], 1)
                    scores(0)
                    pe.wait_ge(m["gates_out"], l + 1)
                    for ch in range(2):
                        last = nc.tensor.matmul(PS[:, 6, :], ones_ch[:, :], conv[:, ch, :], start=ch == 0, stop=ch == 1)
                    last.then_inc(m["mean_done"], 1)
                    for u in range(QH + 1):
                        if u + 1 < QH:
                            scores(u + 1)
                        if u < QH:
                            prob_transposes(u)
                        if u == 0:
                            pe.wait_ge(m["sq_done"], l + 1)
                            for ch in range(2):
                                last = nc.tensor.matmul(PS[:, 7, :], ones_ch[:, :], sq[:, ch, :], start=ch == 0, stop=ch == 1)
                            last.then_inc(m["var_done"], 1)
                        else:
                            outputs(u - 1)

                @block.scalar
                def _(act):
                    act.wait_ge(m["gates_done"], l + 1)
                    for ch in range(2):
                        nc.scalar.activation(r_g[:, ch, :], PS[:, 4 + 2 * ch, :], ACT.Sigmoid, bias=small[:, ch, BA:BA + 1])
                        nc.scalar.activation(i_g[:, ch, :], PS[:, 5 + 2 * ch, :], ACT.Sigmoid, bias=small[:, ch, BX:BX + 1])
                    act.drain().then_inc(m["gates_out"], 1)
                    for ch in range(2):
                        nc.scalar.activation(th[:, ch, :], r_g[:, ch, :], ACT.Tanh, scale=lamc[:, ch, 7:8])
                        last = nc.scalar.activation(sig[:, ch, :], r_g[:, ch, :], ACT.Exp, scale=lamc[:, ch, 6:7])
                    last.then_inc(m["tanh_out"], 1)
                    for u in range(QH + 1):
                        if u < QH:
                            act.wait_ge(m["max_out"], U + u + 1)
                            nc.scalar.activation(esink[:, u % 4, :], smax[:, u % 2, :], ACT.Exp)
                            for b in range(TB):
                                k0 = P if b == 0 else 0
                                last = nc.scalar.activation(prob[:, u % 2, b, k0:], prob[:, u % 2, b, k0:], ACT.Exp, bias=nmax[:, u % 2, b:b + 1], accum_out=dsum[:, u % 4, b:b + 1])
                            last.then_inc(m["probs_out"], 1)
                        if u >= 1:
                            act.wait_ge(m["ptr_done"], U + u)
                            if u >= 3:
                                act.wait_ge(m["o_done"], U + u - 2)
                            nc.scalar.activation(pT[:, (u - 1) % 2, 1, :, :], PS[:, 5, :].rearrange("k (b q) -> k b q", q=P), ACT.Copy).then_inc(m["pt_out1"], 1)
                        if u == 3:
                            act.wait_ge(m["mult_sq"], l + 1)
                            nc.scalar.activation(th[:, :, :], th[:, :, :], ACT.Sqrt).then_inc(m["mult_out"], 1)
                        if u == 2:
                            act.wait_ge(m["var_done"], l + 1)
                            nc.scalar.activation(xb[:, 0, 0:SEQ], PS[:, 7, :], ACT.Sqrt, bias=eps[:, 0:1]).then_inc(m["std_out"], 1)
                        if u == 6:
                            act.wait_ge(m["scan_out"], l + 1)
                            nc.scalar.activation(xT_hi[:, 2:4, :], xc[:, :, :], ACT.Copy).then_inc(m["y_hi"], 1)
                    ahead_out.hi(0)
                    ahead_out.hi(1)

                @block.vector
                def _(dve):
                    V = nc.vector

                    def maxima(u):
                        sc = PS[:, 2 * (u % 2):2 * (u % 2) + 2, :].rearrange("q a (b k) -> q (a b) k", k=BAND)
                        pr, mx = prob[:, u % 2], smax[:, u % 2]
                        if u == 0:
                            dve.wait_ge(m["table_in"], 16 * (l + 1))
                        dve.wait_ge(m["scores_done"], U + u + 1)
                        V.tensor_tensor(pr[:, 0, P:], sc[:, 0, P:], bias_tab[:, u, P:], ALU.add)
                        V.tensor_tensor(pr[:, 1:, :], sc[:, 1:, :], bias_tab[:, u:u + 1, :].to_broadcast([P, TB - 1, BAND]), ALU.add)
                        dve.drain().then_inc(m["scores_read"], 1)
                        V.tensor_reduce(mx[:, 0:1], pr[:, 0, P:], AX.X, ALU.max)
                        V.tensor_reduce(mx[:, 1:], pr[:, 1:, :], AX.X, ALU.max)
                        dve.drain()
                        V.tensor_scalar(nmax[:, u % 2, :], mx, sink_l[:, u:u + 1], -1.0, ALU.max, ALU.mult)
                        dve.drain()
                        V.tensor_scalar(mx, nmax[:, u % 2, :], sink_l[:, u:u + 1], None, ALU.add)
                        dve.drain().then_inc(m["max_out"], 1)

                    def copy_transposed(u):
                        dve.wait_ge(m["ptr_done"], U + u + 1)
                        V.tensor_copy(pT[:, u % 2, 0, 1:, :], PS[:, 4, P:].rearrange("k (b q) -> k b q", q=P)).then_inc(m["pt_out0"], 1)
                        V.tensor_tensor(dsum[:, u % 4, :], dsum[:, u % 4, :], esink[:, u % 4, :], ALU.add)
                        dve.drain()
                        V.reciprocal(dsum[:, u % 4, :], dsum[:, u % 4, :])
                        dve.drain()

                    def normalised(u):
                        dve.wait_ge(m["o_done"], U + u + 1)
                        h = u // 2 + 4 * (u % 2)
                        V.tensor_tensor(o_tok[:, :, h * HD:(h + 1) * HD], PS[:, 6 + u % 2, 0:TB * HD].rearrange("q (b d) -> q b d", d=HD),
                                        dsum[:, u % 4, :].unsqueeze(2).to_broadcast([P, TB, HD]), ALU.mult).then_inc(m["o_out"], 1)

                    for u in range(QH + 2):
                        if u < QH:
                            maxima(u)
                        if 1 <= u <= QH:
                            copy_transposed(u - 1)
                        if u >= 2:
                            normalised(u - 2)
                        if u == 0:
                            dve.wait_ge(m["mean_done"], l + 1)
                            for ch in range(2):
                                V.tensor_tensor(conv[:, ch, :], conv[:, ch, :], PS[:, 6, :], ALU.subtract)
                            dve.drain()
                            V.tensor_tensor(sq[:, :, :], conv[:, :, :], conv[:, :, :], ALU.mult).then_inc(m["sq_done"], 1)
                        elif u == 1:
                            dve.wait_ge(m["divisor"], l + 1)
                            V.reciprocal(i_g[:, 0, :], i_g[:, 0, :])
                        elif u == 2:
                            V.reciprocal(i_g[:, 1, :], i_g[:, 1, :])
                            dve.drain()
                            V.scalar_tensor_tensor(th[:, :, :], th[:, :, :], 2.0, i_g[:, :, :], ALU.mult, ALU.mult).then_inc(m["mult_sq"], 1)
                        elif u == 4:
                            dve.wait_ge(m["mult_out"], l + 1)
                            V.tensor_tensor(xc[:, :, :], xc[:, :, :], th[:, :, :], ALU.mult)
                            dve.drain()
                            for ch in range(2):
                                V.tensor_tensor_scan(th[:, ch, :], sig[:, ch, :], xc[:, ch, :], 0.0, ALU.mult, ALU.add)
                            dve.drain()
                        elif u == 5:
                            V.tensor_tensor(xc[:, :, :], th[:, :, :], gb[:, :, :], ALU.mult).then_inc(m["scan_out"], 1)
                        elif u == 7:
                            dve.wait_ge(m["y_hi"], l * 5 + 1)
                            V.tensor_tensor(xT_lo[:, 2:4, :], xc[:, :, :], xT_hi[:, 2:4, :].bitcast(f32), ALU.subtract)
                    ahead_out.lo(0)
                    ahead_out.lo(1)

            with nc.Block() as block:
                @block.sync
                def _(sp):
                    for n in range(2, N_MOUT):
                        load_tile(sp, T(N_MIN + n), mout_src(l, n))
                    ahead.load(sp)

                @block.scalar
                def _(act):
                    for kc in range(4):
                        act.wait_ge(m["otr_done"], l * 4 + kc + 1)
                        nc.scalar.activation(xT_hi[:, 4 + kc, :], PS[:, 4 + kc, :], ACT.Copy).then_inc(m["y_hi"], 1)
                    for n in range(2, N_MOUT):
                        split_hi(T(N_MIN + n))
                        if n == 2:
                            act.wait_ge(m["norm_out"], l + 1)
                            for ch in range(2):
                                nc.scalar.activation(sq[:, ch, :], conv[:, ch, :], ACT.Silu, bias=small[:, ch, CNB:CNB + 1], scale=small[:, ch, CG:CG + 1])
                            act.drain()
                            nc.scalar.activation(xT_hi[:, 0:2, :], sq[:, :, :], ACT.Copy).then_inc(m["silu_out"], 1)
                    ahead.hi(0)
                    layer_norm_act(act, m, l, normalise_act)

                @block.vector
                def _(dve):
                    for kc in range(4):
                        dve.wait_ge(m["y_hi"], l * 5 + kc + 2)
                        nc.vector.tensor_tensor(xT_lo[:, 4 + kc, :], PS[:, 4 + kc, :], xT_hi[:, 4 + kc, :].bitcast(f32), ALU.subtract).then_inc(m["y_ready"], 1)
                    nc.vector.reciprocal(xb[:, 0, 0:SEQ], xb[:, 0, 0:SEQ])
                    dve.drain()
                    for ch in range(2):
                        last = nc.vector.tensor_tensor(conv[:, ch, :], conv[:, ch, :], xb[:, 0, 0:SEQ], ALU.mult)
                    last.then_inc(m["norm_out"], 1)
                    for n in range(2, N_MOUT):
                        split_lo(T(N_MIN + n))
                        if n == 2:
                            dve.wait_ge(m["silu_out"], l + 1)
                            nc.vector.tensor_tensor(xT_lo[:, 0:2, :], sq[:, :, :], xT_hi[:, 0:2, :].bitcast(f32), ALU.subtract).then_inc(m["conv_ready"], 1)
                        if n == 5:
                            dve.wait_ge(w_used, T(N_MIN + 3).plus(1))
                            sums = half_sums(0, 0)
                            for b in range(TB):
                                sums(b)
                            dve.drain()
                            for b in range(TB):
                                half_stats(b, 0)
                    ahead.lo(0)
                    layer_norm_dve(dve, 4, "rows_done", lambda: dve.wait_ge(w_used, T(N_MIN + 7).plus(1)), m, l, normalise_dve)

                @block.tensor
                def _(pe):
                    for kc in range(4):
                        for b in range(TB):
                            last = nc.tensor.transpose(PS[:, 4 + kc, b * P:(b + 1) * P], o_tok[:, b, kc * P:(kc + 1) * P], ident[:, :])
                        last.then_inc(m["otr_done"], 1)
                    for n in range(N_MOUT):
                        half, kp = n // 4, MOUT_ORDER[n % 4]
                        t = T(N_MIN + n)
                        pe.wait_ge(w_lo, t.plus(1))
                        if half == 0 and kp >= 2:
                            pe.wait_ge(m["y_ready"], l * 4 + 2 * (kp - 1))
                        if half == 0 and kp == 0:
                            pe.wait_ge(m["conv_ready"], l + 1)
                        order = [(kk, b) for kk in range(2) for b in range(TB)]
                        if n == N_MOUT - 1:
                            order = [(kk, b) for b in range(TB) for kk in range(2)]
                        for kk, b in order:
                            kc = 2 * kp + kk
                            last = product(PS[:, 4 * half + b, :], XT, (slice(None), kc, slice(b * P, (b + 1) * P)), W, (slice(None), t.slot, slice(kk * HALF, (kk + 1) * HALF)),
                                           n % 4 == 0 and kk == 0, n % 4 == 3 and kk == 1)
                            if n == N_MOUT - 1 and kk == 1 and b < TB - 1:
                                last.then_inc(m["rows_done"], 1)
                        last.then_inc(w_used, 1)

    def residual_affine(pool, n_rows, read_sem, read_value):
        pool.wait_ge(rows_loaded, 32 * n_rows)
        pool.wait_ge(read_sem, read_value)
        row = lambda r: r[:, :].unsqueeze(1).to_broadcast([P, TB, D])
        nc.gpsimd.tensor_tensor(xtok[:, :, :], xtok[:, :, :], row(g_row), ALU.mult)
        pool.drain()
        nc.gpsimd.tensor_tensor(xtok[:, :, :], xtok[:, :, :], row(b_row), ALU.add).then_inc(residual_ready, 1)

    with nc.Fori(0, LAYERS) as l:
        def tiles(off):
            return lambda at, i=0: Tile(T0 + off + at, l * (N_LAYER // 2) + i)
        ffn(0, l, tiles(0), tiles(N_FFN))
        mixer(l, tiles(N_FFN), tiles(N_FFN + N_MIN + N_MOUT))
        ffn(1, l, tiles(N_FFN + N_MIN + N_MOUT), None)


def constants():
    i = np.arange(P)
    at = np.arange(3 * P)
    distance = np.maximum(2 * P - 1 - at, 0)
    exact = REL_BUCKETS // 2
    large = exact + (np.log(np.maximum(distance, 1).astype(np.float32) / exact) / math.log(REL_MAX_DIST / exact) * (REL_BUCKETS - exact)).astype(np.int32)
    bucket = np.where(distance < exact, distance, np.minimum(large, REL_BUCKETS - 1))
    back = 2 * P - 1 - at
    col, kcol = (np.arange(P) % GRID)[:, None], np.arange(GRID)[None, :]
    start = np.clip(col - KW // 2, 0, GRID - KW)
    wide = lambda row: np.ascontiguousarray(np.broadcast_to(row.astype(np.float32), (P, row.size)))
    return {
        "ident": np.eye(P, dtype=np.float32),
        "before": (i[:, None] < i[None, :]).astype(np.float32),
        "iota": wide(i),
        "first4": wide(np.array([4, 3, 2, 1])),
        "jrow": wide(np.arange(24)),
        "nb_mask": np.where((kcol >= start) & (kcol < start + KW), 0, NEG).astype(np.float32),
        "distance_mask": np.ascontiguousarray(np.broadcast_to(np.where((back >= 0) & (back < P), 0, NEG).astype(np.float32), (QH, DIST))),
        "bucket_hot": (bucket[None, :] == np.arange(REL_BUCKETS)[:, None]).astype(np.float32),
    }


PAIRS = [h for c in range(4) for h in (c, c + 4)]


def laid_out(inputs):
    g = lambda n: np.asarray(inputs[n])
    c = np.ascontiguousarray
    A = {n: g(n) for n in (
        "x", "ctx", "w_ada", "b_ada", "w_in", "rpb", "sgu_ln", "w_out", "rg_b", "re_b", "w1", "w3", "w2", "ffn_w_gate_2", "ffn_w_up_2",
        "ffn_w_down_2", "ln_g_2", "ln_b_2", "lru_wa_2", "lru_wx_2", "w_out_2")}
    A["cT"] = c(np.stack([g("c")[0], g("c_ctx")], 0).reshape(2, KC, P).transpose(2, 1, 0))
    A["b_adaT"] = c(g("b_ada")[0].reshape(6, KC, P).transpose(2, 0, 1))
    A["out_gainT"] = c(g("out_gain")[0].reshape(KC, P).T)
    A["qk_gainT"] = c(np.stack([np.tile(g("q_gain")[0], 2), np.tile(g("k_gain")[0], 2)], 1))
    A["sgu_wT"] = c(g("sgu_w")[0].transpose(2, 0, 1))
    A["sgu_bT"] = c(g("sgu_b")[0].T)
    A["router_w"] = c(np.concatenate([g("rg_w")[0], g("re_w")[0].transpose(1, 0, 2).reshape(D, EXPERTS)], 1).reshape(KC, P, GROUPS + EXPERTS).transpose(1, 0, 2))
    A["lnT_2"] = c(np.stack([g("ln_g_2"), g("ln_b_2")], 2).reshape(LAYERS, 3, 2, KC, P).transpose(0, 4, 1, 2, 3))
    w = g("w_in_2")
    wq = w[:, :, 1024:1536].reshape(LAYERS, D, QH, HD)[:, :, PAIRS].reshape(LAYERS, D, QH * HD)
    A["w_in_2"] = c(np.concatenate([w[:, :, :1024], wq, w[:, :, 1536:]], 2))
    A["rel_bias_2"] = c(g("rel_bias_2")[:, PAIRS])
    A["attn_sinks_2"] = c(g("attn_sinks_2")[:, PAIRS])
    rows = [g("conv_dw_w_2")] + [g(n)[:, None] for n in ("conv_dw_b_2", "conv_ln_g_2", "conv_ln_b_2")] + [g("lru_conv_w_2")] + [
        g(n)[:, None] for n in ("lru_conv_b_2", "lru_ba_2", "lru_bx_2", "lru_lambda_2")]
    A["mix_small_2"] = c(np.concatenate(rows, 1).reshape(LAYERS, 42, 2, P).transpose(0, 3, 2, 1))
    A.update(constants())
    return A


def build(nc, A, out):
    with ExitStack() as ctx:
        S = shared(nc, ctx)
        first_block(nc, ctx, S, A)
        second_block(nc, ctx, N_FIRST, S, A)
        stored = ctx.enter_context(nc.semaphore("stored"))
        with nc.Block() as block:
            @block.sync
            def _(sp):
                sp.dma_start(out[0].rearrange("(b p) d -> p b d", p=P), S.xtok[:, :, :]).then_inc(stored, 16)
                sp.wait_ge(stored, 16)


def kernel(**inputs):
    import concourse.bacc as bacc
    from concourse.bass_utils import run_bass_kernel_spmd as run

    nc = bacc.Bacc("TRN2", target_bir_lowering=False, num_devices=1)
    arrays, A = {}, {}
    for name, a in laid_out(inputs).items():
        arrays["in_" + name] = a
        A[name] = nc.dram_tensor("in_" + name, a.shape, mybir.dt.from_np(a.dtype), kind="ExternalInput").ap()
    out = nc.dram_tensor("out_x", (1, SEQ, D), f32, kind="ExternalOutput").ap()
    build(nc, A, out)
    return run(nc, [arrays], core_ids=[0]).results[0]["out_x"]
```
